# Optimizing a Trainium2 kernel written in Bass

```python
import math
import jax
import jax.numpy as jnp
from jax import lax
import numpy as np

D_MODEL = 1024
BATCH = 1
SEQ = 256
DEPTH = 2

CTX_LEN = 256
GRID_W = 64
N_MIXERS = 3
NORM_EPS = 1e-6
F32 = jnp.float32

RW_HEAD = 64
RW_HEADS = D_MODEL // RW_HEAD
RW_DECAY_LORA = max(32, int(round(1.8 * D_MODEL ** 0.5 / 32)) * 32)
RW_AAA_LORA = max(32, int(round(1.8 * D_MODEL ** 0.5 / 32)) * 32)
RW_MV_LORA = max(32, int(round(1.3 * D_MODEL ** 0.5 / 32)) * 32)
RW_GATE_LORA = max(32, int(round(0.6 * D_MODEL ** 0.8 / 32)) * 32)
RW_LN_EPS = 64e-5

HY_ORDER = 2
HY_SHORT = 3
HY_EMB = 33
HY_BANDS = (HY_EMB - 1) // 2
HY_FILTER_HIDDEN = 64
HY_INNER_MLPS = 2
HY_FAST_DECAY = 0.3
HY_SLOW_DECAY = 1.5
HY_TARGET = 1e-2

MLA_HEADS = 16
MLA_NOPE = 64
MLA_ROPE = 32
MLA_V = 64
MLA_Q_LORA = 384
MLA_KV_LORA = 256
MLA_SCALE = (MLA_NOPE + MLA_ROPE) ** -0.5
MLA_Q_BLOCK = 128
ROPE_BASE = 10000.0

MOE_GROUPS = 4
MOE_PER_GROUP = 8
MOE_EXPERTS = MOE_GROUPS * MOE_PER_GROUP
MOE_TOPK = 2
MOE_HIDDEN = 512
MOE_ROWS = 256

kernel_name = 'hybrid_rwkv7_hyena_mla_hmoe_dit'

def _rms_norm(x, g):
    xf = x.astype(F32)
    return (xf * lax.rsqrt(jnp.mean(xf * xf, -1, keepdims=True) + NORM_EPS) * g).astype(x.dtype)

def _centred_shift(x):
    prev = jnp.pad(x[:, :-1], ((0, 0), (1, 0), (0, 0)))
    nxt = jnp.pad(x[:, 1:], ((0, 0), (0, 1), (0, 0)))
    return 0.5 * (prev + nxt)

def _axial_rope(n_tokens):
    rows = n_tokens // GRID_W
    row = jnp.repeat(jnp.arange(rows, dtype=F32), GRID_W)
    col = jnp.tile(jnp.arange(GRID_W, dtype=F32), rows)
    n_freq = MLA_ROPE // 4
    inv = ROPE_BASE ** (-jnp.arange(n_freq, dtype=F32) / n_freq)
    ang = jnp.concatenate([row[:, None] * inv, col[:, None] * inv], -1)
    return jnp.cos(ang), jnp.sin(ang)

def _rope(t, cos, sin):
    half = t.shape[-1] // 2
    t1, t2 = t[..., :half], t[..., half:]
    return jnp.concatenate([t1 * cos - t2 * sin, t1 * sin + t2 * cos], -1).astype(t.dtype)

def _rwkv7_features(h, mix, wrkv, w0, w1, w2, a0, a1, a2, g1, g2, k_k, k_a, vres, v_first):
    heads = lambda t: t.reshape(t.shape[:-1] + (RW_HEADS, RW_HEAD))
    xx = _centred_shift(h) - h
    xr, xw, xk, xv, xa, xg = (h + xx * mix[n] for n in range(6))
    r = xr @ wrkv[0]
    k = xk @ wrkv[1]
    v = xv @ wrkv[2]
    if vres is not None:
        v0, v1, v2 = vres
        v = v + (v_first - v) * jax.nn.sigmoid(v0 + (xv @ v1) @ v2)
    wlog = -jax.nn.softplus(-(w0[:, None, None] + jnp.einsum('zblr,zrd->zbld', jnp.tanh(jnp.einsum('bld,zdr->zblr', xw, w1)), w2))) - 0.5
    decay = jnp.exp(-jnp.exp(wlog.astype(F32)))
    a = jax.nn.sigmoid(a0[:, None, None] + jnp.einsum('zblr,zrd->zbld', jnp.einsum('bld,zdr->zblr', xa, a1), a2))
    g = jax.nn.sigmoid(xg @ g1) @ g2
    kk = heads((k * k_k).astype(F32))
    kk = kk / jnp.maximum(jnp.linalg.norm(kk, axis=-1, keepdims=True), 1e-12)
    k_dir = k[None] * (1.0 + (a - 1.0) * k_a)
    return heads(r), heads(decay), heads(k_dir), heads(v), kk, heads(a), g, v

def _rwkv7_bidir_scan(r, decay, k, v, kk, a, s0):
    orient = lambda t2: jnp.stack([t2[0], jnp.flip(t2[1], 1)])
    both = lambda t: jnp.stack([t, jnp.flip(t, 1)])
    seqs = (both(r), orient(decay), orient(k), both(v), both(-kk), orient(kk[None] * a))
    xs = tuple(jnp.moveaxis(t.astype(F32), 2, 0) for t in seqs)

    def step(S, inp):
        r_t, w_t, k_t, v_t, a_t, b_t = inp
        sa = jnp.einsum('zbhvk,zbhk->zbhv', S, a_t)
        S = S * w_t[..., None, :] + sa[..., None] * b_t[..., None, :] + v_t[..., None] * k_t[..., None, :]
        return S, jnp.einsum('zbhvk,zbhk->zbhv', S, r_t)

    s_final, y = lax.scan(step, s0, xs)
    y = jnp.moveaxis(y, 0, 2)
    return y[0] + jnp.flip(y[1], 1), s_final

def _rwkv7_out(y, feats, r_k, ln_w, ln_b, wo):
    r, _, k, v, _, _, g, _ = feats
    B, L = y.shape[:2]
    mu = jnp.mean(y, -1, keepdims=True)
    var = jnp.mean(jnp.square(y - mu), -1, keepdims=True)
    yn = ((y - mu) * lax.rsqrt(var + RW_LN_EPS)).reshape(B, L, -1) * ln_w + ln_b
    bonus = jnp.sum(r * (k[0] + k[1]) * r_k, -1, keepdims=True) * v
    return ((yn + bonus.reshape(B, L, -1)) * g).astype(g.dtype) @ wo

def _rwkv7_mixer(hx, hc, mix, wrkv, wo, w0, w1, w2, a0, a1, a2, g1, g2, k_k, k_a, r_k, ln_w, ln_b,
                 vres, vf_x, vf_c, need_ctx):
    fc = _rwkv7_features(hc, mix, wrkv, w0, w1, w2, a0, a1, a2, g1, g2, k_k, k_a, vres, vf_c)
    fx = _rwkv7_features(hx, mix, wrkv, w0, w1, w2, a0, a1, a2, g1, g2, k_k, k_a, vres, vf_x)
    s0 = jnp.zeros((2, hx.shape[0], RW_HEADS, RW_HEAD, RW_HEAD), F32)
    yc, s_ctx = _rwkv7_bidir_scan(*fc[:6], s0)
    yx, _ = _rwkv7_bidir_scan(*fx[:6], s_ctx)
    ox = _rwkv7_out(yx, fx, r_k, ln_w, ln_b, wo)
    oc = _rwkv7_out(yc, fc, r_k, ln_w, ln_b, wo) if need_ctx else None
    return ox, oc, fx[7], fc[7]

def _hyena_filters(L, f_w1, f_b1, f_freq, f_wi, f_bi, f_w3):
    D = f_w3.shape[-1] // (2 * HY_ORDER)
    t = jnp.linspace(0.0, 1.0, L, dtype=F32)[:, None]
    w = 2.0 * math.pi * jnp.arange(L, dtype=F32)[:, None] / L
    f = jnp.linspace(1e-4, HY_BANDS - 1, HY_BANDS, dtype=F32)[None]
    z = jnp.concatenate([t, jnp.cos(f * w), -jnp.sin(f * w)], -1)
    hdn = jnp.sin(f_freq * (z @ f_w1 + f_b1))
    for n in range(HY_INNER_MLPS):
        hdn = jnp.sin(f_freq * (hdn @ f_wi[n] + f_bi[n]))
    h = (hdn @ f_w3).astype(F32).reshape(L, HY_ORDER, 2, D)
    max_decay = math.log(HY_TARGET) / HY_FAST_DECAY
    min_decay = math.log(HY_TARGET) / HY_SLOW_DECAY
    deltas = jnp.abs(jnp.linspace(min_decay, max_decay, D, dtype=F32))
    h = h * jnp.exp(-t[:, :, None, None] * deltas)
    kern = jnp.concatenate([h[:, :, 0], jnp.zeros((1, HY_ORDER, D), F32), jnp.flip(h[1:, :, 1], 0)], 0)
    return kern / jnp.sum(jnp.abs(kern), 0, keepdims=True)

def _fft_conv(u, kern, skip):
    n, L = kern.shape[0], u.shape[1]
    y = jnp.fft.irfft(jnp.fft.rfft(u, n=n, axis=1) * jnp.fft.rfft(kern, axis=0)[None], n=n, axis=1)[:, :L]
    return y + u * skip

def _hyena_seq(h, w_in, b_in, conv_w, conv_b, kern, skip, w_out, b_out):
    u = h @ w_in + b_in
    up = jnp.pad(u, ((0, 0), (1, 1), (0, 0)))
    u = up[:, :-2] * conv_w[0] + up[:, 1:-1] * conv_w[1] + up[:, 2:] * conv_w[2] + conv_b
    v, x1, x2 = jnp.split(u.astype(F32), 3, -1)
    z = x1 * _fft_conv(v, kern[:, 0], skip[0])
    y = x2 * _fft_conv(z, kern[:, 1], skip[1])
    return y.astype(h.dtype) @ w_out + b_out

def _mla_q(dq, q_norm, w_uq, rope):
    B, L, _ = dq.shape
    q = (_rms_norm(dq, q_norm) @ w_uq).reshape(B, L, MLA_HEADS, MLA_NOPE + MLA_ROPE)
    qn, qr = q[..., :MLA_NOPE], q[..., MLA_NOPE:]
    if rope is not None:
        qr = _rope(qr, rope[0][:, None], rope[1][:, None])
    return qn, qr

def _mla_kv(dkv, kv_norm, w_ukv, rope):
    B, L, _ = dkv.shape
    ckv, kr = dkv[..., :MLA_KV_LORA], dkv[..., MLA_KV_LORA:]
    kv = (_rms_norm(ckv, kv_norm) @ w_ukv).reshape(B, L, MLA_HEADS, MLA_NOPE + MLA_V)
    kn, v = kv[..., :MLA_NOPE], kv[..., MLA_NOPE:]
    if rope is not None:
        kr = _rope(kr, rope[0], rope[1])
    return kn, kr, v

def _mla_attend(qn, qr, kn, kr, v):
    s = jnp.einsum('bqhd,bkhd->bhqk', qn, kn) + jnp.einsum('bqhr,bkr->bhqk', qr, kr)
    p = jax.nn.softmax(s.astype(F32) * MLA_SCALE, -1).astype(v.dtype)
    return jnp.einsum('bhqk,bkhd->bqhd', p, v)

def _mla_mixer(hx, hc, rope_x, w_down, q_norm, kv_norm, w_uq, w_ukv, w_o, need_ctx):
    B, L, _ = hx.shape
    C = hc.shape[1]
    dx = hx @ w_down
    qn_x, qr_x = _mla_q(dx[..., :MLA_Q_LORA], q_norm, w_uq, rope_x)
    kn_x, kr_x, v_x = _mla_kv(dx[..., MLA_Q_LORA:], kv_norm, w_ukv, rope_x)
    if need_ctx:
        dc = hc @ w_down
        qn_c, qr_c = _mla_q(dc[..., :MLA_Q_LORA], q_norm, w_uq, None)
        kn_c, kr_c, v_c = _mla_kv(dc[..., MLA_Q_LORA:], kv_norm, w_ukv, None)
    else:
        kn_c, kr_c, v_c = _mla_kv(hc @ w_down[:, MLA_Q_LORA:], kv_norm, w_ukv, None)
    kn = jnp.concatenate([kn_c, kn_x], 1)
    kr = jnp.concatenate([kr_c, kr_x], 1)
    v = jnp.concatenate([v_c, v_x], 1)
    nb = L // MLA_Q_BLOCK
    to_blocks = lambda t: jnp.moveaxis(t.reshape((B, nb, MLA_Q_BLOCK) + t.shape[2:]), 1, 0)
    o = lax.map(lambda qs: _mla_attend(qs[0], qs[1], kn, kr, v), (to_blocks(qn_x), to_blocks(qr_x)))
    ox = jnp.moveaxis(o, 0, 1).reshape(B, L, MLA_HEADS * MLA_V) @ w_o
    oc = _mla_attend(qn_c, qr_c, kn_c, kr_c, v_c).reshape(B, C, MLA_HEADS * MLA_V) @ w_o if need_ctx else None
    return ox, oc

def _moe_dispatch(h, expert, weight, w_gate, w_up, w_down):
    N, D = h.shape
    A = N * MOE_TOPK
    e_flat = expert.reshape(A)
    w_flat = weight.reshape(A)
    tok_flat = jnp.arange(A, dtype=jnp.int32) // MOE_TOPK
    order = jnp.argsort(e_flat)
    e_sorted = e_flat[order]
    counts = jax.ops.segment_sum(jnp.ones((A,), jnp.int32), e_flat, num_segments=MOE_EXPERTS)
    padded = (counts + MOE_ROWS - 1) // MOE_ROWS * MOE_ROWS
    pad_end = jnp.cumsum(padded)
    pad_start = pad_end - padded
    start = jnp.cumsum(counts) - counts
    dest = pad_start[e_sorted] + jnp.arange(A, dtype=jnp.int32) - start[e_sorted]
    n_blocks = -(-A // MOE_ROWS) + MOE_EXPERTS
    R = n_blocks * MOE_ROWS
    slot_tok = jnp.full((R,), N, jnp.int32).at[dest].set(tok_flat[order])
    slot_w = jnp.zeros((R,), w_flat.dtype).at[dest].set(w_flat[order])
    block_expert = jnp.minimum(jnp.searchsorted(pad_end, jnp.arange(n_blocks, dtype=jnp.int32) * MOE_ROWS, side='right'), MOE_EXPERTS - 1)
    h_pad = jnp.concatenate([h, jnp.zeros((1, D), h.dtype)], 0)
    xs = h_pad[slot_tok].reshape(n_blocks, MOE_ROWS, D)

    def expert_block(args):
        xb, e = args
        return (jax.nn.silu(xb @ w_gate[e]) * (xb @ w_up[e])) @ w_down[e]

    ys = lax.map(expert_block, (xs, block_expert)).reshape(R, D)
    out = jnp.zeros((N + 1, D), ys.dtype).at[slot_tok].add(ys * slot_w[:, None].astype(ys.dtype))
    return out[:N]

def _hier_moe(h, router_w, router_b, w_gate, w_up, w_down):
    N = h.shape[0]
    logits = (h @ router_w + router_b).astype(F32)
    g_logits = logits[:, :MOE_GROUPS]
    e_logits = logits[:, MOE_GROUPS:].reshape(N, MOE_GROUPS, MOE_PER_GROUP)
    _, g_idx = lax.top_k(g_logits, 1)
    p_group = jnp.take_along_axis(jax.nn.softmax(g_logits, -1), g_idx, 1)
    in_group = e_logits[jnp.arange(N), g_idx[:, 0]]
    top_v, top_i = lax.top_k(in_group, MOE_TOPK)
    weight = p_group * jax.nn.softmax(top_v, -1)
    expert = g_idx * MOE_PER_GROUP + top_i
    return _moe_dispatch(h, expert, weight, w_gate, w_up, w_down)

def setup_inputs(seed: int = 0) -> dict:
    key = jax.random.key(seed)
    keys = iter(jax.random.split(key, 80))
    nrm = lambda shape, scale: scale * jax.random.normal(next(keys), shape, F32)
    near_one = lambda shape, s=0.1: 1.0 + nrm(shape, s)
    D = D_MODEL
    nA, nB, nC = (len(range(m, DEPTH, N_MIXERS)) for m in range(N_MIXERS))
    nV = max(nA - 1, 0)
    HF = HY_FILTER_HIDDEN
    ramp = (jnp.arange(D, dtype=F32) / (D - 1)) ** 0.85
    return {
        'x': nrm((BATCH, SEQ, D), 1.0),
        'c': nrm((BATCH, D), 1.0),
        'ctx': nrm((BATCH, CTX_LEN, D), 1.0),
        'c_ctx': nrm((D,), 1.0),
        'ada_w': nrm((DEPTH, D, 6 * D), 0.5 * D ** -0.5),
        'ada_b': nrm((DEPTH, 6 * D), 0.02),
        'norm_g': near_one((DEPTH, 2, D)),
        'final_g': near_one((D,)),
        'rw_mix': jax.random.uniform(next(keys), (nA, 6, D), F32),
        'rw_wrkv': nrm((nA, 3, D, D), D ** -0.5),
        'rw_wo': nrm((nA, D, D), D ** -0.5),
        'rw_w0': -6.5 + 5.0 * ramp + nrm((nA, 2, D), 0.1),
        'rw_w1': nrm((nA, 2, D, RW_DECAY_LORA), D ** -0.5),
        'rw_w2': nrm((nA, 2, RW_DECAY_LORA, D), 0.1 * RW_DECAY_LORA ** -0.5),
        'rw_a0': nrm((nA, 2, D), 0.5),
        'rw_a1': nrm((nA, 2, D, RW_AAA_LORA), D ** -0.5),
        'rw_a2': nrm((nA, 2, RW_AAA_LORA, D), 0.5 * RW_AAA_LORA ** -0.5),
        'rw_g1': nrm((nA, D, RW_GATE_LORA), D ** -0.5),
        'rw_g2': nrm((nA, RW_GATE_LORA, D), RW_GATE_LORA ** -0.5),
        'rw_kk': 0.85 + nrm((nA, D), 0.05),
        'rw_ka': near_one((nA, D), 0.05),
        'rw_rk': nrm((nA, RW_HEADS, RW_HEAD), 0.1),
        'rw_lnw': near_one((nA, D)),
        'rw_lnb': nrm((nA, D), 0.02),
        'rw_v0': near_one((nV, D)),
        'rw_v1': nrm((nV, D, RW_MV_LORA), D ** -0.5),
        'rw_v2': nrm((nV, RW_MV_LORA, D), 0.5 * RW_MV_LORA ** -0.5),
        'hy_w_in': nrm((nB, D, 3 * D), D ** -0.5),
        'hy_b_in': nrm((nB, 3 * D), 0.02),
        'hy_conv_w': nrm((nB, HY_SHORT, 3 * D), HY_SHORT ** -0.5),
        'hy_conv_b': nrm((nB, 3 * D), 0.02),
        'hy_f_w1': nrm((nB, HY_EMB, HF), HY_EMB ** -0.5),
        'hy_f_b1': nrm((nB, HF), 0.02),
        'hy_f_freq': near_one((nB, HF)),
        'hy_f_wi': nrm((nB, HY_INNER_MLPS, HF, HF), HF ** -0.5),
        'hy_f_bi': nrm((nB, HY_INNER_MLPS, HF), 0.02),
        'hy_f_w3': nrm((nB, HF, HY_ORDER * 2 * D), HF ** -0.5),
        'hy_skip': near_one((nB, HY_ORDER, D)),
        'hy_w_out': nrm((nB, D, D), D ** -0.5),
        'hy_b_out': nrm((nB, D), 0.02),
        'mla_w_down': nrm((nC, D, MLA_Q_LORA + MLA_KV_LORA + MLA_ROPE), D ** -0.5),
        'mla_q_norm': near_one((nC, MLA_Q_LORA)),
        'mla_kv_norm': near_one((nC, MLA_KV_LORA)),
        'mla_w_uq': nrm((nC, MLA_Q_LORA, MLA_HEADS * (MLA_NOPE + MLA_ROPE)), MLA_Q_LORA ** -0.5),
        'mla_w_ukv': nrm((nC, MLA_KV_LORA, MLA_HEADS * (MLA_NOPE + MLA_V)), MLA_KV_LORA ** -0.5),
        'mla_w_o': nrm((nC, MLA_HEADS * MLA_V, D), (MLA_HEADS * MLA_V) ** -0.5),
        'moe_router': nrm((DEPTH, D, MOE_GROUPS + MOE_EXPERTS), D ** -0.5),
        'moe_router_b': nrm((DEPTH, MOE_GROUPS + MOE_EXPERTS), 0.01),
        'moe_w_gate': nrm((DEPTH, MOE_EXPERTS, D, MOE_HIDDEN), D ** -0.5),
        'moe_w_up': nrm((DEPTH, MOE_EXPERTS, D, MOE_HIDDEN), D ** -0.5),
        'moe_w_down': nrm((DEPTH, MOE_EXPERTS, MOE_HIDDEN, D), MOE_HIDDEN ** -0.5),
    }

def reference(x, c, ctx, c_ctx, ada_w, ada_b, norm_g, final_g,
              rw_mix, rw_wrkv, rw_wo, rw_w0, rw_w1, rw_w2, rw_a0, rw_a1, rw_a2, rw_g1, rw_g2,
              rw_kk, rw_ka, rw_rk, rw_lnw, rw_lnb, rw_v0, rw_v1, rw_v2,
              hy_w_in, hy_b_in, hy_conv_w, hy_conv_b, hy_f_w1, hy_f_b1, hy_f_freq, hy_f_wi, hy_f_bi,
              hy_f_w3, hy_skip, hy_w_out, hy_b_out,
              mla_w_down, mla_q_norm, mla_kv_norm, mla_w_uq, mla_w_ukv, mla_w_o,
              moe_router, moe_router_b, moe_w_gate, moe_w_up, moe_w_down):
    B, L, D = x.shape
    C = ctx.shape[1]
    cond_x = jax.nn.silu(c)
    cond_c = jax.nn.silu(c_ctx)[None]
    v_first_x = v_first_c = None
    for i in range(DEPTH):
        mixer, j = i % N_MIXERS, i // N_MIXERS
        need_ctx = i < DEPTH - 1
        mx = (cond_x @ ada_w[i] + ada_b[i])[:, None, :]
        mc = (cond_c @ ada_w[i] + ada_b[i])[:, None, :]
        sh1x, sc1x, g1x, sh2x, sc2x, g2x = jnp.split(mx, 6, -1)
        sh1c, sc1c, g1c, sh2c, sc2c, g2c = jnp.split(mc, 6, -1)
        hx = _rms_norm(x, norm_g[i, 0]) * (1.0 + sc1x) + sh1x
        if need_ctx or mixer != 1:
            hc = _rms_norm(ctx, norm_g[i, 0]) * (1.0 + sc1c) + sh1c
        if mixer == 0:
            vres = None if j == 0 else (rw_v0[j - 1], rw_v1[j - 1], rw_v2[j - 1])
            ox, oc, vx, vc = _rwkv7_mixer(hx, hc, rw_mix[j], rw_wrkv[j], rw_wo[j], rw_w0[j], rw_w1[j], rw_w2[j],
                                          rw_a0[j], rw_a1[j], rw_a2[j], rw_g1[j], rw_g2[j], rw_kk[j], rw_ka[j],
                                          rw_rk[j], rw_lnw[j], rw_lnb[j], vres, v_first_x, v_first_c, need_ctx)
            if j == 0:
                v_first_x, v_first_c = vx, vc
        elif mixer == 1:
            fparams = (hy_f_w1[j], hy_f_b1[j], hy_f_freq[j], hy_f_wi[j], hy_f_bi[j], hy_f_w3[j])
            ox = _hyena_seq(hx, hy_w_in[j], hy_b_in[j], hy_conv_w[j], hy_conv_b[j], _hyena_filters(L, *fparams),
                            hy_skip[j], hy_w_out[j], hy_b_out[j])
            if need_ctx:
                oc = _hyena_seq(hc, hy_w_in[j], hy_b_in[j], hy_conv_w[j], hy_conv_b[j], _hyena_filters(C, *fparams),
                                hy_skip[j], hy_w_out[j], hy_b_out[j])
        else:
            ox, oc = _mla_mixer(hx, hc, _axial_rope(L), mla_w_down[j], mla_q_norm[j], mla_kv_norm[j],
                                mla_w_uq[j], mla_w_ukv[j], mla_w_o[j], need_ctx)
        x = x + g1x * ox
        hx = _rms_norm(x, norm_g[i, 1]) * (1.0 + sc2x) + sh2x
        if need_ctx:
            ctx = ctx + g1c * oc
            hc = _rms_norm(ctx, norm_g[i, 1]) * (1.0 + sc2c) + sh2c
            tokens = jnp.concatenate([hx.reshape(B * L, D), hc.reshape(B * C, D)], 0)
            out = _hier_moe(tokens, moe_router[i], moe_router_b[i], moe_w_gate[i], moe_w_up[i], moe_w_down[i])
            x = x + g2x * out[:B * L].reshape(B, L, D)
            ctx = ctx + g2c * out[B * L:].reshape(B, C, D)
        else:
            out = _hier_moe(hx.reshape(B * L, D), moe_router[i], moe_router_b[i], moe_w_gate[i], moe_w_up[i], moe_w_down[i])
            x = x + g2x * out.reshape(B, L, D)
    return _rms_norm(x, final_g)


_drawn_inputs = setup_inputs


def setup_inputs(seed=0):
    import zlib

    import numpy as np

    out = dict(_drawn_inputs(seed))
    spreads = {}
    factors = {'rw_w1': 8.0,
     'rw_w2': 8.0,
     'rw_lnb': 8.0,
     'hy_b_in': 4.342,
     'hy_conv_b': 4.061,
     'hy_f_b1': 8.0,
     'hy_f_freq': 5.221,
     'hy_f_bi': 6.966,
     'hy_b_out': 8.0,
     'moe_router_b': 5.8}
    for name, (base, spread) in spreads.items():
        noise = np.random.default_rng([zlib.crc32(name.encode()), seed]).standard_normal(out[name].shape)
        drawn = base * np.exp(spread * noise) if base else spread * noise
        out[name] = jnp.asarray(drawn.astype(out[name].dtype))
    for name, factor in factors.items():
        out[name] = (out[name] * factor).astype(out[name].dtype)
    return out
```

```python
import math
from contextlib import ExitStack

import numpy as np

import concourse.bass as bass
from concourse import mybir

F32 = mybir.dt.float32
I32 = mybir.dt.int32
U32 = mybir.dt.uint32
ALU = mybir.AluOpType
ACT = mybir.ActivationFunctionType
AX = mybir.AxisListType

P = 128
D = 1024
L = 256
KT = D // P
TT = L // P
NORM_EPS = 1e-6
EXPERTS, GROUPS, PER_GROUP, HIDDEN = 32, 4, 8, 512
CAP = 64
HK = HIDDEN // P
EXTRA = 8
PAIRS = EXPERTS // 2


def constants():
    i = np.arange(P)
    r, c = i[:, None], i[None, :]
    parts = {
        "ident": (r == c),
        "ones": np.ones((P, P)),
        "before": (r < c),
        "after": (r > c),
        "head_ones": (r // 64 == c // 64),
        "upto": (r <= c),
        "from": (r >= c),
    }
    for n in range(7):
        b = 2 ** n
        same = (r // (2 * b) == c // (2 * b))
        parts[f"low{n}"] = same & (r % (2 * b) >= b) & (c % (2 * b) < b)
        parts[f"up{n}"] = parts[f"low{n}"].T
    parts["iota"] = np.broadcast_to(c, (P, P))
    at, cols = {}, 0
    for name, m in parts.items():
        at[name] = cols
        cols += P
    return at, np.concatenate([np.asarray(m, np.float32) for m in parts.values()], 1)


CONST_AT, CONST_ARRAY = constants()
N_CONST = CONST_ARRAY.shape[1]


class Shared:

    def __init__(self, nc, ctx, arena_cols):
        self.nc, self.ctx = nc, ctx
        self.const = ctx.enter_context(nc.sbuf_tensor("const", [P, N_CONST], F32))
        self.x_res = ctx.enter_context(nc.sbuf_tensor("x_res", [P, TT, D], F32))[:, :, :]
        self.arena = ctx.enter_context(nc.sbuf_tensor("arena", [P, arena_cols], F32))
        self.psum = [ctx.enter_context(nc.psum_tensor(f"bank{b}", [P, 512], F32)) for b in range(8)]
        self.cols = arena_cols
        self.at = 0
        self.sems = []

    def c(self, name, width=P, rows=P):
        return self.const[0:rows, CONST_AT[name]:CONST_AT[name] + width]

    def sem(self, name):
        self.sems.append(self.nc.alloc_semaphore(name=name))
        return self.sems[-1]

    def clear_semaphores(self):
        self.nc.clear_and_free_semaphores(self.sems)
        self.sems = []
        self.nc.all_engine_barrier()

    def take(self, *shape):
        n = int(np.prod(shape))
        assert self.at + n <= self.cols, (self.at, n, self.cols)
        v = self.arena[:, self.at:self.at + n]
        self.at += n
        names = " ".join(f"a{i}" for i in range(len(shape)))
        if len(shape) > 1:
            v = v.rearrange(f"p ({names}) -> p {names}", **{f"a{i}": s for i, s in enumerate(shape)})
        return v


def modulation(s, ins, mods):
    nc = s.nc
    s.at = 0
    SLOTS, WIDE, PARTS = 8, 2048, 4
    raw = s.take(2, KT)
    sig = s.take(2, KT)
    cond = s.take(KT, 32)
    ring = [s.take(WIDE) for _ in range(SLOTS)]
    BLOCKS = 6 * D // WIDE
    bias = [s.take(512) for _ in range(BLOCKS)]
    row = [s.take(512) for _ in range(BLOCKS)]
    cond_in, sig_done, cond_ready = s.sem("cond_in"), s.sem("cond_sig"), s.sem("cond_ready")
    ada_in = [s.sem(f"ada_in{k}") for k in range(SLOTS)]
    bias_in = [s.sem(f"ada_b_in{k}") for k in range(BLOCKS)]
    ada_used, row_ready = s.sem("ada_used"), s.sem("ada_row")
    row_out = [s.sem(f"ada_row_out{k}") for k in range(BLOCKS)]
    ada = ins["ada_w"].rearrange("l (p t) n -> l p t n", t=KT)

    with nc.Block(name="modulation", no_gpsimd_drain=True) as block:

        @block.sync
        def _(sp):
            sp.dma_start(raw[:, 0], ins["c"].rearrange("b (p t) -> p (b t)", t=KT)).then_inc(cond_in, 16)
            sp.dma_start(raw[:, 1], ins["c_ctx"].rearrange("(p t) -> p t", t=KT)).then_inc(cond_in, 16)
            with sp.Fori(0, 2) as l:
                for b in range(BLOCKS):
                    for t in range(KT):
                        n = l * BLOCKS + b
                        sp.wait_ge(ada_used, n * KT + (t + 1))
                        sp.dma_start(ring[t], ada[l, :, t, b * WIDE:(b + 1) * WIDE]).then_inc(ada_in[t], 16)

        @block.scalar
        def _(act):
            act.wait_ge(cond_in, 32)
            act.activation(sig, raw, ACT.Sigmoid).then_inc(sig_done, 1)
            with act.Fori(0, 2) as l:
                for b in range(BLOCKS):
                    n = l * BLOCKS + b
                    act.wait_ge(row_ready, n + (1 + BLOCKS))
                    for q in range(PARTS):
                        for i in range(2):
                            act.dma_start(mods[l, i, b * WIDE + q * 512:b * WIDE + (q + 1) * 512].unsqueeze(0),
                                          row[b][q * 32 + i:q * 32 + i + 1, :]).then_inc(row_out[b], 16)
            for b in range(BLOCKS):
                act.wait_ge(row_out[b], 3 * PARTS * 2 * 16)

        @block.gpsimd
        def _(pool):
            with pool.Fori(0, 2) as l:
                for b in range(BLOCKS):
                    n = l * BLOCKS + b
                    pool.wait_ge(row_ready, n + 1)
                    for q in range(PARTS):
                        pool.dma_start(bias[b][q * 32:(q + 1) * 32, :],
                                       ins["ada_b"][l, b * WIDE + q * 512:b * WIDE + (q + 1) * 512]
                                       .partition_broadcast(32)).then_inc(bias_in[b], 16)

        @block.tensor
        def _(pe):
            pe.wait_ge(cond_ready, 1)
            pe.sem_inc(ada_used, KT)
            with pe.Fori(0, 2) as l:
                for b in range(BLOCKS):
                    n = l * BLOCKS + b
                    pe.wait_ge(row_ready, n + 1)
                    for t in range(KT):
                        pe.wait_ge(ada_in[t], n * 16 + 16)
                        for q in range(PARTS):
                            mm = pe.matmul(s.psum[b][q * 32:(q + 1) * 32, :], cond[:, t],
                                           ring[t][:, q * 512:(q + 1) * 512], start=(t == 0), stop=(t == KT - 1),
                                           tile_position=(0, q * 32))
                        mm.then_inc(ada_used, 1)

        @block.vector
        def _(dve):
            dve.memset(cond, 0.0)
            dve.drain()
            dve.wait_ge(sig_done, 1)
            dve.tensor_tensor(cond[:, :, 0:2].rearrange("p t i -> p i t"), raw, sig, ALU.mult).then_inc(cond_ready, 1)
            dve.sem_inc(row_ready, BLOCKS)
            for b in range(BLOCKS):
                dve.sem_inc(row_out[b], PARTS * 2 * 16)
            with dve.Fori(0, 2) as l:
                for b in range(BLOCKS):
                    n = l * BLOCKS + b
                    dve.wait_ge(ada_used, n * KT + 2 * KT)
                    dve.wait_ge(bias_in[b], l * (PARTS * 16) + PARTS * 16)
                    dve.wait_ge(row_out[b], l * (PARTS * 32) + PARTS * 32)
                    dve.tensor_tensor(row[b], s.psum[b][:, :], bias[b], ALU.add).then_inc(row_ready, 1)


RW_LORA = 64
RW_GATE = 160
HEAD = 64
RW_LN_EPS = 64e-5
TOK = 2 * L
CH = D // P
HALF_DECAY = math.exp(-0.5)


class RwkvTensors:

    def __init__(self, s):
        s.at = 0
        self.xk, self.xv = s.take(KT, TOK), s.take(KT, TOK)
        self.xr = s.take(KT, L)
        self.wl, self.al = s.take(TOK), s.take(TOK)
        self.gl = s.take(2, L)
        self.oT = s.take(CH, L)
        self.chv = s.take(9, CH)
        self.after = s.at


def rwkv_inputs(s, r, ins, mods):
    nc = s.nc
    s.at = r.after
    hT = s.take(KT * 2, L + 2)
    xx = s.take(KT * 2, L)
    xw, xa = s.take(KT, TOK), s.take(KT, TOK)
    xg = s.take(KT, L)
    w1, a1 = s.take(KT, 2, RW_LORA), s.take(KT, 2, RW_LORA)
    g1 = s.take(KT, RW_GATE)
    ctxn = xw.rearrange("p (i a) b -> p i (a b)", i=4)[:, 0:TT]
    xn = xa.rearrange("p (i a) b -> p i (a b)", i=4)[:, 0:TT]
    xx_n = xx.rearrange("p (i a) b -> p i (a b)", i=4)[:, 2:4]
    junk = xx.rearrange("p a b -> p (a b)")[:, 0:D]
    rows = xg.rearrange("p a b -> p (a b)")[:, 0:P]
    mix = s.take(6, KT)
    sc, sh, ng = s.take(2, KT), s.take(2, KT), s.take(KT)
    stat = s.take(4)
    tok_in, vec_in, rows_in, w_in = s.sem("tok_in"), s.sem("vec_in"), s.sem("chrow_in"), s.sem("lora_in")
    sq_done, var_done, root_done, xn_ready = s.sem("sq_done"), s.sem("var_done"), s.sem("root1"), s.sem("xn_ready")
    scale_ready, xnT_done, hT_ready = s.sem("scale_ready"), s.sem("xnT_done"), s.sem("hT_ready")
    chv_done, pad_done, mixed = s.sem("chv_done"), s.sem("pad_done"), s.sem("mixed")
    lora_done, lora_out = s.sem("lora_done"), s.sem("lora_out")
    order = ("w", "a", "g", "k", "v", "r")
    which = {"r": 0, "w": 1, "k": 2, "v": 3, "a": 4, "g": 5}
    dst = {"r": r.xr, "w": xw, "k": r.xk, "v": r.xv, "a": xa, "g": xg}
    tiles = [(ctxn, 0), (ctxn, 1), (s.x_res, 0), (s.x_res, 1)]

    with nc.Block(name="rwkv_inputs", no_gpsimd_drain=True) as block:

        @block.sync
        def _(sp):
            sp.dma_start(ctxn, ins["ctx"].rearrange("b (i p) d -> p (b i) d", p=P)).then_inc(tok_in, 16)
            sp.dma_start(s.x_res, ins["x"].rearrange("b (i p) d -> p (b i) d", p=P)).then_inc(tok_in, 16)
            for i in range(2):
                sp.dma_start(sc[:, i], mods[0, 1 - i, D:2 * D].rearrange("(p t) -> p t", t=KT)).then_inc(vec_in, 16)
                sp.dma_start(sh[:, i], mods[0, 1 - i, 0:D].rearrange("(p t) -> p t", t=KT)).then_inc(vec_in, 16)
            sp.dma_start(ng, ins["norm_g"][0, 0].rearrange("(p t) -> p t", t=KT)).then_inc(vec_in, 16)
            sp.dma_start(mix, ins["rw_mix"][0].rearrange("n (p t) -> p n t", t=KT)).then_inc(vec_in, 16)
            for z in range(2):
                sp.dma_start(w1[:, :, z], ins["rw_w1"][0, z].rearrange("(p t) r -> p t r", t=KT)).then_inc(w_in, 16)
                sp.dma_start(a1[:, :, z], ins["rw_a1"][0, z].rearrange("(p t) r -> p t r", t=KT)).then_inc(w_in, 16)
            sp.dma_start(g1, ins["rw_g1"][0].rearrange("(p t) r -> p t r", t=KT)).then_inc(w_in, 16)
            vecs = [ins["rw_w0"][0, 0], ins["rw_w0"][0, 1], ins["rw_a0"][0, 0], ins["rw_a0"][0, 1], ins["rw_kk"][0],
                    ins["rw_ka"][0], ins["rw_lnw"][0], ins["rw_lnb"][0], ins["rw_rk"][0].rearrange("h k -> (h k)")]
            for n, v in enumerate(vecs):
                sp.dma_start(rows[n * CH:(n + 1) * CH, :], v.rearrange("(m p) -> m p", p=P)).then_inc(rows_in, 16)

        @block.scalar
        def _(act):
            act.wait_ge(tok_in, 32)
            for n, (src, i) in enumerate(tiles):
                act.activation(junk, src[:, i], ACT.Square, accum_out=stat[:, n:n + 1])
                act.drain()
            act.sem_inc(sq_done, 1)
            act.wait_ge(var_done, 1)
            act.activation(stat, stat, ACT.Sqrt).then_inc(root_done, 1)
            act.wait_ge(scale_ready, 1)
            for t in range(KT):
                act.wait_ge(xnT_done, t + 1)
                for i in range(2):
                    act.activation(hT[:, t * 2 + i, 1:L + 1], s.psum[t][:, i * L:(i + 1) * L], ACT.Identity,
                                   bias=sh[:, i, t:t + 1], scale=sc[:, i, t:t + 1]).then_inc(hT_ready, 1)
            act.wait_ge(lora_done, 1)
            act.activation(r.wl, s.psum[0][:, :], ACT.Tanh)
            act.wait_ge(lora_done, 2)
            act.activation(r.al, s.psum[1][:, :], ACT.Copy)
            act.wait_ge(lora_done, 3)
            act.activation(r.gl[:, 0], s.psum[2][:, 0:L], ACT.Sigmoid)
            act.activation(r.gl[0:RW_GATE - P, 1], s.psum[2][0:RW_GATE - P, L:2 * L], ACT.Sigmoid)

        @block.tensor
        def _(pe):
            pe.wait_ge(rows_in, 9 * 16)
            pe.transpose(s.psum[7][:, 0:9 * CH], rows[0:9 * CH, :], s.c("ident")[0:9 * CH, 0:9 * CH]).then_inc(chv_done, 1)
            pe.wait_ge(xn_ready, 4)
            pe.wait_ge(chv_done, 2)
            for t in range(KT):
                for n in range(4):
                    src = xn[:, n, t::KT] if n < 2 else xx_n[:, n - 2, t::KT]
                    mm = pe.transpose(s.psum[t][:, n * P:(n + 1) * P], src, s.c("ident"))
                mm.then_inc(xnT_done, 1)
            pe.wait_ge(w_in, 5 * 16)
            pe.wait_ge(hT_ready, 2 * KT)
            for n, (w, x, bank) in enumerate(((w1, xw, 0), (a1, xa, 1))):
                pe.wait_ge(mixed, n + 1)
                for t in range(KT):
                    mm = pe.matmul(s.psum[bank][:, :], w[:, t].rearrange("p a b -> p (a b)"), x[:, t], start=(t == 0), stop=(t == KT - 1))
                mm.then_inc(lora_done, 1)
            pe.wait_ge(mixed, 3)
            for t in range(KT):
                pe.matmul(s.psum[2][:, 0:L], g1[:, t, 0:P], xg[:, t], start=(t == 0), stop=(t == KT - 1))
            for t in range(KT):
                mm = pe.matmul(s.psum[2][0:RW_GATE - P, L:2 * L], g1[:, t, P:RW_GATE], xg[:, t], start=(t == 0), stop=(t == KT - 1))
            mm.then_inc(lora_done, 1)

        @block.vector
        def _(dve):
            dve.memset(hT[:, :, 0:1], 0.0)
            dve.memset(hT[:, :, L + 1:L + 2], 0.0)
            dve.wait_ge(chv_done, 1)
            dve.tensor_copy(r.chv.rearrange("p a b -> p (a b)"), s.psum[7][:, 0:9 * CH]).then_inc(chv_done, 1)
            dve.wait_ge(vec_in, 6 * 16)
            dve.tensor_scalar(sc, sc, 1.0, None, ALU.add)
            dve.drain()
            dve.tensor_tensor(sc, sc, ng.unsqueeze(1).to_broadcast([P, 2, KT]), ALU.mult).then_inc(scale_ready, 1)
            dve.wait_ge(sq_done, 1)
            dve.tensor_scalar(stat, stat, 1.0 / D, NORM_EPS, ALU.mult, ALU.add).then_inc(var_done, 1)
            dve.wait_ge(root_done, 1)
            dve.reciprocal(stat, stat)
            dve.drain()
            for n, (src, i) in enumerate(tiles):
                out = xn[:, n] if n < 2 else xx_n[:, n - 2]
                dve.tensor_scalar(out, src[:, i], stat[:, n:n + 1], None, ALU.mult).then_inc(xn_ready, 1)
            dve.wait_ge(hT_ready, 2 * KT)
            dve.drain()
            dve.tensor_tensor(xx, hT[:, :, 0:L], hT[:, :, 2:L + 2], ALU.add)
            dve.drain()
            dve.scalar_tensor_tensor(xx, xx, 0.5, hT[:, :, 1:L + 1], ALU.mult, ALU.subtract)
            dve.drain()
            for name in order:
                k = which[name]
                for t in range(KT):
                    if name in "rg":
                        args = (dst[name][:, t], xx[:, t * 2 + 1], mix[:, k, t:t + 1], hT[:, t * 2 + 1, 1:L + 1])
                    else:
                        args = (dst[name][:, t].rearrange("p (i c) -> p i c", i=2), xx[:, t * 2:t * 2 + 2],
                                mix[:, k, t:t + 1], hT[:, t * 2:t * 2 + 2, 1:L + 1])
                    op = dve.scalar_tensor_tensor(*args, ALU.mult, ALU.add)
                op.then_inc(mixed, 1)


STEPS = TOK // P
CHUNK = [[0, 1, 2, 3], [1, 0, 3, 2]]
LEVELS = 7


def rwkv_heads(s, r, ins):
    nc = s.nc
    s.at = r.after
    wkv = [s.take(KT, P) for _ in range(3)]
    w2, a2 = s.take(P), s.take(P)
    g2 = s.take(2, P)
    cv = s.take(16)
    kT, vT, kk = s.take(TOK), s.take(TOK), s.take(TOK)
    rT, gT = s.take(L), s.take(L)
    sg = [s.take(TOK) for _ in range(2)]
    av = [s.take(TOK) for _ in range(2)]
    kd = [s.take(TOK) for _ in range(2)]
    cum, dif, dex = s.take(TOK), s.take(TOK), s.take(TOK)
    ex = [s.take(TOK) for _ in range(3)]
    fade = [s.take(4) for _ in range(2)]
    farg = s.take(4)
    fdif = s.take(4)
    reset = s.take(TOK)
    A = [s.take(TOK) for _ in range(2)]
    B = [s.take(TOK) for _ in range(2)]
    K = [s.take(TOK) for _ in range(2)]
    R = [s.take(L) for _ in range(2)]
    padAR = [s.take(4, TOK) for _ in range(2)]
    padB = [s.take(2, TOK) for _ in range(2)]
    Btok = [s.take(STEPS, P) for _ in range(2)]
    Ktok = [s.take(STEPS, P) for _ in range(2)]
    Vtok = s.take(STEPS, P)
    Lm = [s.take(2, P) for _ in range(2)]
    X = [s.take(2, P) for _ in range(2)]
    XT = [[s.take(2, P) for _ in range(2)] for _ in range(2)]
    Zm = [s.take(2, P) for _ in range(2)]
    LakT = [[s.take(2, P) for _ in range(2)] for _ in range(2)]
    ArkT = [[s.take(2, P) for _ in range(2)] for _ in range(2)]
    ArbT = [[s.take(2, P) for _ in range(2)] for _ in range(2)]
    G, U = s.take(2, P), s.take(2, P)
    H, Hn = s.take(2, P), s.take(2, P)
    yt = s.take(TT, P)
    yc, ysq = s.take(TT, P), s.take(TT, P)
    st = s.take(8)
    bon = s.take(L)
    sq, nrm = ex[0], ex[1]

    w_in = s.sem("rw_w_in")
    cv_ready, sq_ready, v_ready = s.sem("cv_ready"), s.sem("sq_ready"), s.sem("v_ready")
    proj_done, norm_done, nrm_ready = s.sem("proj_done"), s.sem("norm_done"), s.sem("nrm_ready")
    sig_ready, g_ready, dec_ready, ex_ready = s.sem("sig_ready"), s.sem("g_ready"), s.sem("dec_ready"), s.sem("ex_ready")
    ex_used, feat_ready, pad_ready = s.sem("ex_used"), s.sem("feat_ready"), s.sem("pad_ready")
    pad_begun = s.sem("pad_begun")
    turned, tok_ready = s.sem("turned"), s.sem("tok_ready")
    prod_done, prod_read = s.sem("prod_done"), s.sem("prod_read")
    xt0_done, xt0_ready = s.sem("xt0_done"), s.sem("xt0_ready")
    z_done, z_ready, x_done, x_ready = s.sem("z_done"), s.sem("z_ready"), s.sem("x_done"), s.sem("x_ready")
    g_done, gs_ready, u_done, us_ready = s.sem("chG_done"), s.sem("chG_ready"), s.sem("chU_done"), s.sem("chU_ready")
    hy_done, h_ready = s.sem("chHY_done"), s.sem("chH_ready")
    bsum_in, yvar, yroot, yn_ready, yT_done, m_done = (s.sem(n) for n in
        ("bonus_in", "y_var", "y_root", "yn_ready", "yT_done", "m_done"))

    PB, QB, ZB, XB, CB = (0, 6), 1, (2, 3), (4, 5), 7

    def two(v):
        return v.unsqueeze(1).to_broadcast([P, 2, P])

    def pair_view(bank, z):
        return bank[:, z * 256:(z + 1) * 256].rearrange("p (h c) -> p h c", h=2)

    def flat(v):
        return v.rearrange("p a b -> p (a b)")

    def cols(j, z):
        c = CHUNK[z][j]
        return slice(c * P, (c + 1) * P)

    with nc.Block(name="rwkv_heads", no_gpsimd_drain=True) as block:

        @block.sync
        def _(sp):
            col = [ins["rw_wrkv"][0, n].rearrange("(p t) c -> p t c", t=KT) for n in range(3)]
            low = [ins["rw_w2"][0].rearrange("z r c -> (z r) c"), ins["rw_a2"][0].rearrange("z r c -> (z r) c"),
                   ins["rw_g2"][0, 0:P], ins["rw_g2"][0, P:RW_GATE]]
            with sp.Fori(0, CH) as m:
                sp.wait_ge(proj_done, m * 8 + 1)
                at = bass.ds(m * P, P)
                for n in range(3):
                    sp.dma_start(wkv[n], col[n][:, :, at]).then_inc(w_in, 16)
                sp.dma_start(w2, low[0][:, at]).then_inc(w_in, 16)
                sp.dma_start(a2, low[1][:, at]).then_inc(w_in, 16)
                sp.dma_start(g2[:, 0], low[2][:, at]).then_inc(w_in, 16)
                sp.dma_start(g2[0:RW_GATE - P, 1], low[3][:, at]).then_inc(w_in, 16)

        @block.gpsimd
        def _(pool):
            for z in range(2):
                pool.memset(padAR[z], 0.0)
                pool.memset(padB[z], 0.0)
            pool.drain()
            with pool.Fori(0, CH) as m:
                for z in range(2):
                    pool.wait_ge(feat_ready, m * 2 + (z + 1))
                    pool.sem_inc(pad_begun, 1)
                    for h in range(2):
                        rows = slice(h * HEAD, (h + 1) * HEAD)
                        pool.tensor_copy(padB[z][rows, h], B[z][rows])
                        pool.tensor_copy(padAR[z][rows, h], A[z][rows])
                        op = pool.tensor_copy(padAR[z][rows, 2 + h, L:TOK], R[z][rows])
                    pool.drain()
                    pool.sem_inc(pad_ready, 1)

        @block.tensor
        def _(pe):
            pe.sem_inc(proj_done, 1)

            def project(m):
                pe.wait_ge(w_in, m * 112 + 112)
                pe.wait_ge(m_done, m + 1)
                for bank, n, x, c0, n_c in ((0, 1, r.xk, 0, TOK), (1, 2, r.xv, 0, TOK), (2, 0, r.xr, 0, L)):
                    for t in range(KT):
                        mm = pe.matmul(s.psum[bank][:, 0:n_c], wkv[n][:, t], x[:, t], start=(t == 0), stop=(t == KT - 1))
                    mm.then_inc(proj_done, 1)
                for bank, w, x in ((3, w2, r.wl), (5, a2, r.al)):
                    for z in range(2):
                        rows = slice(z * RW_LORA, (z + 1) * RW_LORA)
                        pe.matmul(s.psum[bank + z][:, :], w[rows, :], x[rows, :], start=True, stop=True).then_inc(proj_done, 1)
                pe.matmul(s.psum[2][:, L:TOK], g2[:, 0], r.gl[:, 0], start=True, stop=False)
                rows = slice(0, RW_GATE - P)
                pe.matmul(s.psum[2][:, L:TOK], g2[rows, 1], r.gl[rows, 1], start=False, stop=True).then_inc(proj_done, 1)
                pe.wait_ge(sq_ready, m + 1)
                pe.matmul(s.psum[7][:, :], s.c("head_ones"), sq, start=True, stop=True).then_inc(norm_done, 1)

            def turn(m):
                pe.wait_ge(v_ready, m + 1)
                for n, src in enumerate((vT, B[0], K[0], B[1], K[1])):
                    if n in (1, 3):
                        pe.wait_ge(feat_ready, m * 2 + (n + 1) // 2)
                    for c in range(STEPS):
                        mm = pe.transpose(s.psum[(1, 3, 4, 5, 6)[n]][:, c * P:(c + 1) * P], src[:, c * P:(c + 1) * P], s.c("ident"))
                    mm.then_inc(turned, 1)

            def products(m, j):
                for z in range(2):
                    q = 4 if j >= 2 else 2
                    pe.wait_ge(pad_ready, m * 2 + (z + 1))
                    if z == 0 and j == 0:
                        pe.wait_ge(tok_ready, m * 5 + 5)
                    c = cols(j, z)
                    pe.matmul(s.psum[PB[z]][:, 0:q * P], K[z][:, c], padAR[z][:, 0:q, c], start=True, stop=True)
                    if z or j:
                        pe.wait_ge(prod_read, m * 8 + (j * 2 + z))
                    mm = pe.matmul(s.psum[QB][:, 0:2 * P], A[z][:, c], padB[z][:, :, c], start=True, stop=True)
                    if j >= 2:
                        mm = pe.matmul(s.psum[QB][:, 2 * P:4 * P], B[z][:, c], padAR[z][:, 2:4, c], start=True, stop=True)
                    mm.then_inc(prod_done, 1)

            def chain_G(m, j):
                pe.wait_ge(h_ready, m * 8 + (2 * j + 2))
                for z in range(2):
                    for h in range(2):
                        o = slice(h * HEAD, (h + 1) * HEAD)
                        out = s.psum[CB][:, z * P + h * HEAD:z * P + (h + 1) * HEAD]
                        pe.matmul(out, A[z][:, cols(j, z)], H[:, z, o], start=True, stop=False)
                        mm = pe.matmul(out, LakT[j % 2][z][:, h], Vtok[:, CHUNK[z][j], o], start=False, stop=True)
                mm.then_inc(g_done, 1)

            def chain_U(m, j):
                pe.wait_ge(gs_ready, m * 4 + (j + 1))
                for z in range(2):
                    for h in range(2):
                        o = slice(h * HEAD, (h + 1) * HEAD)
                        mm = pe.matmul(s.psum[CB][:, 256 + z * P + h * HEAD:256 + z * P + (h + 1) * HEAD], XT[j % 2][z][:, h],
                                       G[:, z, o], start=True, stop=True)
                mm.then_inc(u_done, 1)

            def chain_HY(m, j):
                pe.wait_ge(us_ready, m * 4 + (j + 1))
                for z in range(2):
                    c = CHUNK[z][j]
                    if j < STEPS - 1:
                        pe.matmul(s.psum[CB][:, z * P:(z + 1) * P], Btok[z][:, c], U[:, z], start=True, stop=False)
                        mm = pe.matmul(s.psum[CB][:, z * P:(z + 1) * P], Ktok[z][:, c], Vtok[:, c], start=False, stop=True)
                    if j >= 2:
                        y = s.psum[CB][:, 256 + z * P:256 + (z + 1) * P]
                        for h in range(2):
                            o = slice(h * HEAD, (h + 1) * HEAD)
                            pe.matmul(y[:, o], R[z][:, (c - 2) * P:(c - 1) * P], H[:, z, o], start=True, stop=False)
                            pe.matmul(y[:, o], ArbT[j % 2][z][:, h], U[:, z, o], start=False, stop=False)
                            mm = pe.matmul(y[:, o], ArkT[j % 2][z][:, h], Vtok[:, c, o], start=False, stop=True)
                mm.then_inc(hy_done, 1)

            def invert(m, j, between):
                for z in range(2):
                    pe.wait_ge(prod_read, m * 8 + (j * 2 + z + 1))
                    for h in range(2):
                        mm = pe.transpose(s.psum[XB[z]][:, 256 + h * P:256 + (h + 1) * P], X[z][:, h], s.c("ident"))
                    mm.then_inc(xt0_done, 1)
                for n in range(1, LEVELS):
                    for z in range(2):
                        if n == 1:
                            pe.wait_ge(xt0_ready, m * 8 + (j * 2 + z + 1))
                        else:
                            pe.wait_ge(x_ready, m * 48 + (j * 12 + (n - 2) * 2 + z + 1))
                        for h in range(2):
                            mm = pe.matmul(s.psum[ZB[z]][:, h * P:(h + 1) * P], Lm[z][:, h], XT[j % 2][z][:, h],
                                           start=True, stop=True)
                        mm.then_inc(z_done, 1)
                    if n in between:
                        between[n]()
                    for z in range(2):
                        pe.wait_ge(z_ready, m * 48 + (j * 12 + (n - 1) * 2 + z + 1))
                        for h in range(2):
                            mm = pe.matmul(s.psum[XB[z]][:, 256 + h * P:256 + (h + 1) * P], X[z][:, h], Zm[z][:, h], start=True, stop=True)
                            if n < LEVELS - 1:
                                mm = pe.matmul(s.psum[XB[z]][:, h * P:(h + 1) * P], Zm[z][:, h], X[z][:, h], start=True, stop=True)
                        mm.then_inc(x_done, 1)

            with pe.Fori(0, CH) as m:
                project(m)
                turn(m)
                for j in range(STEPS):
                    products(m, j)
                    between = {}
                    if j:
                        between = {1: lambda: chain_G(m, j - 1), 3: lambda: chain_U(m, j - 1), 5: lambda: chain_HY(m, j - 1)}
                    invert(m, j, between)
                j = STEPS - 1
                pe.wait_ge(x_ready, m * 48 + 48)
                chain_G(m, j)
                chain_U(m, j)
                chain_HY(m, j)
                pe.wait_ge(bsum_in, m + 1)
                pe.matmul(s.psum[0][:, 0:L], s.c("head_ones"), bon, start=True, stop=True)
                pe.wait_ge(yn_ready, m + 1)
                for c in range(TT):
                    mm = pe.transpose(s.psum[1][:, c * P:(c + 1) * P], yc[:, c], s.c("ident"))
                mm.then_inc(yT_done, 1)

        @block.scalar
        def _(act):
            def features(m):
                act.wait_ge(m_done, m + 1)
                act.wait_ge(cv_ready, m + 1)
                act.wait_ge(proj_done, m * 8 + 2)
                act.activation(sq, s.psum[0][:, :], ACT.Square, scale=cv[:, 4:5]).then_inc(sq_ready, 1)
                act.activation(kT, s.psum[0][:, :], ACT.Copy)
                act.wait_ge(proj_done, m * 8 + 3)
                act.activation(vT, s.psum[1][:, :], ACT.Copy).then_inc(v_ready, 1)
                act.wait_ge(proj_done, m * 8 + 9)
                act.activation(gT, s.psum[2][:, L:TOK], ACT.Copy)
                act.activation(rT, s.psum[2][:, 0:L], ACT.Copy)
                for z in range(2):
                    act.wait_ge(proj_done, m * 8 + (5 + z))
                    act.activation(sg[z], s.psum[3 + z][:, :], ACT.Sigmoid, bias=cv[:, z:z + 1]).then_inc(sig_ready, 1)
                for z in range(2):
                    act.wait_ge(proj_done, m * 8 + (7 + z))
                    act.activation(av[z], s.psum[5 + z][:, :], ACT.Sigmoid, bias=cv[:, 2 + z:3 + z]).then_inc(sig_ready, 1)
                act.wait_ge(norm_done, m + 1)
                act.activation(nrm, s.psum[7][:, :], ACT.Sqrt).then_inc(nrm_ready, 1)
                for z in range(2):
                    act.wait_ge(dec_ready, m * 2 + (z + 1))
                    act.wait_ge(ex_used, m * 2 + (z + 1))
                    inner, sign = (dex, 1.0) if z == 0 else (dif, -1.0)
                    last, sign_last = (dif, 1.0) if z == 0 else (dex, -1.0)
                    act.activation(ex[0], inner, ACT.Exp, scale=sign)
                    act.activation(ex[1][:, L:TOK], last[:, L:TOK], ACT.Exp, scale=sign_last)
                    act.activation(ex[2], last, ACT.Exp, scale=-sign_last)
                    act.activation(fade[z][:, 0:3], farg[:, 0:3], ACT.Exp).then_inc(ex_ready, 1)

            def evacuate(m):
                for n, dst in enumerate((Vtok, Btok[0], Ktok[0], Btok[1], Ktok[1])):
                    act.wait_ge(turned, m * 5 + (n + 1))
                    act.activation(flat(dst), s.psum[(1, 3, 4, 5, 6)[n]][:, :], ACT.Copy).then_inc(tok_ready, 1)

            def turned_x(m, j):
                for z in range(2):
                    act.wait_ge(xt0_done, m * 8 + (j * 2 + z + 1))
                    act.activation(flat(XT[j % 2][z]), s.psum[XB[z]][:, 256:512], ACT.Copy).then_inc(xt0_ready, 1)

            def chain(m, j):
                act.wait_ge(g_done, m * 4 + (j + 1))
                act.activation(flat(G), s.psum[CB][:, 0:2 * P], ACT.Copy).then_inc(gs_ready, 1)
                act.wait_ge(u_done, m * 4 + (j + 1))
                act.activation(flat(U), s.psum[CB][:, 2 * P:4 * P], ACT.Copy).then_inc(us_ready, 1)

            with act.Fori(0, CH) as m:
                features(m)
                evacuate(m)
                for j in range(STEPS):
                    turned_x(m, j)
                    if j:
                        chain(m, j - 1)
                chain(m, STEPS - 1)
                act.wait_ge(yvar, m + 1)
                act.activation(st[:, 4:8], st[:, 4:8], ACT.Sqrt).then_inc(yroot, 1)

        @block.vector
        def _(dve):
            dve.memset(reset, 1.0)
            dve.drain()
            dve.memset(reset.rearrange("p (c t) -> p c t", c=STEPS)[:, :, 0:1], 0.0)
            dve.sem_inc(m_done, 1)
            dve.drain()

            def by_chunk(v):
                return v.rearrange("p (c t) -> p c t", c=STEPS)

            def features(m):
                dve.tensor_copy(cv[:, 0:9], r.chv[:, :, bass.ds(m, 1)].rearrange("p n o -> p (n o)"))
                dve.drain()
                dve.tensor_scalar(cv[:, 9:10], cv[:, 5:6], -1.0, 1.0, ALU.mult, ALU.add)
                dve.drain()
                dve.sem_inc(cv_ready, 1)
                dve.wait_ge(nrm_ready, m + 1)
                dve.tensor_scalar(nrm, nrm, 1e-12, None, ALU.max)
                dve.drain()
                dve.reciprocal(nrm, nrm)
                dve.drain()
                dve.scalar_tensor_tensor(kk, kT, cv[:, 4:5], nrm, ALU.mult, ALU.mult)
                dve.drain()
                dve.sem_inc(ex_used, 1)
                for z in range(2):
                    dve.tensor_scalar(sg[z], sg[z], -HALF_DECAY, None, ALU.mult)
                    dve.tensor_scalar(kd[z], av[z], cv[:, 5:6], cv[:, 9:10], ALU.mult, ALU.add)
                    dve.drain()
                    if z:
                        dve.wait_ge(ex_ready, m * 2 + 1)
                    dve.tensor_tensor_scan(cum, reset, sg[z], 0.0, ALU.mult, ALU.add)
                    dve.tensor_tensor(kd[z], kd[z], kT, ALU.mult)
                    dve.tensor_tensor(av[z], av[z], kk, ALU.mult)
                    dve.drain()
                    mid, end = by_chunk(cum)[:, :, HEAD - 1:HEAD], by_chunk(cum)[:, :, P - 1:P]
                    dve.tensor_tensor(by_chunk(dif), by_chunk(cum), mid.to_broadcast([P, STEPS, P]), ALU.subtract)
                    dve.tensor_tensor(fdif.unsqueeze(2), end, mid, ALU.subtract)
                    dve.drain()
                    dve.tensor_tensor(dex, dif, sg[z], ALU.subtract)
                    if z == 0:
                        dve.tensor_tensor(farg[:, 0:3].unsqueeze(2), fdif[:, 0:3].unsqueeze(2), mid[:, 1:4], ALU.add)
                    else:
                        for n in range(3):
                            a, b = CHUNK[1][n], CHUNK[1][n + 1]
                            dve.tensor_tensor(farg[:, n:n + 1].unsqueeze(2), mid[:, a:a + 1], fdif[:, b:b + 1].unsqueeze(2), ALU.add)
                    dve.drain()
                    dve.sem_inc(dec_ready, 1)
                    dve.wait_ge(ex_ready, m * 2 + (z + 1))
                    dve.scalar_tensor_tensor(A[z], kk, -1.0, ex[0], ALU.mult, ALU.mult)
                    dve.tensor_tensor(B[z], av[z], ex[2], ALU.mult)
                    dve.tensor_tensor(K[z], kd[z], ex[2], ALU.mult)
                    dve.tensor_tensor(R[z], rT, ex[1][:, L:TOK], ALU.mult)
                    dve.drain()
                    dve.sem_inc(feat_ready, 1)
                    if z == 0:
                        dve.sem_inc(ex_used, 1)
                dve.tensor_tensor(bon, kd[0][:, L:TOK], kd[1][:, L:TOK], ALU.add)
                dve.drain()
                dve.scalar_tensor_tensor(bon, bon, cv[:, 8:9], rT, ALU.mult, ALU.mult).then_inc(bsum_in, 1)

            def masked(m, j):
                for z in range(2):
                    strict, strict_T, incl_T = (("after", "before", "upto"), ("before", "after", "from"))[z]
                    dve.wait_ge(prod_done, m * 8 + (j * 2 + z + 1))
                    if j:
                        dve.wait_ge(x_done, m * 48 + (j * 12))
                    dve.tensor_tensor(Lm[z], pair_view(s.psum[QB], 0), two(s.c(strict)), ALU.mult)
                    dve.tensor_tensor(LakT[j % 2][z], pair_view(s.psum[PB[z]], 0), two(s.c(strict_T)), ALU.mult)
                    if j >= 2:
                        dve.tensor_tensor(ArkT[j % 2][z], pair_view(s.psum[PB[z]], 1), two(s.c(incl_T)), ALU.mult)
                        dve.tensor_tensor(ArbT[j % 2][z], pair_view(s.psum[QB], 1), two(s.c(incl_T)), ALU.mult)
                    dve.drain()
                    dve.tensor_tensor(X[z], Lm[z], two(s.c(("low0", "up0")[z])), ALU.mult)
                    dve.drain()
                    dve.tensor_tensor(X[z], X[z], two(s.c("ident")), ALU.add).then_inc(prod_read, 1)

            def level(m, j, n):
                for z in range(2):
                    dve.wait_ge(z_done, m * 48 + (j * 12 + (n - 1) * 2 + z + 1))
                    dve.tensor_tensor(Zm[z], pair_view(s.psum[ZB[z]], 0), two(s.c(("up", "low")[z] + str(n))), ALU.mult).then_inc(z_ready, 1)
                for z in range(2):
                    dve.wait_ge(x_done, m * 48 + (j * 12 + (n - 1) * 2 + z + 1))
                    if n < LEVELS - 1:
                        dve.tensor_tensor(X[z], pair_view(s.psum[XB[z]], 0), X[z], ALU.add)
                    dve.tensor_tensor(XT[j % 2][z], pair_view(s.psum[XB[z]], 1), XT[j % 2][z], ALU.add).then_inc(x_ready, 1)

            def state(m, j):
                dve.wait_ge(hy_done, m * 4 + (j + 1))
                for z in range(2):
                    dve.tensor_tensor(Hn[:, z], s.psum[CB][:, z * P:(z + 1) * P], H[:, z], ALU.add)
                dve.drain()
                for z in range(2):
                    dve.scalar_tensor_tensor(H[:, z], Hn[:, z], fade[z][:, j:j + 1], s.c("head_ones"), ALU.mult, ALU.mult).then_inc(h_ready, 1)

            def rows(m, j):
                dve.wait_ge(hy_done, m * 4 + (j + 1))
                for z in range(2):
                    y, dst = s.psum[CB][:, 256 + z * P:256 + (z + 1) * P], yt[:, CHUNK[z][j] - 2]
                    if j == 2:
                        dve.tensor_copy(dst, y)
                    else:
                        dve.tensor_tensor(dst, y, dst, ALU.add)
                dve.drain()

            with dve.Fori(0, CH) as m:
                features(m)
                dve.memset(H, 0.0)
                dve.drain()
                dve.sem_inc(h_ready, 2)
                for j in range(STEPS):
                    masked(m, j)
                    for n in range(1, LEVELS):
                        level(m, j, n)
                        if n == 5 and j:
                            pass
                    if j:
                        if j - 1 >= 2:
                            rows(m, j - 1)
                        state(m, j - 1)
                rows(m, STEPS - 1)
                y4, c4, q4 = (v.rearrange("p c (h k) -> p (c h) k", h=2) for v in (yt, yc, ysq))
                dve.tensor_reduce(st[:, 0:4], y4, AX.X, ALU.add)
                dve.drain()
                dve.tensor_scalar(st[:, 0:4], st[:, 0:4], 1.0 / HEAD, None, ALU.mult)
                dve.drain()
                dve.tensor_tensor(c4, y4, st[:, 0:4].unsqueeze(2).to_broadcast([P, 4, HEAD]), ALU.subtract)
                dve.drain()
                dve.tensor_tensor(q4, c4, c4, ALU.mult)
                dve.drain()
                dve.tensor_reduce(st[:, 4:8], q4, AX.X, ALU.add)
                dve.drain()
                dve.tensor_scalar(st[:, 4:8], st[:, 4:8], 1.0 / HEAD, RW_LN_EPS, ALU.mult, ALU.add).then_inc(yvar, 1)
                dve.wait_ge(yroot, m + 1)
                dve.reciprocal(st[:, 4:8], st[:, 4:8])
                dve.drain()
                dve.tensor_tensor(c4, c4, st[:, 4:8].unsqueeze(2).to_broadcast([P, 4, HEAD]), ALU.mult).then_inc(yn_ready, 1)
                dve.wait_ge(yT_done, m + 1)
                dve.tensor_tensor(bon, s.psum[0][:, 0:L], vT[:, L:TOK], ALU.mult)
                dve.drain()
                dve.scalar_tensor_tensor(bon, s.psum[1][:, 0:L], cv[:, 6:7], bon, ALU.mult, ALU.add)
                dve.drain()
                dve.scalar_tensor_tensor(r.oT[:, bass.ds(m, 1)].rearrange("p o c -> p (o c)"), bon, cv[:, 7:8], gT, ALU.add, ALU.mult)
                dve.drain()
                dve.sem_inc(m_done, 1)


def rwkv_output(s, r, ins, mods):
    nc = s.nc
    s.at = r.after
    wo = s.take(CH, D)
    gate = s.take(D)
    g_in, o_done = s.sem("gate1_in"), s.sem("wo_done")
    wo_in = [s.sem(f"wo_in{h}") for h in range(2)]
    with nc.Block(name="rwkv_output", no_gpsimd_drain=True) as block:

        @block.sync
        def _(sp):
            sp.dma_start(gate, mods[0, 0, 2 * D:3 * D].partition_broadcast(P)).then_inc(g_in, 16)
            src = ins["rw_wo"][0].rearrange("(m p) n -> p m n", p=P)
            for h in range(2):
                sp.dma_start(wo[:, 4 * h:4 * h + 4], src[:, 4 * h:4 * h + 4]).then_inc(wo_in[h], 16)

        @block.tensor
        def _(pe):
            for m in range(CH):
                if m % 4 == 0:
                    pe.wait_ge(wo_in[m // 4], 16)
                for i in range(TT):
                    for h in range(2):
                        mm = pe.matmul(s.psum[i * 2 + h][:, :], r.oT[:, m, i * P:(i + 1) * P], wo[:, m, h * 512:(h + 1) * 512],
                                       start=(m == 0), stop=(m == CH - 1))
                        if m == CH - 1:
                            mm.then_inc(o_done, 1)

        @block.vector
        def _(dve):
            dve.wait_ge(g_in, 16)
            tmp = r.xk.rearrange("p a b -> p (a b)")
            for i in range(TT):
                for h in range(2):
                    k = i * 2 + h
                    c = slice(h * 512, (h + 1) * 512)
                    dve.wait_ge(o_done, k + 1)
                    dve.tensor_tensor(tmp[:, k * 512:(k + 1) * 512], s.psum[k][:, :], gate[:, c], ALU.mult)
                    dve.drain()
                    dve.tensor_tensor(s.x_res[:, i, c], s.x_res[:, i, c], tmp[:, k * 512:(k + 1) * 512], ALU.add)


def expert_layer(s, layer, ins, mods):
    nc = s.nc
    s.at = 0
    wg = [[s.take(KT, HIDDEN) for _ in range(2)] for _ in range(2)]
    wu = [s.take(KT, HIDDEN) for _ in range(2)]
    wd = [s.take(HK, D) for _ in range(2)]
    hx = s.take(TT, D)
    acc = s.take(TT, D)
    xg = s.take(D)
    xT = s.take(KT, P)
    sg = s.take(HIDDEN)
    h = s.take(HIDDEN)
    hT = s.take(HK, P)
    y = s.take(D)
    sel = [s.take(TT, 2, CAP) for _ in range(2)]
    selw = [s.take(TT, 2, CAP) for _ in range(2)]
    selwT = s.take(TT, P)
    NE = EXPERTS + EXTRA
    slot_of = s.take(TT, NE)
    weight_of = s.take(TT, NE)
    router = s.take(KT, GROUPS + EXPERTS)
    router_b = s.take(GROUPS + EXPERTS)
    logit = s.take(TT, GROUPS + EXPERTS)
    glog = s.take(TT, 8)
    top = s.take(TT, 8)
    topi = s.take(TT, 8).bitcast(U32)
    small = s.take(TT, 16)
    member = s.take(TT, EXPERTS)
    tmp = s.take(TT, EXPERTS)
    tmp2 = s.take(TT, EXPERTS)
    cnt = s.take(EXPERTS)
    flag = s.take(3, EXPERTS)
    order = s.take(3 * EXPERTS)
    num = s.take(3, EXPERTS)
    pick = s.take(3 * EXPERTS)
    prod = s.take(3 * EXPERTS)
    base = s.take(TT, 3, EXPERTS)
    wbase = s.take(TT, 3, EXPERTS)
    extra_f = s.take(EXTRA + 1)
    extra_i = s.take(EXTRA + 1).bitcast(I32)
    scale_b = xg
    shift_b = y
    gate_b = wg[0][0].rearrange("p a b -> p (a b)")[:, 0:D]

    G, U, X0, X1, S0, S1, Y0, Y1 = s.psum
    iota = s.c("iota")
    q = f"{layer}_"
    wg_in = [[s.sem(f"{q}wg_in{a}{b}") for b in range(2)] for a in range(2)]
    wu_in = [s.sem(f"{q}wu_in{b}") for b in range(2)]
    wd_in = [s.sem(f"{q}wd_in{b}") for b in range(2)]
    rows_in, router_in, gate_in = s.sem(q + "rows_in"), s.sem(q + "router_in"), s.sem(q + "gate_in")
    squares_done, root_done, hx_ready = s.sem(q + "squares"), s.sem(q + "root"), s.sem(q + "hx")
    hxT_done, hxT_ready, logits_done = s.sem(q + "hxT_done"), s.sem(q + "hxT_ready"), s.sem(q + "logits")
    shifted, exps_done = s.sem(q + "shifted"), s.sem(q + "exps")
    member_ready, rank_done, extra_ready = s.sem(q + "member"), s.sem(q + "rank"), s.sem(q + "extra")
    sel_ready, gath_done, xg_ready = s.sem(q + "sel"), s.sem(q + "gath"), s.sem(q + "xg")
    xgT_done, xT_ready = s.sem(q + "xgT"), s.sem(q + "xT")
    gate_done, up_done, down_done = s.sem(q + "gate"), s.sem(q + "up"), s.sem(q + "down")
    silu_ready, h_ready, hT_done, hT_ready = s.sem(q + "silu"), s.sem(q + "h"), s.sem(q + "hTd"), s.sem(q + "hT")
    y_ready, scat_done, acc_done = s.sem(q + "y"), s.sem(q + "scat"), s.sem(q + "acc")
    all_added = s.sem(q + "all_added")
    w_gate = ins["moe_w_gate"].rearrange("l e (p t) n -> l e p (t n)", t=KT)
    w_up = ins["moe_w_up"].rearrange("l e (p t) n -> l e p (t n)", t=KT)
    w_down = ins["moe_w_down"].rearrange("l e (p t) n -> l e p (t n)", t=HK)

    def flat(v):
        return v.rearrange("p a b -> p (a b)")

    def mod_row(i, k):
        return mods[layer, i, k * D:(k + 1) * D].partition_broadcast(P)

    with nc.Block(name=f"experts{layer}", no_gpsimd_drain=True) as block:

        @block.sync
        def _(sp):
            sp.dma_start(scale_b, mod_row(0, 4)).then_inc(rows_in, 16)
            sp.dma_start(shift_b, mod_row(0, 3)).then_inc(rows_in, 16)
            sp.dma_start(acc[:, 0, :], ins["norm_g"][layer, 1].partition_broadcast(P)).then_inc(rows_in, 16)
            sp.dma_start(router, ins["moe_router"][layer].rearrange("(p t) n -> p t n", t=KT)).then_inc(router_in, 16)
            sp.dma_start(router_b, ins["moe_router_b"][layer].partition_broadcast(P)).then_inc(router_in, 16)

            def load(dst, src, e, sem):
                sp.dma_start(flat(dst), src[layer, e]).then_inc(sem, 16)

            for j in range(2):
                load(wg[0][j], w_gate, j, wg_in[0][j])
            for j in range(2):
                load(wu[j], w_up, j, wu_in[j])
            for j in range(2):
                load(wd[j], w_down, j, wd_in[j])
            for j in range(2):
                load(wg[1][j], w_gate, 2 + j, wg_in[1][j])

            def after(i, par):
                sp.wait_ge(gate_done, i + 1)
                for j in range(2):
                    load(wg[par][j], w_gate, i * 2 + (4 + j), wg_in[par][j])
                sp.wait_ge(up_done, i + 1)
                for j in range(2):
                    load(wu[j], w_up, i * 2 + (2 + j), wu_in[j])
                sp.wait_ge(down_done, i + 1)
                for j in range(2):
                    load(wd[j], w_down, i * 2 + (2 + j), wd_in[j])

            with sp.Fori(0, PAIRS // 2 - 1) as n:
                after(n * 2, 0)
                after(n * 2 + 1, 1)
            i = PAIRS - 2
            sp.wait_ge(up_done, i + 1)
            for j in range(2):
                load(wu[j], w_up, 2 * i + 2 + j, wu_in[j])
            sp.wait_ge(down_done, i + 1)
            for j in range(2):
                load(wd[j], w_down, 2 * i + 2 + j, wd_in[j])
            sp.wait_ge(extra_ready, 1)
            n_extra = sp.value_load(extra_i[0:1, EXTRA:EXTRA + 1], min_val=0, max_val=EXTRA)
            with sp.Fori(0, EXTRA // 2) as m:
                with sp.If(n_extra > m * 2):
                    sp.wait_ge(acc_done, 4 * PAIRS + 2 + m * 4)
                    for j in range(2):
                        e = sp.value_load(extra_i[0:1, bass.ds(m * 2 + j, 1)], min_val=0, max_val=EXPERTS - 1)
                        load(wg[0][j], w_gate, e, wg_in[0][j])
                        load(wu[j], w_up, e, wu_in[j])
                        load(wd[j], w_down, e, wd_in[j])
            sp.wait_ge(all_added, 1)
            sp.dma_start(gate_b, mod_row(0, 5)).then_inc(gate_in, 16)

        def gather(pe, i, par):
            pe.wait_ge(sel_ready, i + 1)
            for half, bank in enumerate((X0, X1)):
                for t in range(TT):
                    mm = pe.matmul(bank[:, :], sel[par][:, t].rearrange("p a b -> p (a b)"),
                                   hx[:, t, half * 512:(half + 1) * 512], start=(t == 0), stop=(t == TT - 1))
            mm.then_inc(gath_done, 1)

        def turn_gathered(pe, i):
            pe.wait_ge(xg_ready, i + 1)
            for t in range(KT):
                mm = pe.transpose((X0, X1)[t // 4][:, t % 4 * P:(t % 4 + 1) * P], xg[:, t::KT], s.c("ident"))
            mm.then_inc(xgT_done, 1)

        def gate_product(pe, i, par, uses):
            pe.wait_ge(xT_ready, i + 1)
            for j in range(2):
                pe.wait_ge(wg_in[par][j], uses * 16)
            for t in range(KT):
                for j in range(2):
                    mm = pe.matmul(G[j * CAP:(j + 1) * CAP, :], xT[:, t, j * CAP:(j + 1) * CAP], wg[par][j][:, t],
                                   start=(t == 0), stop=(t == KT - 1))
            mm.then_inc(gate_done, 1)

        def up_product(pe, i):
            for j in range(2):
                pe.wait_ge(wu_in[j], (i + 1) * 16)
            for t in range(KT):
                for j in range(2):
                    mm = pe.matmul(U[j * CAP:(j + 1) * CAP, :], xT[:, t, j * CAP:(j + 1) * CAP], wu[j][:, t],
                                   start=(t == 0), stop=(t == KT - 1))
            mm.then_inc(up_done, 1)

        def turn_hidden(pe, i, par):
            pe.wait_ge(h_ready, i + 1)
            for t in range(HK):
                pe.transpose(G[:, t * P:(t + 1) * P], h[:, t::HK], s.c("ident"))
            for t in range(TT):
                mm = pe.transpose(U[:, t * P:(t + 1) * P], selw[par][:, t].rearrange("p a b -> p (a b)"), s.c("ident"))
            mm.then_inc(hT_done, 1)

        def down_product(pe, i):
            pe.wait_ge(hT_ready, i + 1)
            for j in range(2):
                pe.wait_ge(wd_in[j], (i + 1) * 16)
            for half, bank in enumerate((Y0, Y1)):
                for t in range(HK):
                    for j in range(2):
                        mm = pe.matmul(bank[j * CAP:(j + 1) * CAP, :], hT[:, t, j * CAP:(j + 1) * CAP],
                                       wd[j][:, t, half * 512:(half + 1) * 512], start=(t == 0), stop=(t == HK - 1))
            mm.then_inc(down_done, 1)

        def scatter(pe, i):
            pe.wait_ge(y_ready, i + 1)
            for k in range(4):
                pe.wait_ge(acc_done, i * 4 + (k + 1))
                pe.matmul((S0, S1)[k % 2][:, :], selwT[:, k // 2], y[:, k % 2 * 512:(k % 2 + 1) * 512],
                          start=True, stop=True).then_inc(scat_done, 1)

        @block.tensor
        def _(pe):
            for t in range(TT):
                pe.wait_ge(hx_ready, t + 1)
                if t:
                    pe.wait_ge(hxT_ready, t)
                for k in range(KT):
                    mm = pe.transpose((X0, X1)[k // 4][:, k % 4 * P:(k % 4 + 1) * P], hx[:, t, k::KT], s.c("ident"))
                mm.then_inc(hxT_done, 1)
                pe.wait_ge(hxT_ready, t + 1)
                pe.wait_ge(router_in, 32)
                for k in range(KT):
                    mm = pe.matmul(S0[:, t * 64:t * 64 + GROUPS + EXPERTS], xT[:, k], router[:, k],
                                   start=(k == 0), stop=(k == KT - 1))
                mm.then_inc(logits_done, 1)
            pe.wait_ge(member_ready, 1)
            pe.matmul(S1[:, 0:EXPERTS], s.c("before"), member[:, 0], start=True, stop=True)
            for t in range(TT):
                mm = pe.matmul(S1[:, EXPERTS:2 * EXPERTS], s.c("ones" if t == 0 else "before"), member[:, t],
                               start=(t == 0), stop=(t == TT - 1))
            for t in range(TT):
                mm = pe.matmul(S1[:, 2 * EXPERTS:3 * EXPERTS], s.c("ones"), member[:, t],
                               start=(t == 0), stop=(t == TT - 1))
            mm.then_inc(rank_done, 1)

            gather(pe, 0, 0)
            turn_gathered(pe, 0)

            def pair(i, par, uses, first=False, last=False):
                gate_product(pe, i, par, uses)
                if not last:
                    gather(pe, i + 1, 1 - par)
                up_product(pe, i)
                if not last:
                    turn_gathered(pe, i + 1)
                if not first:
                    scatter(pe, i - 1)
                turn_hidden(pe, i, par)
                down_product(pe, i)

            pair(0, 0, 1, first=True)
            with pe.Fori(0, PAIRS // 2 - 1) as n:
                pair(n * 2 + 1, 1, n + 1)
                pair(n * 2 + 2, 0, n + 2)
            pair(PAIRS - 1, 1, PAIRS // 2, last=True)
            scatter(pe, PAIRS - 1)

            pe.wait_ge(extra_ready, 1)
            n_extra = pe.value_load(extra_i[0:1, EXTRA:EXTRA + 1], min_val=0, max_val=EXTRA)
            with pe.Fori(0, EXTRA // 2) as m:
                with pe.If(n_extra > m * 2):
                    i = m + PAIRS
                    gather(pe, i, 0)
                    turn_gathered(pe, i)
                    gate_product(pe, i, 0, m + (PAIRS // 2 + 1))
                    up_product(pe, i)
                    turn_hidden(pe, i, 0)
                    down_product(pe, i)
                    scatter(pe, i)

        def silu_gate(act, i):
            act.wait_ge(gate_done, i + 1)
            act.activation(sg, G[:, :], ACT.Silu).then_inc(silu_ready, 1)

        def copy_gathered(act, i):
            act.wait_ge(gath_done, i + 1)
            act.activation(xg[:, 0:512], X0[:, :], ACT.Copy)
            act.activation(xg[:, 512:D], X1[:, :], ACT.Copy).then_inc(xg_ready, 1)

        def copy_hidden(act, i):
            act.wait_ge(hT_done, i + 1)
            act.activation(flat(selwT), U[:, 0:TT * P], ACT.Copy)
            act.activation(flat(hT), G[:, :], ACT.Copy).then_inc(hT_ready, 1)

        def copy_rows(act, i):
            act.wait_ge(down_done, i + 1)
            act.activation(y[:, 0:512], Y0[:, :], ACT.Copy)
            act.activation(y[:, 512:D], Y1[:, :], ACT.Copy).then_inc(y_ready, 1)

        @block.scalar
        def _(act):
            for t in range(TT):
                act.activation(acc[:, 1, :], s.x_res[:, t], ACT.Square, accum_out=small[:, t, 0:1])
                act.drain()
            act.sem_inc(squares_done, 1)
            act.wait_ge(root_done, 1)
            act.activation(small[:, :, 2:3], small[:, :, 1:2], ACT.Sqrt).then_inc(root_done, 1)
            act.wait_ge(shifted, 1)
            for t in range(TT):
                act.activation(glog[:, t, 4:8], glog[:, t, 0:4], ACT.Exp, bias=small[:, t, 3:4],
                               accum_out=small[:, t, 4:5])
            act.activation(small[:, :, 6:7], small[:, :, 5:6], ACT.Exp)
            act.drain()
            act.sem_inc(exps_done, 1)

            copy_gathered(act, 0)

            def pair(i, last=False):
                silu_gate(act, i)
                if not last:
                    copy_gathered(act, i + 1)
                copy_hidden(act, i)
                copy_rows(act, i)

            with act.Fori(0, PAIRS - 1) as i:
                pair(i)
            pair(PAIRS - 1, last=True)
            act.wait_ge(extra_ready, 1)
            n_extra = act.value_load(extra_i[0:1, EXTRA:EXTRA + 1], min_val=0, max_val=EXTRA)
            with act.Fori(0, EXTRA // 2) as m:
                with act.If(n_extra > m * 2):
                    i = m + PAIRS
                    copy_gathered(act, i)
                    silu_gate(act, i)
                    copy_hidden(act, i)
                    copy_rows(act, i)

        def select_slots(dve, i, par):
            two = slice(2 * i, 2 * i + 2) if isinstance(i, int) else bass.ds(i * 2, 2)
            at = slot_of[:, :, two].unsqueeze(3).to_broadcast([P, TT, 2, CAP])
            wt = weight_of[:, :, two].unsqueeze(3).to_broadcast([P, TT, 2, CAP])
            io = iota[:, 0:CAP].unsqueeze(1).unsqueeze(1).to_broadcast([P, TT, 2, CAP])
            dve.tensor_tensor(sel[par], io, at, ALU.is_equal)
            dve.drain()
            dve.tensor_tensor(selw[par], sel[par], wt, ALU.mult).then_inc(sel_ready, 1)

        def hidden_rows(dve, i):
            dve.wait_ge(silu_ready, i + 1)
            dve.wait_ge(up_done, i + 1)
            dve.tensor_tensor(h, U[:, :], sg, ALU.mult).then_inc(h_ready, 1)

        def copy_turned(dve, i):
            dve.wait_ge(xgT_done, i + 1)
            dve.tensor_copy(xT[:, 0:4].rearrange("p a b -> p (a b)"), X0[:, :])
            dve.tensor_copy(xT[:, 4:8].rearrange("p a b -> p (a b)"), X1[:, :]).then_inc(xT_ready, 1)

        def add_up(dve, i):
            for k in range(4):
                dve.wait_ge(scat_done, i * 4 + (k + 1))
                part = acc[:, k // 2, k % 2 * 512:(k % 2 + 1) * 512]
                dve.tensor_tensor(part, (S0, S1)[k % 2][:, :], part, ALU.add).then_inc(acc_done, 1)

        @block.vector
        def _(dve):
            dve.wait_ge(rows_in, 48)
            dve.tensor_scalar(scale_b, scale_b, 1.0, None, ALU.add)
            dve.drain()
            dve.tensor_tensor(scale_b, scale_b, acc[:, 0, :], ALU.mult)
            dve.wait_ge(squares_done, 1)
            dve.tensor_scalar(small[:, :, 1:2], small[:, :, 0:1], 1.0 / D, NORM_EPS, ALU.mult, ALU.add).then_inc(root_done, 1)
            dve.wait_ge(root_done, 2)
            dve.reciprocal(small[:, :, 2:3], small[:, :, 2:3])
            dve.drain()
            for t in range(TT):
                dve.scalar_tensor_tensor(hx[:, t], s.x_res[:, t], small[:, t, 2:3], scale_b, ALU.mult, ALU.mult)
                dve.drain()
                dve.tensor_tensor(hx[:, t], hx[:, t], shift_b, ALU.add).then_inc(hx_ready, 1)
            for t in range(TT):
                dve.wait_ge(hxT_done, t + 1)
                if t:
                    dve.wait_ge(logits_done, t)
                dve.tensor_copy(xT[:, 0:4].rearrange("p a b -> p (a b)"), X0[:, :])
                dve.tensor_copy(xT[:, 4:8].rearrange("p a b -> p (a b)"), X1[:, :]).then_inc(hxT_ready, 1)
            dve.memset(acc, 0.0)
            dve.wait_ge(logits_done, TT)
            NL = GROUPS + EXPERTS
            for t in range(TT):
                dve.tensor_tensor(logit[:, t], S0[:, t * 64:t * 64 + NL], router_b, ALU.add)
            dve.memset(glog, -3.0e38)
            dve.drain()
            dve.tensor_copy(glog[:, :, 0:4], logit[:, :, 0:4])
            dve.drain()
            for t in range(TT):
                dve.max(top[:, t], glog[:, t])
            dve.drain()
            for t in range(TT):
                dve.max_index(topi[:, t], top[:, t], glog[:, t])
            dve.drain()
            dve.tensor_scalar(small[:, :, 3:4], top[:, :, 0:1], -1.0, None, ALU.mult)
            dve.tensor_copy(small[:, :, 8:9], topi[:, :, 0:1])
            dve.drain()
            of_group = iota[:, 0:GROUPS].unsqueeze(1).to_broadcast([P, TT, GROUPS])
            dve.tensor_tensor(tmp[:, :, 0:GROUPS], of_group, small[:, :, 8:9].to_broadcast([P, TT, GROUPS]), ALU.is_equal)
            dve.drain()
            for t in range(TT):
                dve.tensor_tensor(tmp2[:, t].rearrange("p (e g) -> p g e", g=GROUPS),
                                  logit[:, t, GROUPS:].rearrange("p (g e) -> p g e", g=GROUPS),
                                  tmp[:, t, 0:GROUPS].unsqueeze(2).to_broadcast([P, GROUPS, PER_GROUP]), ALU.mult)
            dve.drain()
            for t in range(TT):
                dve.tensor_reduce(member[:, t, 0:PER_GROUP], tmp2[:, t].rearrange("p (e g) -> p e g", g=GROUPS), AX.X, ALU.add)
            dve.drain()
            for t in range(TT):
                dve.max(top[:, t], member[:, t, 0:PER_GROUP])
            dve.drain()
            for t in range(TT):
                dve.max_index(topi[:, t], top[:, t], member[:, t, 0:PER_GROUP])
            dve.tensor_tensor(small[:, :, 5:6], top[:, :, 1:2], top[:, :, 0:1], ALU.subtract)
            dve.drain()
            dve.sem_inc(shifted, 1)
            dve.tensor_copy(small[:, :, 9:11], topi[:, :, 0:2])
            dve.drain()
            dve.tensor_scalar(small[:, :, 8:9], small[:, :, 8:9], float(PER_GROUP), None, ALU.mult)
            dve.drain()
            dve.tensor_tensor(small[:, :, 9:11], small[:, :, 9:11], small[:, :, 8:9].to_broadcast([P, TT, 2]), ALU.add)
            dve.drain()
            dve.wait_ge(exps_done, 1)
            dve.tensor_scalar(small[:, :, 11:12], small[:, :, 6:7], 1.0, None, ALU.add)
            dve.drain()
            dve.tensor_tensor(small[:, :, 11:12], small[:, :, 11:12], small[:, :, 4:5], ALU.mult)
            dve.drain()
            dve.reciprocal(small[:, :, 12:13], small[:, :, 11:12])
            dve.drain()
            dve.tensor_tensor(small[:, :, 13:14], small[:, :, 12:13], small[:, :, 6:7], ALU.mult)
            dve.drain()
            of_expert = iota[:, 0:EXPERTS].unsqueeze(1).to_broadcast([P, TT, EXPERTS])
            dve.tensor_tensor(tmp, of_expert, small[:, :, 9:10].to_broadcast([P, TT, EXPERTS]), ALU.is_equal)
            dve.tensor_tensor(tmp2, of_expert, small[:, :, 10:11].to_broadcast([P, TT, EXPERTS]), ALU.is_equal)
            dve.drain()
            dve.tensor_tensor(member, tmp, tmp2, ALU.add).then_inc(member_ready, 1)
            dve.tensor_tensor(tmp, tmp, small[:, :, 12:13].to_broadcast([P, TT, EXPERTS]), ALU.mult)
            dve.tensor_tensor(tmp2, tmp2, small[:, :, 13:14].to_broadcast([P, TT, EXPERTS]), ALU.mult)
            dve.drain()
            dve.tensor_tensor(weight_of[:, :, 0:EXPERTS], tmp, tmp2, ALU.add)
            dve.wait_ge(rank_done, 1)
            dve.drain()
            dve.scalar_tensor_tensor(slot_of[:, :, 0:EXPERTS], S1[:, 0:2 * EXPERTS].rearrange("p (t e) -> p t e", t=TT),
                                     1.0, member, ALU.add, ALU.mult)
            dve.tensor_copy(cnt, S1[:, 2 * EXPERTS:3 * EXPERTS])
            dve.drain()
            dve.tensor_scalar(slot_of[:, :, 0:EXPERTS], slot_of[:, :, 0:EXPERTS], -1.0, None, ALU.add)
            dve.drain()
            select_slots(dve, 0, 0)
            for b in range(3):
                dve.tensor_scalar(flag[:, b], cnt, float(CAP * (b + 1)), None, ALU.is_gt)
                dve.tensor_scalar(base[:, :, b], slot_of[:, :, 0:EXPERTS], float(1 - CAP * (b + 1)), None, ALU.add)
                dve.tensor_copy(wbase[:, :, b], weight_of[:, :, 0:EXPERTS])
                dve.tensor_copy(num[:, b], iota[:, 0:EXPERTS])
            dve.drain()
            flags = flat(flag)
            dve.tensor_tensor_scan(order, s.c("ones", 3 * EXPERTS), flags, 0.0, ALU.mult, ALU.add)
            dve.drain()
            for k in range(EXTRA):
                dve.scalar_tensor_tensor(pick, order, float(k + 1), flags, ALU.is_equal, ALU.mult)
                dve.drain()
                for src, out in [(flat(num), extra_f[:, k:k + 1])] + [
                        (v[:, t].rearrange("p a b -> p (a b)"), o[:, t, EXPERTS + k:EXPERTS + k + 1])
                        for v, o in ((base, slot_of), (wbase, weight_of)) for t in range(TT)]:
                    dve.tensor_tensor(prod, pick, src, ALU.mult)
                    dve.drain()
                    dve.tensor_reduce(out, prod, AX.X, ALU.add)
                    dve.drain()
            dve.tensor_scalar(slot_of[:, :, EXPERTS:NE], slot_of[:, :, EXPERTS:NE], -1.0, None, ALU.add)
            dve.tensor_copy(extra_f[:, EXTRA:EXTRA + 1], order[:, 3 * EXPERTS - 1:3 * EXPERTS])
            dve.drain()
            dve.tensor_copy(extra_i, extra_f).then_inc(extra_ready, 1)
            dve.sem_inc(acc_done, 2)

            copy_turned(dve, 0)

            def pair(i, par, first=False, last=False):
                if not first:
                    dve.wait_ge(hT_done, i)
                if not last:
                    select_slots(dve, i + 1, 1 - par)
                hidden_rows(dve, i)
                if not last:
                    copy_turned(dve, i + 1)
                if not first:
                    add_up(dve, i - 1)

            pair(0, 0, first=True)
            with dve.Fori(0, PAIRS // 2 - 1) as n:
                pair(n * 2 + 1, 1)
                pair(n * 2 + 2, 0)
            pair(PAIRS - 1, 1, last=True)
            add_up(dve, PAIRS - 1)
            n_extra = dve.value_load(extra_i[0:1, EXTRA:EXTRA + 1], min_val=0, max_val=EXTRA)
            with dve.Fori(0, EXTRA // 2) as m:
                with dve.If(n_extra > m * 2):
                    i = m + PAIRS
                    dve.wait_ge(hT_done, i)
                    select_slots(dve, i, 0)
                    copy_turned(dve, i)
                    hidden_rows(dve, i)
                    add_up(dve, i)
            dve.drain()
            dve.sem_inc(all_added, 1)
            dve.wait_ge(gate_in, 16)
            for t in range(TT):
                dve.tensor_tensor(acc[:, t], acc[:, t], gate_b, ALU.mult)
            dve.drain()
            dve.tensor_tensor(s.x_res, s.x_res, acc, ALU.add)


EMB, BANDS, FH = 33, 16, 64
FREQ = L
TWO_PI = 2.0 * math.pi
TWO_PI_HI = 6.28125
TWO_PI_LO = TWO_PI - TWO_PI_HI
ROUND = 1.5 * 2.0 ** 23


def hyena_constants():
    t32 = np.linspace(0.0, 1.0, L, dtype=np.float32)
    w = (np.float32(2.0 * math.pi) * np.arange(L, dtype=np.float32) / np.float32(L))[:, None]
    f = np.linspace(1e-4, BANDS - 1, BANDS, dtype=np.float32)[None]
    z = np.zeros((P, L), np.float32)
    z[:EMB] = np.concatenate([t32[:, None], np.cos(f * w), -np.sin(f * w)], -1).T
    ang = np.arange(L)[:, None] * (np.arange(FREQ)[None] + 0.5) * (math.pi / FREQ)
    tiles = lambda m: m.reshape(2, P, -1).transpose(1, 0, 2).reshape(P, -1)
    cos, sin = np.cos(ang), np.sin(ang)
    minus_t = -t32.reshape(TT, P).T
    keep = (np.arange(L) > 0).astype(np.float32).reshape(TT, P).T
    mats = [tiles(cos), tiles(sin), tiles(cos.T), tiles(sin.T)]
    deltas = np.abs(np.linspace(math.log(1e-2) / 1.5, math.log(1e-2) / 0.3, D, dtype=np.float32))
    return np.concatenate([z, minus_t, keep] + mats, 1).astype(np.float32), deltas


HY_CONST, HY_DELTAS = hyena_constants()


def hyena_layer(s, ins, mods):
    nc = s.nc
    s.at = 0
    BLK = 3 * CH
    SLOTS = 3
    win_ring = [s.take(KT, 512) for _ in range(SLOTS)]
    hc = s.take(HY_CONST.shape[1])
    zT = hc[:, 0:L]
    minus_t, keep = hc[:, L:L + TT], hc[:, L + TT:L + 2 * TT]
    o = L + 2 * TT
    fwd = [hc[:, o + n * 512:o + (n + 1) * 512].rearrange("p (i f) -> p i f", i=2) for n in range(2)]
    inv = [hc[:, o + (2 + n) * 512:o + (3 + n) * 512].rearrange("p (i f) -> p i f", i=2) for n in range(2)]
    khat = s.take(2, 2, 2, D)
    big = s.take(2, 2, 2, D)
    hsum, hdif = big[:, 0], big[:, 1]
    vhat, prod = big[:, 0], big[:, 1]
    area = s.at
    f_w3 = s.take(2 * 2 * D)
    window = s.take(TT, D)
    s.at = area
    hT = s.take(KT, L)
    vt = s.take(TT, D)
    tmp = s.take(2, D)
    u = s.take(BLK, L)
    up = [s.take(L + 2) for _ in range(2)]
    w1, wi = s.take(FH), s.take(2, FH)
    fv = s.take(4)
    hd = s.take(L)
    arg, turns = s.take(L), s.take(L)
    chv = s.take(P)
    skip = s.take(16)
    norm = s.take(16)
    sc, sh, ng = s.take(KT), s.take(KT), s.take(KT)
    stat = s.take(2)
    pos = s.take(L)
    rows, rows2 = up[0][:, 0:P], up[1][:, 0:P]
    gate, b_out = tmp[:, 0], tmp[:, 1]
    w_out = s.arena[:, 0:CH * D].rearrange("p (m n) -> p m n", m=CH)
    w_scratch = s.arena[:, CH * D:(CH + 2) * D].rearrange("p (i n) -> p i n", i=2)
    S = lambda n: s.sem("hy_" + n)
    hc_in, w_in, f3_in, win_in = S("hc_in"), S("w_in"), S("f3_in"), S("window_in")
    ring_in = [S(f"ring_in{k}") for k in range(SLOTS)]
    arg_done, hd_ready, f_done, win_ready = S("arg"), S("hd"), S("f"), S("win")
    taps_done, taps_ready, spec_done, spec_ready, abs_ready, abs_done = (S(n) for n in
        ("taps_done", "taps_ready", "spec_done", "spec_ready", "abs_ready", "abs_done"))
    mag_ready = S("mag_ready")

    with nc.Block(name="hyena_filters", no_gpsimd_drain=True) as block:

        @block.sync
        def _(sp):
            sp.dma_start(hc, ins["hy_const"]).then_inc(hc_in, 16)
            sp.dma_start(w1[0:EMB, :], ins["hy_f_w1"][0]).then_inc(w_in, 16)
            sp.dma_start(wi[0:FH], ins["hy_f_wi"][0].rearrange("n i o -> i n o")).then_inc(w_in, 16)
            for n, v in enumerate((ins["hy_f_freq"][0], ins["hy_f_b1"][0], ins["hy_f_bi"][0, 0], ins["hy_f_bi"][0, 1])):
                sp.dma_start(fv[0:FH, n:n + 1], v.unsqueeze(1)).then_inc(w_in, 16)
            sp.dma_start(window[:, 0], ins["hy_deltas"].partition_broadcast(P)).then_inc(win_in, 16)
            sp.dma_start(window[:, 1], ins["hy_deltas"].partition_broadcast(P)).then_inc(win_in, 16)
            sp.dma_start(f_w3[0:FH, :], ins["hy_f_w3"][0]).then_inc(f3_in, 16)
            src = ins["hy_w_in"][0].rearrange("(p t) n -> p t n", t=KT)
            for k in range(SLOTS):
                sp.dma_start(win_ring[k], src[:, :, k * 512:(k + 1) * 512]).then_inc(ring_in[k], 16)

        @block.tensor
        def _(pe):
            pe.wait_ge(hc_in, 16)
            pe.wait_ge(w_in, 96)
            pe.matmul(s.psum[0][0:FH, 0:L], w1[0:EMB, :], zT[0:EMB, :], start=True, stop=True).then_inc(f_done, 1)
            for n in range(2):
                pe.wait_ge(hd_ready, n + 1)
                pe.matmul(s.psum[0][0:FH, 0:L], wi[0:FH, n], hd[0:FH, :], start=True, stop=True).then_inc(f_done, 1)
            pe.wait_ge(hd_ready, 3)
            pe.wait_ge(f3_in, 16)
            for n in range(8):
                od, i, half = n // 4, n // 2 % 2, n % 2
                if n >= 4:
                    pe.wait_ge(taps_ready, n - 3)
                for sign in range(2):
                    c = (od * 2 + sign) * D + half * 512
                    mm = pe.matmul(s.psum[n % 4 * 2 + sign][:, :], hd[0:FH, i * P:(i + 1) * P], f_w3[0:FH, c:c + 512],
                                   start=True, stop=True)
                mm.then_inc(taps_done, 1)
            for n in range(16):
                od, part, ft, half = n // 8, n // 4 % 2, n // 2 % 2, n % 2
                pe.wait_ge(taps_ready, 8)
                if n >= 8:
                    pe.wait_ge(spec_ready, n - 7)
                src = (hsum, hdif)[part]
                for i in range(TT):
                    mm = pe.matmul(s.psum[n % 8][:, :], fwd[part][:, i, ft * P:(ft + 1) * P],
                                   src[:, od, i, half * 512:(half + 1) * 512], start=(i == 0), stop=(i == TT - 1))
                mm.then_inc(spec_done, 1)
            pe.wait_ge(abs_ready, 1)
            for od in range(2):
                for m in range(CH):
                    for i in range(TT):
                        mm = pe.matmul(s.psum[0][:, od * CH + m:od * CH + m + 1], hsum[:, od, i, m * P:(m + 1) * P],
                                       s.c("ones")[:, 0:1], start=(i == 0), stop=(i == TT - 1))
            mm.then_inc(abs_done, 1)

        @block.scalar
        def _(act):
            act.wait_ge(win_in, 32)
            act.wait_ge(hc_in, 16)
            for i in range(TT):
                act.activation(window[:, i], window[:, i], ACT.Exp, scale=minus_t[:, i:i + 1]).then_inc(win_ready, 1)
            for n in range(3):
                act.wait_ge(arg_done, n + 1)
                act.activation(hd[0:FH, :], arg[0:FH, :], ACT.Sin).then_inc(hd_ready, 1)
            for n in range(16):
                act.wait_ge(spec_done, n + 1)
                od, part, ft, half = n // 8, n // 4 % 2, n // 2 % 2, n % 2
                act.activation(khat[:, od, part, ft, half * 512:(half + 1) * 512], s.psum[n % 8][:, :], ACT.Copy).then_inc(spec_ready, 1)
            act.activation(hsum, hsum, ACT.Abs)
            act.activation(hdif, hdif, ACT.Abs).then_inc(mag_ready, 1)

        @block.vector
        def _(dve):
            for n in range(3):
                dve.wait_ge(f_done, n + 1)
                x, k = arg[0:FH, :], turns[0:FH, :]
                dve.tensor_scalar(x, s.psum[0][0:FH, 0:L], fv[0:FH, n + 1:n + 2], fv[0:FH, 0:1], ALU.add, ALU.mult)
                dve.drain()
                dve.tensor_scalar(k, x, 1.0 / TWO_PI, ROUND, ALU.mult, ALU.add)
                dve.drain()
                dve.tensor_scalar(k, k, -ROUND, None, ALU.add)
                dve.drain()
                dve.scalar_tensor_tensor(x, k, -TWO_PI_HI, x, ALU.mult, ALU.add)
                dve.drain()
                dve.scalar_tensor_tensor(x, k, -TWO_PI_LO, x, ALU.mult, ALU.add)
                dve.drain()
                dve.tensor_scalar(x, x, math.pi, -math.pi, ALU.min, ALU.max).then_inc(arg_done, 1)
            dve.wait_ge(win_ready, TT)
            for n in range(8):
                od, i, half = n // 4, n // 2 % 2, n % 2
                c = slice(half * 512, (half + 1) * 512)
                dve.wait_ge(taps_done, n + 1)
                a, b = s.psum[n % 4 * 2], s.psum[n % 4 * 2 + 1]
                dve.tensor_tensor(u[:, 0:2].rearrange("p a b -> p (a b)"), a[:, :], window[:, i, c], ALU.mult)
                dve.scalar_tensor_tensor(u[:, 2:4].rearrange("p a b -> p (a b)"), b[:, :], keep[:, i:i + 1], window[:, i, c],
                                         ALU.mult, ALU.mult)
                dve.drain()
                h0, h1 = (u[:, k:k + 2].rearrange("p a b -> p (a b)") for k in (0, 2))
                dve.tensor_tensor(hsum[:, od, i, c], h0, h1, ALU.add)
                dve.tensor_tensor(hdif[:, od, i, c], h0, h1, ALU.subtract)
                dve.drain()
                dve.sem_inc(taps_ready, 1)
            dve.wait_ge(mag_ready, 1)
            for od in range(2):
                dve.tensor_tensor(hsum[:, od], hsum[:, od], hdif[:, od], ALU.max)
            dve.drain()
            dve.sem_inc(abs_ready, 1)
            dve.wait_ge(abs_done, 1)
            dve.wait_ge(spec_ready, 16)
            dve.reciprocal(norm, s.psum[0][:, 0:16])
            dve.drain()
            dve.tensor_scalar(norm, norm, 1.0 / FREQ, None, ALU.mult)

    vec_in, rows_in, chv_done = S("vec_in"), S("rows_in"), S("chv_done")
    sq_done, var_done, root_done, xn_ready, xnT_done, hT_ready, scale_ready = (S(n) for n in
        ("sq", "var", "root", "xn", "xnT", "hT", "scale"))
    in_done, up_ready, u_ready = S("in_done"), S("up_ready"), S("u_ready")
    wout_in, row_in = [S(f"wout_in{h}") for h in range(2)], S("row_in")

    with nc.Block(name="hyena_inputs", no_gpsimd_drain=True) as block:

        @block.sync
        def _(sp):
            sp.dma_start(sc, mods[1, 0, D:2 * D].rearrange("(p t) -> p t", t=KT)).then_inc(vec_in, 16)
            sp.dma_start(sh, mods[1, 0, 0:D].rearrange("(p t) -> p t", t=KT)).then_inc(vec_in, 16)
            sp.dma_start(ng, ins["norm_g"][1, 0].rearrange("(p t) -> p t", t=KT)).then_inc(vec_in, 16)
            vecs = [ins["hy_b_in"][0], ins["hy_conv_b"][0]] + [ins["hy_conv_w"][0, k] for k in range(3)]
            for n, v in enumerate(vecs):
                sp.dma_start(rows[n * BLK:(n + 1) * BLK, :], v.rearrange("(m p) -> m p", p=P)).then_inc(rows_in, 16)
            sp.dma_start(rows2[0:16, :], ins["hy_skip"][0].rearrange("o (m p) -> (o m) p", p=P)).then_inc(rows_in, 16)
            src = ins["hy_w_in"][0].rearrange("(p t) n -> p t n", t=KT)
            for k in range(SLOTS):
                sp.wait_ge(in_done, 4 * k + 4)
                b = SLOTS + k
                sp.dma_start(win_ring[k], src[:, :, b * 512:(b + 1) * 512]).then_inc(ring_in[k], 16)

        @block.tensor
        def _(pe):
            pe.wait_ge(rows_in, 96)
            pe.transpose(s.psum[7][:, 0:5 * BLK], rows[0:5 * BLK, :], s.c("ident")[0:5 * BLK, 0:5 * BLK])
            pe.transpose(s.psum[7][:, 128:144], rows2[0:16, :], s.c("ident")[0:16, 0:16]).then_inc(chv_done, 1)
            pe.wait_ge(xn_ready, TT)
            for t in range(KT):
                if t == 7:
                    pe.wait_ge(chv_done, 2)
                for i in range(TT):
                    mm = pe.transpose(s.psum[t][:, i * P:(i + 1) * P], vt[:, i, t::KT], s.c("ident"))
                mm.then_inc(xnT_done, 1)
            pe.wait_ge(hT_ready, KT)
            with pe.Fori(0, 2) as l:
                for k in range(SLOTS):
                    pe.wait_ge(ring_in[k], l * 16 + 16)
                    for q in range(4):
                        n = l * (4 * SLOTS) + (4 * k + q)
                        pe.wait_ge(up_ready, n + 1)
                        for t in range(KT):
                            mm = pe.matmul(s.psum[q % 2][:, 0:L], win_ring[k][:, t, q * P:(q + 1) * P], hT[:, t],
                                           start=(t == 0), stop=(t == KT - 1))
                        mm.then_inc(in_done, 1)

        @block.scalar
        def _(act):
            for i in range(TT):
                act.activation(tmp[:, 0], s.x_res[:, i], ACT.Square, accum_out=stat[:, i:i + 1])
                act.drain()
            act.sem_inc(sq_done, 1)
            act.wait_ge(var_done, 1)
            act.activation(stat, stat, ACT.Sqrt).then_inc(root_done, 1)
            act.wait_ge(scale_ready, 1)
            for t in range(KT):
                act.wait_ge(xnT_done, t + 1)
                act.activation(hT[:, t], s.psum[t][:, 0:L], ACT.Identity, bias=sh[:, t:t + 1], scale=sc[:, t:t + 1]).then_inc(hT_ready, 1)
            act.sem_inc(up_ready, 2)
            with act.Fori(0, BLK // 2) as g:
                for q in range(2):
                    n = g * 2 + q
                    act.wait_ge(in_done, n + 1)
                    act.wait_ge(u_ready, n + 1)
                    act.activation(up[q][:, 1:L + 1], s.psum[q][:, 0:L], ACT.Identity,
                                   bias=chv[:, bass.ds(n, 1)]).then_inc(up_ready, 1)

        @block.vector
        def _(dve):
            dve.wait_ge(chv_done, 1)
            dve.tensor_copy(chv[:, 0:5 * BLK], s.psum[7][:, 0:5 * BLK])
            dve.tensor_copy(skip, s.psum[7][:, 128:144])
            for k in range(2):
                dve.memset(up[k][:, 0:1], 0.0)
                dve.memset(up[k][:, L + 1:L + 2], 0.0)
            dve.drain()
            dve.sem_inc(chv_done, 1)
            dve.sem_inc(u_ready, 2)
            dve.wait_ge(vec_in, 48)
            dve.tensor_scalar(sc, sc, 1.0, None, ALU.add)
            dve.drain()
            dve.tensor_tensor(sc, sc, ng, ALU.mult).then_inc(scale_ready, 1)
            dve.wait_ge(sq_done, 1)
            dve.tensor_scalar(stat, stat, 1.0 / D, NORM_EPS, ALU.mult, ALU.add).then_inc(var_done, 1)
            dve.wait_ge(root_done, 1)
            dve.reciprocal(stat, stat)
            dve.drain()
            for i in range(TT):
                dve.tensor_scalar(vt[:, i], s.x_res[:, i], stat[:, i:i + 1], None, ALU.mult).then_inc(xn_ready, 1)
            with dve.Fori(0, BLK // 2) as g:
                for q in range(2):
                    n = g * 2 + q
                    dve.wait_ge(up_ready, n + 3)
                    at = lambda k: chv[:, bass.ds(n + k * BLK, 1)]
                    dst = u[:, bass.ds(n, 1)].rearrange("p o c -> p (o c)")
                    dve.tensor_scalar(pos, up[q][:, 0:L], at(2), at(1), ALU.mult, ALU.add)
                    dve.drain()
                    dve.scalar_tensor_tensor(pos, up[q][:, 1:L + 1], at(3), pos, ALU.mult, ALU.add)
                    dve.drain()
                    dve.scalar_tensor_tensor(dst, up[q][:, 2:L + 2], at(4), pos, ALU.mult, ALU.add)
                    dve.drain()
                    dve.sem_inc(u_ready, 1)

    vT_done, vt_ready, dft_done, vhat_ready, prod_ready, y_done, y_ready = (S(n) for n in
        ("vT_done", "vt_ready", "dft_done", "vhat_ready", "prod_ready", "y_done", "y_ready"))
    o_done = S("o_done")
    with nc.Block(name="hyena_convolutions", no_gpsimd_drain=True) as block:

        @block.sync
        def _(sp):
            src = ins["hy_w_out"][0].rearrange("(m p) n -> p m n", p=P)
            for h in range(2):
                sp.dma_start(w_out[:, 4 * h:4 * h + 4], src[:, 4 * h:4 * h + 4]).then_inc(wout_in[h], 16)
            sp.dma_start(gate, mods[1, 0, 2 * D:3 * D].partition_broadcast(P)).then_inc(row_in, 16)
            sp.dma_start(b_out, ins["hy_b_out"][0].partition_broadcast(P)).then_inc(row_in, 16)

        @block.tensor
        def _(pe):
            for od in range(2):
                if od:
                    pe.wait_ge(y_ready, 8)
                for i in range(TT):
                    for m in range(CH):
                        mm = pe.transpose(s.psum[i * 2 + m // 4][:, m % 4 * P:(m % 4 + 1) * P], u[:, m, i * P:(i + 1) * P], s.c("ident"))
                        if m % 4 == 3:
                            mm.then_inc(vT_done, 1)
                pe.wait_ge(vt_ready, od * 4 + 4)
                for n in range(8):
                    part, ft, half = n // 4, n // 2 % 2, n % 2
                    for i in range(TT):
                        mm = pe.matmul(s.psum[(n + 4) % 8][:, :], fwd[part][:, i, ft * P:(ft + 1) * P],
                                       vt[:, i, half * 512:(half + 1) * 512], start=(i == 0), stop=(i == TT - 1))
                    mm.then_inc(dft_done, 1)
                pe.wait_ge(prod_ready, od * 2 + 2)
                for m in range(CH):
                    pe.wait_ge(vhat_ready, od * 8 + 8)
                    k = 0
                    for part in range(2):
                        for ft in range(2):
                            mm = pe.matmul(s.psum[m][:, 0:L], prod[:, part, ft, m * P:(m + 1) * P], inv[part][:, ft],
                                           start=(k == 0), stop=(k == 3))
                            k += 1
                    mm.then_inc(y_done, 1)
            for m in range(CH):
                pe.wait_ge(y_ready, 16)
                if m % 4 == 0:
                    pe.wait_ge(wout_in[m // 4], 16)
                for i in range(TT):
                    for h in range(2):
                        mm = pe.matmul(s.psum[i * 2 + h][:, :], u[:, m, i * P:(i + 1) * P], w_out[:, m, h * 512:(h + 1) * 512],
                                       start=(m == 0), stop=(m == CH - 1))
                        if m == CH - 1:
                            mm.then_inc(o_done, 1)

        @block.scalar
        def _(act):
            for od in range(2):
                for n in range(4):
                    act.wait_ge(vT_done, od * 4 + n + 1)
                    act.activation(vt[:, n // 2, n % 2 * 512:(n % 2 + 1) * 512], s.psum[n][:, :], ACT.Copy).then_inc(vt_ready, 1)
                for n in range(8):
                    part, ft, half = n // 4, n // 2 % 2, n % 2
                    act.wait_ge(dft_done, od * 8 + n + 1)
                    act.activation(vhat[:, part, ft, half * 512:(half + 1) * 512], s.psum[(n + 4) % 8][:, :], ACT.Copy).then_inc(vhat_ready, 1)

        @block.vector
        def _(dve):
            for od in range(2):
                c, d = khat[:, od, 0], khat[:, od, 1]
                dve.wait_ge(vhat_ready, od * 8 + 8)
                t = w_scratch
                dve.tensor_tensor(prod[:, 0], vhat[:, 0], c, ALU.mult)
                dve.tensor_tensor(t, vhat[:, 1], d, ALU.mult)
                dve.drain()
                dve.tensor_tensor(prod[:, 0], prod[:, 0], t, ALU.subtract).then_inc(prod_ready, 1)
                dve.drain()
                dve.tensor_tensor(prod[:, 1], vhat[:, 0], d, ALU.mult)
                dve.tensor_tensor(t, vhat[:, 1], c, ALU.mult)
                dve.drain()
                dve.tensor_tensor(prod[:, 1], prod[:, 1], t, ALU.add).then_inc(prod_ready, 1)
                for m in range(CH):
                    dve.wait_ge(y_done, od * 8 + m + 1)
                    dve.tensor_scalar(u[:, m], u[:, m], skip[:, od * CH + m:od * CH + m + 1], None, ALU.mult)
                    dve.drain()
                    dve.scalar_tensor_tensor(u[:, m], s.psum[m][:, 0:L], norm[:, od * CH + m:od * CH + m + 1], u[:, m], ALU.mult, ALU.add)
                    dve.drain()
                    dve.tensor_tensor(u[:, m], u[:, m], u[:, (1 + od) * CH + m], ALU.mult).then_inc(y_ready, 1)
            dve.wait_ge(row_in, 32)
            out = khat.rearrange("p a b c d -> p (a b c d)")
            for i in range(TT):
                for h in range(2):
                    k = i * 2 + h
                    c = slice(h * 512, (h + 1) * 512)
                    part = out[:, k * 512:(k + 1) * 512]
                    dve.wait_ge(o_done, k + 1)
                    dve.tensor_tensor(part, s.psum[k][:, :], b_out[:, c], ALU.add)
                    dve.drain()
                    dve.tensor_tensor(part, part, gate[:, c], ALU.mult)
                    dve.drain()
                    dve.tensor_tensor(s.x_res[:, i, c], s.x_res[:, i, c], part, ALU.add)


def final_norm(s, ins, out):
    nc = s.nc
    s.at = 0
    g = s.take(D)
    junk = s.take(D)
    y = s.take(TT, D)
    stat = s.take(2)
    g_in, sq_done, var_done, root_done, y_ready, y_out = (s.sem("fin_" + n) for n in ("g", "sq", "var", "root", "y", "out"))
    with nc.Block(name="final_norm", no_gpsimd_drain=True) as block:

        @block.sync
        def _(sp):
            sp.dma_start(g, ins["final_g"].partition_broadcast(P)).then_inc(g_in, 16)
            dst = out[0].rearrange("(i p) d -> i p d", p=P)
            for i in range(TT):
                sp.wait_ge(y_ready, i + 1)
                sp.dma_start(dst[i], y[:, i]).then_inc(y_out, 16)
            sp.wait_ge(y_out, 16 * TT)

        @block.scalar
        def _(act):
            for i in range(TT):
                act.activation(junk, s.x_res[:, i], ACT.Square, accum_out=stat[:, i:i + 1])
                act.drain()
            act.sem_inc(sq_done, 1)
            act.wait_ge(var_done, 1)
            act.activation(stat, stat, ACT.Sqrt).then_inc(root_done, 1)

        @block.vector
        def _(dve):
            dve.wait_ge(sq_done, 1)
            dve.tensor_scalar(stat, stat, 1.0 / D, NORM_EPS, ALU.mult, ALU.add).then_inc(var_done, 1)
            dve.wait_ge(root_done, 1)
            dve.reciprocal(stat, stat)
            dve.wait_ge(g_in, 16)
            dve.drain()
            for i in range(TT):
                dve.scalar_tensor_tensor(y[:, i], s.x_res[:, i], stat[:, i:i + 1], g, ALU.mult, ALU.mult).then_inc(y_ready, 1)


def load_constants(s, ins):
    nc = s.nc
    const_in = s.sem("const_in")
    with nc.Block(name="constants", no_gpsimd_drain=True) as block:

        @block.sync
        def _(sp):
            sp.dma_start(s.const[:, :], ins["const"]).then_inc(const_in, 16)
            sp.wait_ge(const_in, 16)


USED = ["x", "c", "ctx", "c_ctx", "ada_w", "ada_b", "norm_g", "final_g",
        "rw_mix", "rw_wrkv", "rw_wo", "rw_w0", "rw_w1", "rw_w2", "rw_a0", "rw_a1", "rw_a2", "rw_g1", "rw_g2",
        "rw_kk", "rw_ka", "rw_rk", "rw_lnw", "rw_lnb",
        "hy_w_in", "hy_b_in", "hy_conv_w", "hy_conv_b", "hy_f_w1", "hy_f_b1", "hy_f_freq", "hy_f_wi", "hy_f_bi",
        "hy_f_w3", "hy_skip", "hy_w_out", "hy_b_out",
        "moe_router", "moe_router_b", "moe_w_gate", "moe_w_up", "moe_w_down"]
ARENA = 48000


def build(nc, ins, out):
    mods = nc.dram_tensor("mods", (2, 2, 6 * D), F32, kind="Internal").ap()
    with ExitStack() as ctx:
        s = Shared(nc, ctx, ARENA)
        load_constants(s, ins)
        modulation(s, ins, mods)
        r = RwkvTensors(s)
        rwkv_inputs(s, r, ins, mods)
        rwkv_heads(s, r, ins)
        rwkv_output(s, r, ins, mods)
        s.clear_semaphores()
        expert_layer(s, 0, ins, mods)
        hyena_layer(s, ins, mods)
        expert_layer(s, 1, ins, mods)
        final_norm(s, ins, out)


def kernel(**inputs):
    import concourse.bacc as bacc
    from concourse.bass_utils import run_bass_kernel_spmd

    nc = bacc.Bacc("TRN2", target_bir_lowering=False, num_devices=1)
    arrays = {f"in_{n}": np.ascontiguousarray(inputs[n]) for n in USED}
    arrays["in_const"], arrays["in_hy_const"], arrays["in_hy_deltas"] = CONST_ARRAY, HY_CONST, HY_DELTAS
    ins = {n[3:]: nc.dram_tensor(n, a.shape, F32, kind="ExternalInput").ap() for n, a in arrays.items()}
    out = nc.dram_tensor("out", (1, L, D), F32, kind="ExternalOutput").ap()
    build(nc, ins, out)
    result = run_bass_kernel_spmd(nc, [arrays], core_ids=[0])
    return result.results[0]["out"]
```

```python
import math
from contextlib import ExitStack

import numpy as np

import concourse.bass as bass
from concourse import mybir

F32 = mybir.dt.float32
I32 = mybir.dt.int32
U32 = mybir.dt.uint32
ALU = mybir.AluOpType
ACT = mybir.ActivationFunctionType
AX = mybir.AxisListType

P = 128
D = 1024
L = 256
KT = D // P
TT = L // P
NORM_EPS = 1e-6
EXPERTS, GROUPS, PER_GROUP, HIDDEN = 32, 4, 8, 512
CAP = 64
HK = HIDDEN // P
EXTRA = 8
PAIRS = EXPERTS // 2


def constants():
    i = np.arange(P)
    r, c = i[:, None], i[None, :]
    parts = {
        "ident": (r == c),
        "ones": np.ones((P, P)),
        "before": (r < c),
        "after": (r > c),
        "head_ones": (r // 64 == c // 64),
        "upto": (r <= c),
        "from": (r >= c),
    }
    for n in range(7):
        b = 2 ** n
        same = (r // (2 * b) == c // (2 * b))
        parts[f"low{n}"] = same & (r % (2 * b) >= b) & (c % (2 * b) < b)
        parts[f"up{n}"] = parts[f"low{n}"].T
    parts["iota"] = np.broadcast_to(c, (P, P))
    at, cols = {}, 0
    for name, m in parts.items():
        at[name] = cols
        cols += P
    return at, np.concatenate([np.asarray(m, np.float32) for m in parts.values()], 1)


CONST_AT, CONST_ARRAY = constants()
N_CONST = CONST_ARRAY.shape[1]


class Shared:

    def __init__(self, nc, ctx, arena_cols):
        self.nc, self.ctx = nc, ctx
        self.const = ctx.enter_context(nc.sbuf_tensor("const", [P, N_CONST], F32))
        self.x_res = ctx.enter_context(nc.sbuf_tensor("x_res", [P, TT, D], F32))[:, :, :]
        self.cond = ctx.enter_context(nc.sbuf_tensor("cond", [P, KT], F32))[:, :]
        self.arena = ctx.enter_context(nc.sbuf_tensor("arena", [P, arena_cols], F32))
        self.banks = ctx.enter_context(nc.psum_tensor("banks", [P, 8, 512], F32))
        self.psum = [self.banks[:, b] for b in range(8)]
        self.cols = arena_cols
        self.at = 0
        self.sems = []

    def c(self, name, width=P, rows=P):
        return self.const[0:rows, CONST_AT[name]:CONST_AT[name] + width]

    def sem(self, name):
        self.sems.append(self.nc.alloc_semaphore(name=name))
        return self.sems[-1]

    def clear_semaphores(self):
        self.nc.clear_and_free_semaphores(self.sems)
        self.sems = []
        self.nc.all_engine_barrier()

    def take(self, *shape):
        n = int(np.prod(shape))
        assert self.at + n <= self.cols, (self.at, n, self.cols)
        v = self.arena[:, self.at:self.at + n]
        self.at += n
        names = " ".join(f"a{i}" for i in range(len(shape)))
        if len(shape) > 1:
            v = v.rearrange(f"p ({names}) -> p {names}", **{f"a{i}": s for i, s in enumerate(shape)})
        return v


FIRST = 2 * D


class FirstModulation:
    PARTS = FIRST // 512

    def __init__(self, s, ins, mods, low):
        self.s, self.ins, self.mods = s, ins, mods
        self.raw, self.sig, self.cond = s.take(2, KT), s.take(2, KT), s.take(KT, 32)
        self.w = [low[:, t * FIRST:(t + 1) * FIRST] for t in range(6)] + [s.take(FIRST) for _ in range(KT - 6)]
        self.bias, self.row = s.take(512), s.take(512)
        self.cond_in, self.sig_done, self.cond_ready = s.sem("cond_in"), s.sem("cond_sig"), s.sem("cond_ready")
        self.ada_in = [s.sem(f"ada_in{t}") for t in range(KT)]
        self.bias_in, self.sum_done, self.row_ready, self.row_out = (s.sem(n) for n in ("ada_b_in", "ada_sum", "ada_row", "ada_row_out"))

    def load_conditions(self, sp):
        sp.dma_start(self.raw[:, 0], self.ins["c"].rearrange("b (p t) -> p (b t)", t=KT)).then_inc(self.cond_in, 16)
        sp.dma_start(self.raw[:, 1], self.ins["c_ctx"].rearrange("(p t) -> p t", t=KT)).then_inc(self.cond_in, 16)

    def load_weights(self, sp):
        ada = self.ins["ada_w"].rearrange("l (p t) n -> l p t n", t=KT)
        for q in range(self.PARTS):
            sp.dma_start(self.bias[q * 32:(q + 1) * 32, :],
                         self.ins["ada_b"][0, q * 512:(q + 1) * 512].partition_broadcast(32)).then_inc(self.bias_in, 16)
        for t in range(KT):
            sp.dma_start(self.w[t], ada[0, :, t, 0:FIRST]).then_inc(self.ada_in[t], 16)

    def sigmoid(self, act):
        act.wait_ge(self.cond_in, 32)
        act.activation(self.sig, self.raw, ACT.Sigmoid).then_inc(self.sig_done, 1)

    def store(self, act):
        act.wait_ge(self.row_ready, 1)
        for q in range(self.PARTS):
            for i in range(2):
                act.dma_start(self.mods[0, i, q * 512:(q + 1) * 512].unsqueeze(0),
                              self.row[q * 32 + i:q * 32 + i + 1, :]).then_inc(self.row_out, 16)

    def wait_stored(self, sp):
        sp.wait_ge(self.row_out, self.PARTS * 2 * 16)

    def products(self, pe, bank):
        pe.wait_ge(self.cond_ready, 1)
        for t in range(KT):
            pe.wait_ge(self.ada_in[t], 16)
            for q in range(self.PARTS):
                mm = pe.matmul(bank[q * 32:(q + 1) * 32, :], self.cond[:, t],
                               self.w[t][:, q * 512:(q + 1) * 512], start=(t == 0), stop=(t == KT - 1),
                               tile_position=(0, q * 32))
                if t == KT - 1:
                    mm.then_inc(self.sum_done, 1)

    def conditions(self, dve):
        dve.memset(self.cond, 0.0)
        dve.drain()
        dve.wait_ge(self.sig_done, 1)
        dve.tensor_tensor(self.s.cond, self.raw[:, 0], self.sig[:, 0], ALU.mult)
        dve.tensor_tensor(self.cond[:, :, 0:2].rearrange("p t i -> p i t"), self.raw, self.sig, ALU.mult).then_inc(self.cond_ready, 1)

    def add_bias(self, dve, bank):
        dve.wait_ge(self.sum_done, self.PARTS)
        dve.wait_ge(self.bias_in, self.PARTS * 16)
        dve.tensor_tensor(self.row, bank[:, :], self.bias, ALU.add).then_inc(self.row_ready, 1)


class LaterModulation:
    PIECES = 3
    RING = 4
    OPS = PIECES * KT

    def __init__(self, s, ins, mods):
        self.s, self.ins, self.mods = s, ins, mods
        self.acc = [s.take(512), s.take(384), s.take(384)]
        self.ring = [s.take(512) for _ in range(self.RING)]
        self.bias, self.row = s.take(512), s.take(512)
        self.w_in = [s.sem(f"later_w_in{k}") for k in range(self.RING)]
        self.bias_in, self.used, self.row_out = (s.sem(n) for n in ("later_b_in", "later_used", "later_out"))

    @staticmethod
    def width(piece):
        return 512 if piece == 0 else 384

    def columns(self, m, piece):
        if piece == 0:
            return 0, m.at(512, FIRST)
        return 1, m.at(2 * 384, (piece - 1) * 384)

    def place(self, m, piece):
        layer, col = self.columns(m, piece)
        return layer, (bass.ds(col, self.width(piece)) if m.q is not None else slice(col, col + self.width(piece)))

    def load(self, sp, m):
        ada = self.ins["ada_w"].rearrange("l (p t) n -> l p t n", t=KT)
        for k in range(self.OPS):
            piece, t = divmod(k, KT)
            layer, cols = self.place(m, piece)
            if not (m.first and k < self.RING):
                sp.wait_ge(self.used, m.at(self.OPS, k - self.RING + 1))
            if t == 0:
                sp.dma_start(self.bias[0:1, 0:self.width(piece)], self.ins["ada_b"][layer, cols].unsqueeze(0)).then_inc(self.bias_in, 16)
            sp.dma_start(self.ring[k % self.RING][:, 0:self.width(piece)], ada[layer, :, t, cols]).then_inc(self.w_in[k % self.RING], 16)

    def accumulate(self, dve, m, k, wait_summed):
        dve.drain()
        piece, t = divmod(k, KT)
        acc = self.acc[piece][:, 0:self.width(piece)]
        w = self.ring[k % self.RING][:, 0:self.width(piece)]
        if t == 0:
            dve.wait_ge(self.bias_in, m.at(16 * self.PIECES, 16 * (piece + 1)))
            if not m.first:
                wait_summed(piece)
        dve.wait_ge(self.w_in[k % self.RING], m.at(16 * (self.OPS // self.RING), 16 * (k // self.RING + 1)))
        add = self.bias[:, 0:self.width(piece)] if t == 0 else acc
        dve.scalar_tensor_tensor(acc, w, self.s.cond[:, t:t + 1], add, ALU.mult, ALU.add).then_inc(self.used, 1)

    def total(self, pe, m, piece, bank):
        pe.wait_ge(self.used, m.at(self.OPS, KT * (piece + 1)))
        return pe.matmul(bank[0:1, 0:self.width(piece)], self.s.c("ones")[:, 0:1], self.acc[piece][:, 0:self.width(piece)], start=True, stop=True)


RW_LORA = 64
RW_GATE = 160
HEAD = 64
RW_LN_EPS = 64e-5
TOK = 2 * L
CH = D // P
HALF_DECAY = math.exp(-0.5)


class RwkvTensors:

    def __init__(self, s):
        s.at = 0
        self.xk, self.xv = s.take(KT, TOK), s.take(KT, TOK)
        self.xr = s.take(KT, L)
        self.wl, self.al = s.take(TOK), s.take(TOK)
        self.gl = s.take(2, L)
        self.oT = s.take(CH, L)
        self.chv = s.take(9, CH)
        self.after = s.at


def rwkv_inputs(s, r, ins, mods):
    nc = s.nc
    s.at = r.after
    hT = s.take(KT * 2, L + 2)
    xx = s.take(KT * 2, L)
    xw, xa = s.take(KT, TOK), s.take(KT, TOK)
    xg = s.take(KT, L)
    w1, a1 = s.take(KT, 2, RW_LORA), s.take(KT, 2, RW_LORA)
    g1 = s.take(KT, RW_GATE)
    ctxn = xw.rearrange("p (i a) b -> p i (a b)", i=4)[:, 0:TT]
    xn = xa.rearrange("p (i a) b -> p i (a b)", i=4)[:, 0:TT]
    xx_n = xx.rearrange("p (i a) b -> p i (a b)", i=4)[:, 2:4]
    junk = xx.rearrange("p a b -> p (a b)")[:, 0:D]
    rows = xg.rearrange("p a b -> p (a b)")[:, 0:P]
    mix = s.take(6, KT)
    sc, sh, ng = s.take(2, KT), s.take(2, KT), s.take(KT)
    stat = s.take(4)
    first = FirstModulation(s, ins, mods, s.arena[:, 0:6 * FIRST])
    tok_in, vec_in, rows_in, w_in = s.sem("tok_in"), s.sem("vec_in"), s.sem("chrow_in"), s.sem("lora_in")
    sq_done, var_done, root_done, xn_ready = s.sem("sq_done"), s.sem("var_done"), s.sem("root1"), s.sem("xn_ready")
    scale_ready, xnT_done, hT_ready = s.sem("scale_ready"), s.sem("xnT_done"), s.sem("hT_ready")
    chv_done, pad_done, mixed = s.sem("chv_done"), s.sem("pad_done"), s.sem("mixed")
    lora_done, lora_out = s.sem("lora_done"), s.sem("lora_out")
    order = ("w", "a", "g", "k", "r")
    turn_order = (1, 2, 3, 4, 5, 6, 7, 0)
    which = {"r": 0, "w": 1, "k": 2, "v": 3, "a": 4, "g": 5}
    dst = {"r": r.xr, "w": xw, "k": r.xk, "v": r.xv, "a": xa, "g": xg}
    xx_ready = s.sem("xx_ready")

    def mix_tokens(dve, name):
        k = which[name]
        for t in range(KT):
            if name in "rg":
                args = (dst[name][:, t], xx[:, t * 2 + 1], mix[:, k, t:t + 1], hT[:, t * 2 + 1, 1:L + 1])
            else:
                args = (dst[name][:, t].rearrange("p (i c) -> p i c", i=2), xx[:, t * 2:t * 2 + 2],
                        mix[:, k, t:t + 1], hT[:, t * 2:t * 2 + 2, 1:L + 1])
            op = dve.scalar_tensor_tensor(*args, ALU.mult, ALU.add)
        return op

    tiles = [(ctxn, 0), (ctxn, 1), (s.x_res, 0), (s.x_res, 1)]

    with nc.Block(name="rwkv_inputs", no_gpsimd_drain=True) as block:

        @block.sync
        def _(sp):
            first.load_conditions(sp)
            sp.dma_start(ctxn, ins["ctx"].rearrange("b (i p) d -> p (b i) d", p=P)).then_inc(tok_in, 16)
            sp.dma_start(s.x_res, ins["x"].rearrange("b (i p) d -> p (b i) d", p=P)).then_inc(tok_in, 16)
            sp.dma_start(ng, ins["norm_g"][0, 0].rearrange("(p t) -> p t", t=KT)).then_inc(vec_in, 16)
            sp.dma_start(mix, ins["rw_mix"][0].rearrange("n (p t) -> p n t", t=KT)).then_inc(vec_in, 16)
            vecs = [ins["rw_w0"][0, 0], ins["rw_w0"][0, 1], ins["rw_a0"][0, 0], ins["rw_a0"][0, 1], ins["rw_kk"][0],
                    ins["rw_ka"][0], ins["rw_lnw"][0], ins["rw_lnb"][0], ins["rw_rk"][0].rearrange("h k -> (h k)")]
            for n, v in enumerate(vecs):
                sp.dma_start(rows[n * CH:(n + 1) * CH, :], v.rearrange("(m p) -> m p", p=P)).then_inc(rows_in, 16)
            first.load_weights(sp)
            for z in range(2):
                sp.dma_start(w1[:, :, z], ins["rw_w1"][0, z].rearrange("(p t) r -> p t r", t=KT)).then_inc(w_in, 16)
                sp.dma_start(a1[:, :, z], ins["rw_a1"][0, z].rearrange("(p t) r -> p t r", t=KT)).then_inc(w_in, 16)
            sp.dma_start(g1, ins["rw_g1"][0].rearrange("(p t) r -> p t r", t=KT)).then_inc(w_in, 16)
            first.wait_stored(sp)
            for i in range(2):
                sp.dma_start(sc[:, i], mods[0, 1 - i, D:2 * D].rearrange("(p t) -> p t", t=KT)).then_inc(vec_in, 16)
                sp.dma_start(sh[:, i], mods[0, 1 - i, 0:D].rearrange("(p t) -> p t", t=KT)).then_inc(vec_in, 16)

        @block.scalar
        def _(act):
            first.sigmoid(act)
            act.wait_ge(tok_in, 32)
            for n, (src, i) in enumerate(tiles):
                act.activation(junk, src[:, i], ACT.Square, accum_out=stat[:, n:n + 1])
                act.drain()
            act.sem_inc(sq_done, 1)
            act.wait_ge(var_done, 1)
            act.activation(stat, stat, ACT.Sqrt).then_inc(root_done, 1)
            first.store(act)
            act.wait_ge(scale_ready, 1)
            for k, t in enumerate(turn_order):
                act.wait_ge(xnT_done, k + 1)
                for i in range(2):
                    act.activation(hT[:, t * 2 + i, 1:L + 1], s.psum[t][:, i * L:(i + 1) * L], ACT.Identity,
                                   bias=sh[:, i, t:t + 1], scale=sc[:, i, t:t + 1]).then_inc(hT_ready, 1)
            act.wait_ge(lora_done, 1)
            act.activation(r.wl, s.psum[0][:, :], ACT.Tanh)
            act.wait_ge(lora_done, 2)
            act.activation(r.al, s.psum[1][:, :], ACT.Copy)
            act.wait_ge(lora_done, 3)
            act.activation(r.gl[:, 0], s.psum[2][:, 0:L], ACT.Sigmoid)
            act.activation(r.gl[0:RW_GATE - P, 1], s.psum[2][0:RW_GATE - P, L:2 * L], ACT.Sigmoid)

        @block.tensor
        def _(pe):
            pe.wait_ge(rows_in, 9 * 16)
            pe.transpose(s.psum[7][:, 0:9 * CH], rows[0:9 * CH, :], s.c("ident")[0:9 * CH, 0:9 * CH]).then_inc(chv_done, 1)
            pe.wait_ge(xn_ready, 4)
            pe.wait_ge(chv_done, 2)
            for t in turn_order:
                if t == 0:
                    first.products(pe, s.psum[0])
                    pe.wait_ge(first.row_ready, 1)
                for n in range(4):
                    src = xn[:, n, t::KT] if n < 2 else xx_n[:, n - 2, t::KT]
                    mm = pe.transpose(s.psum[t][:, n * P:(n + 1) * P], src, s.c("ident"))
                mm.then_inc(xnT_done, 1)
            pe.wait_ge(w_in, 5 * 16)
            pe.wait_ge(hT_ready, 2 * KT)
            for n, (w, x, bank) in enumerate(((w1, xw, 0), (a1, xa, 1))):
                pe.wait_ge(mixed, n + 1)
                for t in range(KT):
                    mm = pe.matmul(s.psum[bank][:, :], w[:, t].rearrange("p a b -> p (a b)"), x[:, t], start=(t == 0), stop=(t == KT - 1))
                mm.then_inc(lora_done, 1)
            pe.wait_ge(mixed, 3)
            for t in range(KT):
                pe.matmul(s.psum[2][:, 0:L], g1[:, t, 0:P], xg[:, t], start=(t == 0), stop=(t == KT - 1))
            for t in range(KT):
                mm = pe.matmul(s.psum[2][0:RW_GATE - P, L:2 * L], g1[:, t, P:RW_GATE], xg[:, t], start=(t == 0), stop=(t == KT - 1))
            mm.then_inc(lora_done, 1)

        @block.vector
        def _(dve):
            dve.memset(hT[:, :, 0:1], 0.0)
            dve.memset(hT[:, :, L + 1:L + 2], 0.0)
            first.conditions(dve)
            dve.wait_ge(sq_done, 1)
            dve.tensor_scalar(stat, stat, 1.0 / D, NORM_EPS, ALU.mult, ALU.add).then_inc(var_done, 1)
            dve.wait_ge(root_done, 1)
            dve.reciprocal(stat, stat)
            dve.drain()
            for n, (src, i) in enumerate(tiles):
                out = xn[:, n] if n < 2 else xx_n[:, n - 2]
                dve.tensor_scalar(out, src[:, i], stat[:, n:n + 1], None, ALU.mult).then_inc(xn_ready, 1)
            dve.wait_ge(chv_done, 1)
            dve.tensor_copy(r.chv.rearrange("p a b -> p (a b)"), s.psum[7][:, 0:9 * CH]).then_inc(chv_done, 1)
            first.add_bias(dve, s.psum[0])
            dve.wait_ge(vec_in, 6 * 16)
            dve.tensor_scalar(sc, sc, 1.0, None, ALU.add)
            dve.drain()
            dve.tensor_tensor(sc, sc, ng.unsqueeze(1).to_broadcast([P, 2, KT]), ALU.mult).then_inc(scale_ready, 1)
            dve.wait_ge(hT_ready, 2 * KT)
            dve.drain()
            dve.tensor_tensor(xx, hT[:, :, 0:L], hT[:, :, 2:L + 2], ALU.add)
            dve.drain()
            dve.scalar_tensor_tensor(xx, xx, 0.5, hT[:, :, 1:L + 1], ALU.mult, ALU.subtract)
            dve.drain()
            dve.sem_inc(xx_ready, 1)
            for name in order:
                mix_tokens(dve, name).then_inc(mixed, 1)

        @block.gpsimd
        def _(pool):
            pool.wait_ge(xx_ready, 1)
            to = lambda t: r.xv[:, t].rearrange("p (i c) -> p i c", i=2)
            for t in range(KT):
                pool.tensor_scalar(to(t), xx[:, t * 2:t * 2 + 2], mix[:, which["v"], t:t + 1], None, ALU.mult)
            pool.drain()
            for t in range(KT):
                pool.tensor_tensor(to(t), to(t), hT[:, t * 2:t * 2 + 2, 1:L + 1], ALU.add)
            pool.drain()


STEPS = TOK // P
CHUNK = [[0, 1, 2, 3], [1, 0, 3, 2]]
LEVELS = 7
INV = 2 * (LEVELS - 1)
USES = ("v_tok", "b_tok0", "k_tok0", "b_tok1", "k_tok1", "w0", "w1", "a0", "a1", "rows", "k", "norm", "later0", "rg", "v",
        "later1", "later2", "spare")
FIRST_USES = ("w0", "w1", "a0", "a1", "k", "norm", "rg", "v")


class BlockIndex:

    def __init__(self, q, scale, offset):
        self.q, self.scale, self.offset = q, scale, offset

    def at(self, each, more):
        n = self.offset * each + more
        return n if self.q is None else self.q * (self.scale * each) + n

    def plus(self, k):
        return BlockIndex(self.q, self.scale, self.offset + k)

    @property
    def parity(self):
        return self.offset % 2

    @property
    def first(self):
        return self.q is None and self.offset == 0

    @property
    def last(self):
        return self.q is None and self.offset == CH - 1

    def use_plus(self, name, k):
        if self.q is None and self.offset == -1:
            return FIRST_USES.index(name) + k
        return self.at(len(USES), len(FIRST_USES) + USES.index(name) + k)

    def open_bank(self, name):
        names = FIRST_USES if self.q is None and self.offset == -1 else USES
        return 4 + names.index(name) % 2


def over_blocks(eng, before, body, after):
    before(BlockIndex(None, 0, -1))
    body(BlockIndex(None, 0, 0))
    with eng.Fori(0, CH // 2 - 1) as q:
        body(BlockIndex(q, 2, 1))
        body(BlockIndex(q, 2, 2))
    body(BlockIndex(None, 0, CH - 1))
    after(BlockIndex(None, 0, CH))


def rwkv_heads(s, r, ins, mods):
    nc = s.nc
    s.at = r.after
    wkv = [s.take(KT, P) for _ in range(3)]
    w2, a2 = s.take(P), s.take(P)
    g2 = s.take(2, P)
    cv, cvo = s.take(16), s.take(4)
    kT, kk = s.take(TOK), s.take(TOK)
    vT = [s.take(TOK) for _ in range(2)]
    gT = [s.take(L) for _ in range(2)]
    rT = s.take(L)
    A = [[s.take(TOK) for _ in range(2)] for _ in range(2)]
    R = [[s.take(L) for _ in range(2)] for _ in range(2)]
    B = [s.take(TOK) for _ in range(2)]
    K = [s.take(TOK) for _ in range(2)]
    Vtok = [s.take(STEPS, P) for _ in range(2)]
    Btok = [s.take(STEPS, P) for _ in range(2)]
    Ktok = [s.take(STEPS, P) for _ in range(2)]
    sg = [s.take(TOK) for _ in range(2)]
    cum = [s.take(TOK) for _ in range(2)]
    exR = [s.take(L) for _ in range(2)]
    av = [s.take(TOK) for _ in range(2)]
    kd = [s.take(TOK) for _ in range(2)]
    sqn = s.take(TOK)
    mid_, end_ = s.take(4), s.take(4)
    fargs = [s.take(4) for _ in range(2)]
    fade = [[s.take(4) for _ in range(2)] for _ in range(2)]
    Lm = [s.take(2, P) for _ in range(2)]
    XX = [[s.x_res[:, i, z * 512:(z + 1) * 512].rearrange("p (k h c) -> p k h c", k=2, h=2) for z in range(2)] for i in range(2)]
    Ln = [[None] + [s.take(2, P) for _ in range(1, LEVELS)] for _ in range(2)]
    Zm = [s.take(2, P) for _ in range(2)]
    LakT = [[s.take(2, P) for _ in range(2)] for _ in range(2)]
    ArkT = [[s.take(2, P) for _ in range(2)] for _ in range(2)]
    ArbT = [[s.take(2, P) for _ in range(2)] for _ in range(2)]
    G, U = s.take(2, P), s.take(2, P)
    H, Hn = s.take(2, P), s.take(2, P)
    yt, yc = s.take(TT, P), s.take(TT, P)
    st = s.take(8)
    bon = [s.take(L) for _ in range(2)]
    outT = s.take(TOK)
    ysq = outT[:, 0:L].rearrange("p (a b) -> p a b", a=TT)

    later = LaterModulation(s, ins, mods)
    last_use = BlockIndex(None, 0, CH - 1).use_plus("spare", 2)
    names = ("rw_w_in", "open_done", "open_read", "cv_ready", "sq_ready", "dec_ready", "ex_ready",
             "kk_ready", "kd_ready", "bon_ready", "feat_ready", "prod_done", "prod_read", "lm_ready", "x0_ready",
             "xt0_done", "xt0_ready", "ln_ready", "z_done", "z_ready", "x_done", "x_ready", "g_done", "gs_ready",
             "u_done", "us_ready", "hy_done", "h_ready", "y_var", "y_root", "yn_ready", "o_done", "pool_step")
    (w_in, open_done, open_read, cv_ready, sq_ready, dec_ready, ex_ready,
     kk_ready, kd_ready, bon_ready, feat_ready, prod_done, prod_read, lm_ready, x0_ready,
     xt0_done, xt0_ready, ln_ready, z_done, z_ready, x_done, x_ready, g_done, gs_ready,
     u_done, us_ready, hy_done, h_ready, yvar, yroot, yn_ready, o_done, pool_step) = (s.sem(n) for n in names)

    IB, CB = (2, 3), 7

    def two(v):
        return v.unsqueeze(1).to_broadcast([P, 2, P])

    def flat(v):
        return v.rearrange("p a b -> p (a b)")

    def cols(j, z):
        c = CHUNK[z][j]
        return slice(c * P, (c + 1) * P)

    def after_level(m, j, n, z):
        return m.at(STEPS * INV, j * INV + (n - 1) * 2 + z + 1)

    with nc.Block(name="rwkv_heads", no_gpsimd_drain=True) as block:

        @block.sync
        def _(sp):
            col = [ins["rw_wrkv"][0, n].rearrange("(p t) c -> p t c", t=KT) for n in range(3)]
            low = [ins["rw_w2"][0].rearrange("z r c -> (z r) c"), ins["rw_a2"][0].rearrange("z r c -> (z r) c"),
                   ins["rw_g2"][0, 0:P], ins["rw_g2"][0, P:RW_GATE]]

            def load(at):
                for n in range(3):
                    sp.dma_start(wkv[n], col[n][:, :, at]).then_inc(w_in, 16)
                sp.dma_start(w2, low[0][:, at]).then_inc(w_in, 16)
                sp.dma_start(a2, low[1][:, at]).then_inc(w_in, 16)
                sp.dma_start(g2[:, 0], low[2][:, at]).then_inc(w_in, 16)
                sp.dma_start(g2[0:RW_GATE - P, 1], low[3][:, at]).then_inc(w_in, 16)

            def round_(m):
                sp.wait_ge(open_done, m.plus(-1).use_plus("v", 1))
                if not m.last:
                    at = m.plus(1).at(P, 0)
                    load(bass.ds(at, P) if m.q is not None else slice(at, at + P))
                later.load(sp, m)

            load(slice(0, P))
            over_blocks(sp, lambda m: None, round_, lambda m: None)

        @block.gpsimd
        def _(pool):
            def level_parts(m, j):
                for n in range(1, LEVELS):
                    if n >= 5 and not (m.first and j == 0):
                        before = after_level(m, j - 1, n, 1) if j else after_level(m.plus(-1), STEPS - 1, n, 1)
                        pool.wait_ge(z_done, before)
                        pool.sem_inc(pool_step, 1)
                    for z in range(2):
                        if n == 1:
                            pool.wait_ge(lm_ready, m.at(8, j * 2 + z + 1))
                            pool.sem_inc(pool_step, 1)
                        pool.tensor_tensor(Ln[z][n], Lm[z], two(s.c(("low", "up")[z] + str(n))), ALU.mult)
                        pool.drain()
                        pool.sem_inc(ln_ready, 1)

            def keys(m):
                nx = m.plus(1)
                pool.wait_ge(open_read, m.use_plus("k", 1))
                pool.sem_inc(pool_step, 1)
                for z in range(2):
                    pool.tensor_scalar(kd[z], av[z], cv[:, 5:6], cv[:, 9:10], ALU.mult, ALU.add)
                pool.drain()
                for z in range(2):
                    pool.tensor_tensor(kd[z], kd[z], kT, ALU.mult)
                pool.drain()
                pool.sem_inc(kd_ready, 1)
                pool.wait_ge(open_read, m.use_plus("rg", 1))
                pool.sem_inc(pool_step, 1)
                to = bon[nx.parity]
                pool.tensor_tensor(to, kd[0][:, L:TOK], kd[1][:, L:TOK], ALU.add)
                pool.drain()
                pool.tensor_tensor(to, to, rT, ALU.mult)
                pool.drain()
                pool.tensor_scalar(to, to, cv[:, 8:9], None, ALU.mult)
                pool.drain()
                pool.sem_inc(bon_ready, 1)

            def before(m):
                keys(m)
                level_parts(m.plus(1), 0)

            def body(m):
                level_parts(m, 1)
                level_parts(m, 2)
                if not m.last:
                    keys(m)
                level_parts(m, 3)
                if not m.last:
                    level_parts(m.plus(1), 0)

            over_blocks(pool, before, body, lambda m: None)

        @block.tensor
        def _(pe):
            def open_bank(m, name):
                if not (m.offset == -1 and FIRST_USES.index(name) < 2):
                    pe.wait_ge(open_read, m.use_plus(name, -1))
                return s.psum[m.open_bank(name)]

            def low_rank(m, name):
                nx = m.plus(1)
                if name == "w0":
                    pe.wait_ge(w_in, nx.at(112, 112))
                z = int(name[1])
                w, x = (w2, r.wl) if name[0] == "w" else (a2, r.al)
                rows = slice(z * RW_LORA, (z + 1) * RW_LORA)
                pe.matmul(open_bank(m, name)[:, :], w[rows, :], x[rows, :], start=True, stop=True).then_inc(open_done, 1)

            def project(m, name, steps):
                n, x, n_c = {"k": (1, r.xk, TOK), "v": (2, r.xv, TOK), "rg": (0, r.xr, L)}[name]
                for t in steps:
                    if t == 0:
                        open_bank(m, name)
                    mm = pe.matmul(s.psum[m.open_bank(name)][:, 0:n_c], wkv[n][:, t], x[:, t], start=(t == 0), stop=(t == KT - 1))
                    if t == KT - 1 and name != "rg":
                        mm.then_inc(open_done, 1)

            def gate(m):
                bank = s.psum[m.open_bank("rg")]
                pe.matmul(bank[:, L:TOK], g2[:, 0], r.gl[:, 0], start=True, stop=False)
                rows = slice(0, RW_GATE - P)
                pe.matmul(bank[:, L:TOK], g2[rows, 1], r.gl[rows, 1], start=False, stop=True).then_inc(open_done, 1)

            def total(m, piece, uses=1):
                later.total(pe, m, piece, open_bank(m, f"later{piece}")).then_inc(open_done, uses)

            def norm(m):
                pe.wait_ge(sq_ready, m.plus(1).at(1, 1))
                pe.matmul(open_bank(m, "norm")[:, :], s.c("head_ones"), sqn, start=True, stop=True).then_inc(open_done, 1)

            def turn(m, n):
                name = USES[n]
                if n == 0:
                    pe.wait_ge(open_read, m.use_plus("v_tok", 0))
                src = (vT[m.parity], B[0], K[0], B[1], K[1])[n]
                bank = open_bank(m, name)
                for c in range(STEPS):
                    mm = pe.transpose(bank[:, c * P:(c + 1) * P], src[:, c * P:(c + 1) * P], s.c("ident"))
                mm.then_inc(open_done, 1)

            def rows(m):
                bank = open_bank(m, "rows")
                pe.wait_ge(bon_ready, m.at(1, 0))
                pe.matmul(bank[:, 0:L], s.c("head_ones"), bon[m.plus(1).parity], start=True, stop=True)
                pe.wait_ge(yn_ready, m.at(1, 0))
                for c in range(TT):
                    mm = pe.transpose(bank[:, L + c * P:L + (c + 1) * P], yc[:, c], s.c("ident"))
                mm.then_inc(open_done, 1)

            def products(m, j, z):
                par = m.parity
                c = cols(j, z)
                if j == 0:
                    pe.wait_ge(feat_ready, m.at(2, z + 1))
                if not (m.first and j == 0 and z == 0):
                    pe.wait_ge(prod_read, m.at(8, j * 2 + z))
                left = [A[par][z], K[z], K[z], B[z]]
                right = [B[z], A[par][z], R[par][z], R[par][z]]
                for n in range(4 if j >= 2 else 2):
                    cr = c if n < 2 else slice(c.start - L, c.stop - L)
                    for h in range(2):
                        rows = slice(h * HEAD, (h + 1) * HEAD)
                        mm = pe.matmul(s.psum[h][:, n * P:(n + 1) * P], left[n][rows, c], right[n][rows, cr], start=True, stop=True)
                        done = [mm] if h == 0 else done + [mm]
                for mm in done:
                    mm.then_inc(prod_done, 1)

            def chain_G(m, j):
                par = m.parity
                if j == 0:
                    pe.wait_ge(open_read, m.use_plus("k_tok1", 1))
                pe.wait_ge(h_ready, m.at(8, 2 * j + 2))
                for z in range(2):
                    for h in range(2):
                        o = slice(h * HEAD, (h + 1) * HEAD)
                        out = s.psum[CB][:, z * P + h * HEAD:z * P + (h + 1) * HEAD]
                        pe.matmul(out, A[par][z][:, cols(j, z)], H[:, z, o], start=True, stop=False)
                        mm = pe.matmul(out, LakT[j % 2][z][:, h], Vtok[par][:, CHUNK[z][j], o], start=False, stop=True)
                mm.then_inc(g_done, 1)

            def chain_U(m, j):
                pe.wait_ge(x_ready, after_level(m, j, LEVELS - 1, 1))
                pe.wait_ge(gs_ready, m.at(4, j + 1))
                for z in range(2):
                    for h in range(2):
                        o = slice(h * HEAD, (h + 1) * HEAD)
                        mm = pe.matmul(s.psum[CB][:, 256 + z * P + h * HEAD:256 + z * P + (h + 1) * HEAD], XX[j % 2][z][:, 1, h],
                                       G[:, z, o], start=True, stop=True)
                mm.then_inc(u_done, 1)

            def chain_HY(m, j):
                par = m.parity
                pe.wait_ge(us_ready, m.at(4, j + 1))
                for z in range(2):
                    c = CHUNK[z][j]
                    if j < STEPS - 1:
                        pe.matmul(s.psum[CB][:, z * P:(z + 1) * P], Btok[z][:, c], U[:, z], start=True, stop=False)
                        mm = pe.matmul(s.psum[CB][:, z * P:(z + 1) * P], Ktok[z][:, c], Vtok[par][:, c], start=False, stop=True)
                    if j >= 2:
                        y = s.psum[CB][:, 256 + z * P:256 + (z + 1) * P]
                        for h in range(2):
                            o = slice(h * HEAD, (h + 1) * HEAD)
                            pe.matmul(y[:, o], R[par][z][:, (c - 2) * P:(c - 1) * P], H[:, z, o], start=True, stop=False)
                            pe.matmul(y[:, o], ArbT[j % 2][z][:, h], U[:, z, o], start=False, stop=False)
                            mm = pe.matmul(y[:, o], ArkT[j % 2][z][:, h], Vtok[par][:, c, o], start=False, stop=True)
                mm.then_inc(hy_done, 1)

            def invert(m, j, slot):
                XXj = XX[j % 2]
                for z in range(2):
                    pe.wait_ge(x0_ready, m.at(8, j * 2 + z + 1))
                    if not (m.first and j == 0):
                        pe.wait_ge(x_ready, m.at(STEPS * INV, j * INV - 1 + z))
                    for h in range(2):
                        mm = pe.transpose(s.psum[IB[z]][:, 256 + h * P:256 + (h + 1) * P], XXj[z][:, 0, h], s.c("ident"))
                    mm.then_inc(xt0_done, 1)
                slot(0)
                for n in range(1, LEVELS):
                    for z in range(2):
                        pe.wait_ge(ln_ready, after_level(m, j, n, z))
                        if n == 1:
                            pe.wait_ge(xt0_ready, m.at(8, j * 2 + z + 1))
                        else:
                            pe.wait_ge(x_ready, after_level(m, j, n - 1, z))
                        for h in range(2):
                            mm = pe.matmul(s.psum[IB[z]][:, h * P:(h + 1) * P], Ln[z][n][:, h], XXj[z][:, 1, h], start=True, stop=True)
                        mm.then_inc(z_done, 1)
                    for z in range(2):
                        pe.wait_ge(z_ready, after_level(m, j, n, z))
                        for h in range(2):
                            mm = pe.matmul(s.psum[IB[z]][:, 256 + h * P:256 + (h + 1) * P], XXj[z][:, 0, h], Zm[z][:, h], start=True, stop=True)
                            if n < LEVELS - 1:
                                mm = pe.matmul(s.psum[IB[z]][:, h * P:(h + 1) * P], Zm[z][:, h], XXj[z][:, 0, h], start=True, stop=True)
                        mm.then_inc(x_done, 1)
                    slot(n)

            def before(m):
                for name in ("w0", "w1", "a0", "a1"):
                    low_rank(m, name)
                project(m, "k", range(KT))
                norm(m)
                project(m, "rg", range(KT))
                gate(m)
                project(m, "v", range(KT))
                for z in range(2):
                    products(m.plus(1), 0, z)

            def body(m):
                def skip():
                    pe.sem_inc(open_done, 1)

                def slot(j, n):
                    mc, jc = (m, j - 1) if j else (m.plus(-1), STEPS - 1)
                    if not (m.first and j == 0):
                        if n == 0:
                            chain_G(mc, jc)
                        if n == 1:
                            chain_U(mc, jc)
                        if n == 3:
                            chain_HY(mc, jc)
                    if n in (4, 5) and not (m.last and j == STEPS - 1):
                        mp, jp = (m, j + 1) if j < STEPS - 1 else (m.plus(1), 0)
                        products(mp, jp, n - 4)
                    if j == 0 and n < 5:
                        turn(m, n)
                    if (j, n) == (1, 2):
                        if m.first:
                            skip()
                        else:
                            rows(m)
                    if (j, n) == (3, 4):
                        total(m, 1)
                    if (j, n) == (3, 5):
                        total(m, 2, 2)
                    if m.last:
                        if (j, n) == (0, 6):
                            pe.sem_inc(open_done, 4)
                        if (j, n) == (1, 6):
                            pe.sem_inc(open_done, 2)
                            total(m, 0, 3)
                        return
                    if j == 0 and n == 5:
                        low_rank(m, "w0")
                        low_rank(m, "w1")
                    if j == 0 and n == 6:
                        low_rank(m, "a0")
                        low_rank(m, "a1")
                    if j == 1:
                        steps = {0: (0,), 1: (1,), 2: (2, 3), 3: (4,), 4: (5,), 5: (6, 7)}.get(n, ())
                        project(m, "k", steps)
                        if n == 6:
                            norm(m)
                            total(m, 0)
                    if j == 2 and n == 0:
                        project(m, "rg", (0, 1, 2))
                    if j == 2 and n == 1:
                        project(m, "rg", (3, 4, 5))
                    if j == 2 and n == 2:
                        project(m, "rg", (6, 7))
                        gate(m)
                    if j == 2:
                        project(m, "v", {3: (0,), 6: (1, 2)}.get(n, ()))
                    if j == 3:
                        project(m, "v", {0: (3,), 1: (4,), 2: (5, 6), 3: (7,)}.get(n, ()))

                for j in range(STEPS):
                    invert(m, j, lambda n: slot(j, n))

            def after(m):
                chain_G(m.plus(-1), STEPS - 1)
                chain_U(m.plus(-1), STEPS - 1)
                chain_HY(m.plus(-1), STEPS - 1)
                pe.wait_ge(yn_ready, CH)
                pe.wait_ge(open_read, last_use - 1)
                bank = s.psum[4]
                pe.matmul(bank[:, 0:L], s.c("head_ones"), bon[(CH - 1) % 2], start=True, stop=True)
                for c in range(TT):
                    mm = pe.transpose(bank[:, L + c * P:L + (c + 1) * P], yc[:, c], s.c("ident"))
                mm.then_inc(open_done, 1)

            over_blocks(pe, before, body, after)

        @block.scalar
        def _(act):
            def read(m, name, uses=1):
                act.wait_ge(open_done, m.use_plus(name, uses))
                return s.psum[m.open_bank(name)]

            def low_rank(m, name):
                nx = m.plus(1)
                if name == "w0":
                    act.wait_ge(cv_ready, nx.at(1, 1))
                    if m.offset != -1:
                        act.wait_ge(feat_ready, nx.at(2, 0))
                bank = read(m, name)
                z = int(name[1])
                dst, col = (sg[z], z) if name[0] == "w" else (av[z], 2 + z)
                act.activation(dst, bank[:, :], ACT.Sigmoid, bias=cv[:, col:col + 1]).then_inc(open_read, 1)

            def keys(m):
                bank = read(m, "k")
                act.activation(sqn, bank[:, :], ACT.Square, scale=cv[:, 4:5]).then_inc(sq_ready, 1)
                act.activation(kT, bank[:, :], ACT.Copy).then_inc(open_read, 1)

            def total(m, piece, uses=1):
                n = later.width(piece)
                if not (m.first and piece == 0):
                    act.wait_ge(later.row_out, m.at(16 * later.PIECES, 16 * piece))
                act.activation(later.row[0:1, 0:n], read(m, f"later{piece}", uses)[0:1, 0:n], ACT.Copy).then_inc(open_read, uses)
                act.wait_ge(open_read, m.use_plus(f"later{piece}", uses))
                layer, cols = later.place(m, piece)
                act.dma_start(mods[layer, 0, cols].unsqueeze(0), later.row[0:1, 0:n]).then_inc(later.row_out, 16)

            def norm(m):
                act.activation(sqn, read(m, "norm")[:, :], ACT.Sqrt).then_inc(open_read, 1)

            def receptance(m):
                bank = read(m, "rg")
                if m.offset != -1 and not m.first:
                    act.wait_ge(o_done, m.at(1, 0))
                act.activation(gT[m.plus(1).parity], bank[:, L:TOK], ACT.Copy)
                act.activation(rT, bank[:, 0:L], ACT.Copy).then_inc(open_read, 1)

            def values(m):
                act.activation(vT[m.plus(1).parity], read(m, "v")[:, :], ACT.Copy).then_inc(open_read, 1)

            def factors(m, z):
                nx = m.plus(1)
                act.wait_ge(dec_ready, nx.at(2, z + 1))
                inner, sign = (sg[z], -1.0) if z == 0 else (cum[z], 1.0)
                last = cum[z] if z == 0 else sg[z]
                act.activation(exR[z], last[:, L:TOK], ACT.Exp, scale=sign * HALF_DECAY)
                act.activation(inner, inner, ACT.Exp, scale=sign * HALF_DECAY)
                act.drain()
                act.activation(last, last, ACT.Exp, scale=-sign * HALF_DECAY)
                act.activation(fade[nx.parity][z][:, 0:3], fargs[z][:, 0:3], ACT.Exp, scale=-HALF_DECAY).then_inc(ex_ready, 1)

            def turn(m, n):
                dst = (Vtok[m.parity], Btok[0], Ktok[0], Btok[1], Ktok[1])[n]
                act.activation(flat(dst), read(m, USES[n])[:, :], ACT.Copy).then_inc(open_read, 1)

            def chain_G(m, j):
                act.wait_ge(g_done, m.at(4, j + 1))
                act.activation(flat(G), s.psum[CB][:, 0:2 * P], ACT.Copy).then_inc(gs_ready, 1)

            def chain_U(m, j):
                act.wait_ge(u_done, m.at(4, j + 1))
                act.activation(flat(U), s.psum[CB][:, 2 * P:4 * P], ACT.Copy).then_inc(us_ready, 1)

            def before(m):
                for name in ("w0", "w1", "a0", "a1"):
                    low_rank(m, name)
                keys(m)
                norm(m)
                receptance(m)
                values(m)
                for z in range(2):
                    factors(m, z)

            def body(m):
                def skip():
                    act.wait_ge(open_done, m.use_plus("rows", 1))
                    act.sem_inc(open_read, 1)

                def slot(j, n):
                    mc, jc = (m, j - 1) if j else (m.plus(-1), STEPS - 1)
                    if not (m.first and j == 0):
                        if n == 0:
                            chain_G(mc, jc)
                        if n == 1:
                            chain_U(mc, jc)
                    if j == 0 and n < 5:
                        turn(m, n)
                    if (j, n) == (1, 0) and not m.first:
                        act.wait_ge(yvar, m.at(1, 0))
                        act.activation(st[:, 4:8], st[:, 4:8], ACT.Sqrt).then_inc(yroot, 1)
                    if (j, n) == (1, 2):
                        if m.first:
                            skip()
                        else:
                            act.activation(outT, read(m, "rows")[:, :], ACT.Copy).then_inc(open_read, 1)
                    if (j, n) == (3, 4):
                        total(m, 1)
                    if (j, n) == (3, 5):
                        total(m, 2, 2)
                    if m.last:
                        if (j, n) == (0, 6):
                            act.sem_inc(open_read, 4)
                        if (j, n) == (1, 6):
                            act.sem_inc(open_read, 2)
                            total(m, 0, 3)
                        return
                    if j == 0 and n == 5:
                        low_rank(m, "w0")
                        low_rank(m, "w1")
                    if j == 0 and n == 6:
                        low_rank(m, "a0")
                        low_rank(m, "a1")
                    if j == 1 and n == 5:
                        keys(m)
                    if j == 1 and n == 6:
                        norm(m)
                        total(m, 0)
                    if j == 2 and n == 1:
                        factors(m, 0)
                    if j == 2 and n == 2:
                        receptance(m)
                    if j == 2 and n == 3:
                        factors(m, 1)
                    if j == 3 and n == 3:
                        values(m)

                for j in range(STEPS):
                    for z in range(2):
                        act.wait_ge(xt0_done, m.at(8, j * 2 + z + 1))
                        act.activation(XX[j % 2][z][:, 1].rearrange("p h c -> p (h c)"), s.psum[IB[z]][:, 256:512], ACT.Copy).then_inc(xt0_ready, 1)
                    slot(j, 0)
                    for n in range(1, LEVELS):
                        for z in range(2):
                            act.wait_ge(z_done, after_level(m, j, n, z))
                            act.activation(flat(Zm[z]), s.psum[IB[z]][:, 0:256], ACT.Copy).then_inc(z_ready, 1)
                        slot(j, n)

            def after(m):
                chain_G(m.plus(-1), STEPS - 1)
                chain_U(m.plus(-1), STEPS - 1)
                act.wait_ge(yvar, CH)
                act.activation(st[:, 4:8], st[:, 4:8], ACT.Sqrt).then_inc(yroot, 1)
                act.wait_ge(open_done, last_use)
                act.activation(outT, s.psum[4][:, :], ACT.Copy).then_inc(open_read, 1)
                act.wait_ge(later.row_out, CH * later.PIECES * 16)

            over_blocks(act, before, body, after)

        @block.vector
        def _(dve):
            def by_chunk(v):
                return v.rearrange("p (c t) -> p c t", c=STEPS)

            def vectors(m):
                dve.tensor_copy(cv[:, 0:9], chv_of(m.plus(1), 0, 9))
                dve.drain()
                dve.tensor_scalar(cv[:, 9:10], cv[:, 5:6], -1.0, 1.0, ALU.mult, ALU.add)
                dve.drain()
                dve.sem_inc(cv_ready, 1)

            def chv_of(m, a, b):
                at = bass.ds(m.at(1, 0), 1) if m.q is not None else slice(m.offset, m.offset + 1)
                return r.chv[:, a:b, at].rearrange("p n o -> p (n o)")

            def decay_sum(m, z):
                dve.wait_ge(open_read, m.use_plus(f"w{z}", 1))
                for c in range(STEPS):
                    cc = slice(c * P, (c + 1) * P)
                    dve.tensor_tensor_scan(cum[z][:, cc], s.c("ones"), sg[z][:, cc], 0.0, ALU.mult, ALU.add)
                dve.drain()

            def decay_centre(m, z):
                mid, end = by_chunk(cum[z])[:, :, HEAD - 1:HEAD], by_chunk(cum[z])[:, :, P - 1:P]
                dve.tensor_copy(mid_.unsqueeze(2), mid)
                dve.tensor_tensor(end_.unsqueeze(2), end, mid, ALU.subtract)
                dve.drain()
                dve.tensor_tensor(by_chunk(cum[z]), by_chunk(cum[z]), mid_.unsqueeze(2).to_broadcast([P, STEPS, P]), ALU.subtract)
                if z == 0:
                    dve.tensor_tensor(fargs[z][:, 0:3], end_[:, 0:3], mid_[:, 1:4], ALU.add)
                else:
                    for n in range(3):
                        a, b = CHUNK[1][n], CHUNK[1][n + 1]
                        dve.tensor_tensor(fargs[z][:, n:n + 1], mid_[:, a:a + 1], end_[:, b:b + 1], ALU.add)
                dve.drain()
                dve.tensor_tensor(sg[z], cum[z], sg[z], ALU.subtract).then_inc(dec_ready, 1)

            def key_norms(m, half):
                if half == 0:
                    dve.wait_ge(open_read, m.use_plus("norm", 1))
                    dve.tensor_scalar(sqn, sqn, 1e-12, None, ALU.max)
                    dve.drain()
                c = slice(half * L, (half + 1) * L)
                dve.reciprocal(sqn[:, c], sqn[:, c])
                dve.drain()

            def unit_keys():
                dve.scalar_tensor_tensor(kk, kT, cv[:, 4:5], sqn, ALU.mult, ALU.mult)
                dve.drain()

            def rates(z):
                dve.tensor_tensor(av[z], av[z], kk, ALU.mult)

            def features_AB(m, z):
                nx = m.plus(1)
                dve.wait_ge(ex_ready, nx.at(2, z + 1))
                ea, eb = (sg[z], cum[z]) if z == 0 else (cum[z], sg[z])
                dve.scalar_tensor_tensor(A[nx.parity][z], kk, -1.0, ea, ALU.mult, ALU.mult)
                dve.tensor_tensor(B[z], av[z], eb, ALU.mult)

            def features_KR(m, z):
                nx = m.plus(1)
                eb = cum[z] if z == 0 else sg[z]
                dve.wait_ge(open_read, m.use_plus("rg", 1))
                dve.tensor_tensor(K[z], kd[z], eb, ALU.mult)
                dve.tensor_tensor(R[nx.parity][z], rT, exR[z], ALU.mult)
                dve.drain()
                if z:
                    dve.wait_ge(bon_ready, nx.at(1, 1))
                dve.sem_inc(feat_ready, 1)

            def masked(m, j, z):
                strict, strict_T, incl_T = (("after", "before", "upto"), ("before", "after", "from"))[z]
                dve.wait_ge(prod_done, m.at(16, j * 4 + 2 * z + 2))
                if not (m.first and j == 0):
                    dve.wait_ge(ln_ready, m.at(STEPS * INV, j * INV))
                L_, Lak, Ark, Arb = (s.banks[:, 0:2, n * P:(n + 1) * P] for n in range(4))
                dve.tensor_tensor(Lm[z], L_, two(s.c(strict)), ALU.mult).then_inc(lm_ready, 1)
                X0 = XX[j % 2][z][:, 0]
                dve.tensor_tensor(X0, L_, two(s.c(("low0", "up0")[z])), ALU.mult)
                dve.tensor_tensor(LakT[j % 2][z], Lak, two(s.c(strict_T)), ALU.mult)
                if j >= 2:
                    dve.tensor_tensor(ArkT[j % 2][z], Ark, two(s.c(incl_T)), ALU.mult)
                    dve.tensor_tensor(ArbT[j % 2][z], Arb, two(s.c(incl_T)), ALU.mult)
                dve.drain()
                dve.sem_inc(prod_read, 1)
                dve.tensor_tensor(X0, X0, two(s.c("ident")), ALU.add).then_inc(x0_ready, 1)

            def level(m, j, n):
                for z in range(2):
                    XXz = XX[j % 2][z]
                    dve.wait_ge(x_done, after_level(m, j, n, z))
                    both = XXz.rearrange("p k h c -> p (k h c)")
                    at = slice(0, 512) if n < LEVELS - 1 else slice(256, 512)
                    dve.tensor_tensor(both[:, at], s.psum[IB[z]][:, at], both[:, at], ALU.add).then_inc(x_ready, 1)

            def state(m, j):
                dve.wait_ge(hy_done, m.at(4, j + 1))
                if j >= 2:
                    for z in range(2):
                        y, dst = s.psum[CB][:, 256 + z * P:256 + (z + 1) * P], yt[:, CHUNK[z][j] - 2]
                        if j == 2:
                            dve.tensor_copy(dst, y)
                        else:
                            dve.tensor_tensor(dst, y, dst, ALU.add)
                if j == STEPS - 1:
                    dve.memset(H, 0.0)
                    dve.drain()
                    dve.sem_inc(h_ready, 2)
                    return
                for z in range(2):
                    dve.tensor_tensor(Hn[:, z], s.psum[CB][:, z * P:(z + 1) * P], H[:, z], ALU.add)
                dve.drain()
                for z in range(2):
                    dve.scalar_tensor_tensor(H[:, z], Hn[:, z], fade[m.parity][z][:, j:j + 1], s.c("head_ones"), ALU.mult, ALU.mult).then_inc(h_ready, 1)

            y4, c4, q4 = (v.rearrange("p c (h k) -> p (c h) k", h=2) for v in (yt, yc, ysq))

            def row_means():
                dve.tensor_reduce(st[:, 0:4], y4, AX.X, ALU.add)
                dve.drain()
                dve.tensor_scalar(st[:, 0:4], st[:, 0:4], 1.0 / HEAD, None, ALU.mult)
                dve.drain()
                dve.tensor_tensor(c4, y4, st[:, 0:4].unsqueeze(2).to_broadcast([P, 4, HEAD]), ALU.subtract)
                dve.drain()

            def row_variances():
                dve.tensor_tensor(q4, c4, c4, ALU.mult)
                dve.drain()
                dve.tensor_reduce(st[:, 4:8], q4, AX.X, ALU.add)
                dve.drain()
                dve.tensor_scalar(st[:, 4:8], st[:, 4:8], 1.0 / HEAD, RW_LN_EPS, ALU.mult, ALU.add).then_inc(yvar, 1)

            def row_scales(m):
                dve.wait_ge(yroot, m.at(1, 1))
                dve.reciprocal(st[:, 4:8], st[:, 4:8])
                dve.drain()
                dve.tensor_tensor(c4, c4, st[:, 4:8].unsqueeze(2).to_broadcast([P, 4, HEAD]), ALU.mult).then_inc(yn_ready, 1)

            def output(m, read_count):
                par = m.parity
                dve.tensor_copy(cvo[:, 0:2], chv_of(m, 6, 8))
                dve.wait_ge(open_read, read_count)
                dve.tensor_tensor(outT[:, 0:L], outT[:, 0:L], vT[par][:, L:TOK], ALU.mult)
                dve.drain()
                dve.scalar_tensor_tensor(outT[:, 0:L], outT[:, L:TOK], cvo[:, 0:1], outT[:, 0:L], ALU.mult, ALU.add)
                dve.drain()
                at = bass.ds(m.at(1, 0), 1) if m.q is not None else slice(m.offset, m.offset + 1)
                dve.scalar_tensor_tensor(r.oT[:, at].rearrange("p o c -> p (o c)"), outT[:, 0:L], cvo[:, 1:2], gT[par], ALU.add, ALU.mult)
                dve.drain()
                dve.sem_inc(o_done, 1)

            def before(m):
                dve.memset(H, 0.0)
                dve.memset(later.bias, 0.0)
                dve.drain()
                dve.sem_inc(h_ready, 2)
                vectors(m)
                for z in range(2):
                    decay_sum(m, z)
                    decay_centre(m, z)
                key_norms(m, 0)
                key_norms(m, 1)
                unit_keys()
                dve.wait_ge(kd_ready, 1)
                dve.wait_ge(open_read, m.use_plus("rg", 1))
                for z in range(2):
                    rates(z)
                dve.drain()
                for z in range(2):
                    features_AB(m, z)
                    features_KR(m, z)
                for z in range(2):
                    masked(m.plus(1), 0, z)

            def body(m):
                def slot(j, n):
                    if j * LEVELS + n < later.OPS:
                        later.accumulate(dve, m, j * LEVELS + n,
                                         lambda piece: dve.wait_ge(open_read, m.plus(-1).use_plus(f"later{piece}", 1)))
                    mc, jc = (m, j - 1) if j else (m.plus(-1), STEPS - 1)
                    if n == 3 and not (m.first and j == 0):
                        state(mc, jc)
                    if n in (4, 5) and not (m.last and j == STEPS - 1):
                        mp, jp = (m, j + 1) if j < STEPS - 1 else (m.plus(1), 0)
                        masked(mp, jp, n - 4)
                    if not m.first:
                        if (j, n) == (0, 4):
                            row_means()
                        if (j, n) == (0, 6):
                            row_variances()
                        if (j, n) == (1, 0):
                            row_scales(m.plus(-1))
                        if (j, n) == (1, 4):
                            output(m.plus(-1), m.use_plus("rows", 1))
                    if m.last:
                        return
                    if (j, n) == (0, 1):
                        vectors(m)
                    if (j, n) == (1, 1):
                        decay_sum(m, 0)
                    if (j, n) == (1, 2):
                        decay_centre(m, 0)
                    if (j, n) == (1, 6):
                        decay_sum(m, 1)
                    if (j, n) == (2, 0):
                        decay_centre(m, 1)
                    if (j, n) == (2, 1):
                        key_norms(m, 0)
                    if (j, n) == (2, 2):
                        key_norms(m, 1)
                        unit_keys()
                    if (j, n) == (2, 5):
                        dve.wait_ge(kd_ready, m.plus(1).at(1, 1))
                        rates(0)
                        rates(1)
                        dve.drain()
                    if (j, n) == (2, 6):
                        features_AB(m, 0)
                    if (j, n) == (3, 0):
                        features_KR(m, 0)
                    if (j, n) == (3, 1):
                        features_AB(m, 1)
                    if (j, n) == (3, 2):
                        features_KR(m, 1)

                for j in range(STEPS):
                    slot(j, 0)
                    for n in range(1, LEVELS):
                        level(m, j, n)
                        slot(j, n)

            def after(m):
                state(m.plus(-1), STEPS - 1)
                row_means()
                row_variances()
                row_scales(m.plus(-1))
                output(m.plus(-1), last_use)

            over_blocks(dve, before, body, after)


def rwkv_output(s, r, ins, mods):
    nc = s.nc
    s.at = r.after
    wo = s.take(CH, D)
    gate = s.take(D)
    g_in, o_done = s.sem("gate1_in"), s.sem("wo_done")
    wo_in = [s.sem(f"wo_in{h}") for h in range(4)]
    with nc.Block(name="rwkv_output", no_gpsimd_drain=True) as block:

        @block.sync
        def _(sp):
            src = ins["rw_wo"][0].rearrange("(m p) n -> p m n", p=P)
            for h in range(4):
                sp.dma_start(wo[:, 2 * h:2 * h + 2], src[:, 2 * h:2 * h + 2]).then_inc(wo_in[h], 16)
            sp.dma_start(gate, mods[0, 0, 2 * D:3 * D].partition_broadcast(P)).then_inc(g_in, 16)
            sp.dma_start(s.x_res, ins["x"].rearrange("b (i p) d -> p (b i) d", p=P)).then_inc(g_in, 16)

        @block.tensor
        def _(pe):
            for m in range(CH):
                if m % 2 == 0:
                    pe.wait_ge(wo_in[m // 2], 16)
                for i in range(TT):
                    for h in range(2):
                        mm = pe.matmul(s.psum[i * 2 + h][:, :], r.oT[:, m, i * P:(i + 1) * P], wo[:, m, h * 512:(h + 1) * 512],
                                       start=(m == 0), stop=(m == CH - 1))
                        if m == CH - 1:
                            mm.then_inc(o_done, 1)

        @block.vector
        def _(dve):
            dve.wait_ge(g_in, 32)
            tmp = r.xk.rearrange("p a b -> p (a b)")
            for i in range(TT):
                for h in range(2):
                    k = i * 2 + h
                    c = slice(h * 512, (h + 1) * 512)
                    dve.wait_ge(o_done, k + 1)
                    dve.tensor_tensor(tmp[:, k * 512:(k + 1) * 512], s.psum[k][:, :], gate[:, c], ALU.mult)
                    dve.drain()
                    dve.tensor_tensor(s.x_res[:, i, c], s.x_res[:, i, c], tmp[:, k * 512:(k + 1) * 512], ALU.add)


def expert_layer(s, layer, ins, mods):
    nc = s.nc
    s.at = 0
    wg = [[s.take(KT, HIDDEN) for _ in range(2)] for _ in range(2)]
    wu = [s.take(KT, HIDDEN) for _ in range(2)]
    wd = [s.take(HK, D) for _ in range(2)]
    hx = s.take(TT, D)
    acc = s.take(TT, D)
    xg = s.take(D)
    xT = s.take(KT, P)
    sg = s.take(HIDDEN)
    h = s.take(HIDDEN)
    hT = s.take(HK, P)
    y = s.take(D)
    sel = [s.take(TT, 2, CAP) for _ in range(2)]
    selw = [s.take(TT, 2, CAP) for _ in range(2)]
    selwT = s.take(TT, P)
    NE = EXPERTS + EXTRA
    slot_of = s.take(TT, NE)
    weight_of = s.take(TT, NE)
    router = s.take(KT, GROUPS + EXPERTS)
    router_b = s.take(GROUPS + EXPERTS)
    logit = s.take(TT, GROUPS + EXPERTS)
    glog = s.take(TT, 8)
    top = s.take(TT, 8)
    topi = s.take(TT, 8).bitcast(U32)
    small = s.take(TT, 16)
    member = s.take(TT, EXPERTS)
    tmp = s.take(TT, EXPERTS)
    tmp2 = s.take(TT, EXPERTS)
    cnt = s.take(EXPERTS)
    flag = s.take(3, EXPERTS)
    order = s.take(3 * EXPERTS)
    num = s.take(3, EXPERTS)
    pick = s.take(3 * EXPERTS)
    prod = s.take(3 * EXPERTS)
    base = s.take(TT, 3, EXPERTS)
    wbase = s.take(TT, 3, EXPERTS)
    extra_f = s.take(EXTRA + 1)
    extra_i = s.take(EXTRA + 1).bitcast(I32)
    scale_b = xg
    shift_b = y
    gate_b = s.take(D)

    G, U, X0, X1, S0, S1, Y0, Y1 = s.psum
    iota = s.c("iota")
    q = f"{layer}_"
    wg_in = [[s.sem(f"{q}wg_in{a}{b}") for b in range(2)] for a in range(2)]
    wu_in = [s.sem(f"{q}wu_in{b}") for b in range(2)]
    wd_in = [s.sem(f"{q}wd_in{b}") for b in range(2)]
    rows_in, router_in, gate_in = s.sem(q + "rows_in"), s.sem(q + "router_in"), s.sem(q + "gate_in")
    squares_done, root_done, hx_ready = s.sem(q + "squares"), s.sem(q + "root"), s.sem(q + "hx")
    hxT_done, hxT_ready, logits_done = s.sem(q + "hxT_done"), s.sem(q + "hxT_ready"), s.sem(q + "logits")
    shifted, exps_done = s.sem(q + "shifted"), s.sem(q + "exps")
    member_ready, rank_done, extra_ready = s.sem(q + "member"), s.sem(q + "rank"), s.sem(q + "extra")
    sel_ready, gath_done, xg_ready = s.sem(q + "sel"), s.sem(q + "gath"), s.sem(q + "xg")
    xgT_done, xT_ready = s.sem(q + "xgT"), s.sem(q + "xT")
    gate_done, up_done, down_done = s.sem(q + "gate"), s.sem(q + "up"), s.sem(q + "down")
    silu_ready, h_ready, hT_done, hT_ready = s.sem(q + "silu"), s.sem(q + "h"), s.sem(q + "hTd"), s.sem(q + "hT")
    y_ready, scat_done, acc_done = s.sem(q + "y"), s.sem(q + "scat"), s.sem(q + "acc")
    all_added = s.sem(q + "all_added")
    w_gate = ins["moe_w_gate"].rearrange("l e (p t) n -> l e p (t n)", t=KT)
    w_up = ins["moe_w_up"].rearrange("l e (p t) n -> l e p (t n)", t=KT)
    w_down = ins["moe_w_down"].rearrange("l e (p t) n -> l e p (t n)", t=HK)

    def flat(v):
        return v.rearrange("p a b -> p (a b)")

    def mod_row(i, k):
        return mods[layer, i, k * D:(k + 1) * D].partition_broadcast(P)

    with nc.Block(name=f"experts{layer}", no_gpsimd_drain=True) as block:

        @block.sync
        def _(sp):
            sp.dma_start(scale_b, mod_row(0, 4)).then_inc(rows_in, 16)
            sp.dma_start(shift_b, mod_row(0, 3)).then_inc(rows_in, 16)
            sp.dma_start(acc[:, 0, :], ins["norm_g"][layer, 1].partition_broadcast(P)).then_inc(rows_in, 16)
            sp.dma_start(router, ins["moe_router"][layer].rearrange("(p t) n -> p t n", t=KT)).then_inc(router_in, 16)
            sp.dma_start(router_b, ins["moe_router_b"][layer].partition_broadcast(P)).then_inc(router_in, 16)

            def load(dst, src, e, sem):
                sp.dma_start(flat(dst), src[layer, e]).then_inc(sem, 16)

            for j in range(2):
                load(wg[0][j], w_gate, j, wg_in[0][j])
            for j in range(2):
                load(wu[j], w_up, j, wu_in[j])
            for j in range(2):
                load(wd[j], w_down, j, wd_in[j])
            for j in range(2):
                load(wg[1][j], w_gate, 2 + j, wg_in[1][j])

            sp.dma_start(gate_b, mod_row(0, 5)).then_inc(gate_in, 16)

            def after(i, par):
                sp.wait_ge(gate_done, i + 1)
                for j in range(2):
                    load(wg[par][j], w_gate, i * 2 + (4 + j), wg_in[par][j])
                sp.wait_ge(up_done, i + 1)
                for j in range(2):
                    load(wu[j], w_up, i * 2 + (2 + j), wu_in[j])
                sp.wait_ge(down_done, i + 1)
                for j in range(2):
                    load(wd[j], w_down, i * 2 + (2 + j), wd_in[j])

            with sp.Fori(0, PAIRS // 2 - 1) as n:
                after(n * 2, 0)
                after(n * 2 + 1, 1)
            i = PAIRS - 2
            sp.wait_ge(up_done, i + 1)
            for j in range(2):
                load(wu[j], w_up, 2 * i + 2 + j, wu_in[j])
            sp.wait_ge(down_done, i + 1)
            for j in range(2):
                load(wd[j], w_down, 2 * i + 2 + j, wd_in[j])
            sp.wait_ge(extra_ready, 1)
            n_extra = sp.value_load(extra_i[0:1, EXTRA:EXTRA + 1], min_val=0, max_val=EXTRA)
            with sp.Fori(0, EXTRA // 2) as m:
                with sp.If(n_extra > m * 2):
                    sp.wait_ge(acc_done, 4 * PAIRS + 2 + m * 4)
                    for j in range(2):
                        e = sp.value_load(extra_i[0:1, bass.ds(m * 2 + j, 1)], min_val=0, max_val=EXPERTS - 1)
                        load(wg[0][j], w_gate, e, wg_in[0][j])
                        load(wu[j], w_up, e, wu_in[j])
                        load(wd[j], w_down, e, wd_in[j])

        def gather(pe, i, par):
            pe.wait_ge(sel_ready, i + 1)
            for half, bank in enumerate((X0, X1)):
                for t in range(TT):
                    mm = pe.matmul(bank[:, :], sel[par][:, t].rearrange("p a b -> p (a b)"),
                                   hx[:, t, half * 512:(half + 1) * 512], start=(t == 0), stop=(t == TT - 1))
            mm.then_inc(gath_done, 1)

        def turn_gathered(pe, i):
            pe.wait_ge(xg_ready, i + 1)
            for t in range(KT):
                mm = pe.transpose((X0, X1)[t // 4][:, t % 4 * P:(t % 4 + 1) * P], xg[:, t::KT], s.c("ident"))
            mm.then_inc(xgT_done, 1)

        def gate_product(pe, i, par, uses):
            pe.wait_ge(xT_ready, i + 1)
            for j in range(2):
                pe.wait_ge(wg_in[par][j], uses * 16)
            for t in range(KT):
                for j in range(2):
                    mm = pe.matmul(G[j * CAP:(j + 1) * CAP, :], xT[:, t, j * CAP:(j + 1) * CAP], wg[par][j][:, t],
                                   start=(t == 0), stop=(t == KT - 1))
            mm.then_inc(gate_done, 1)

        def up_product(pe, i):
            for j in range(2):
                pe.wait_ge(wu_in[j], (i + 1) * 16)
            for t in range(KT):
                for j in range(2):
                    mm = pe.matmul(U[j * CAP:(j + 1) * CAP, :], xT[:, t, j * CAP:(j + 1) * CAP], wu[j][:, t],
                                   start=(t == 0), stop=(t == KT - 1))
            mm.then_inc(up_done, 1)

        def turn_hidden(pe, i, par):
            pe.wait_ge(h_ready, i + 1)
            for t in range(HK):
                pe.transpose(G[:, t * P:(t + 1) * P], h[:, t::HK], s.c("ident"))
            for t in range(TT):
                mm = pe.transpose(U[:, t * P:(t + 1) * P], selw[par][:, t].rearrange("p a b -> p (a b)"), s.c("ident"))
            mm.then_inc(hT_done, 1)

        def down_product(pe, i):
            pe.wait_ge(hT_ready, i + 1)
            for j in range(2):
                pe.wait_ge(wd_in[j], (i + 1) * 16)
            for half, bank in enumerate((Y0, Y1)):
                for t in range(HK):
                    for j in range(2):
                        mm = pe.matmul(bank[j * CAP:(j + 1) * CAP, :], hT[:, t, j * CAP:(j + 1) * CAP],
                                       wd[j][:, t, half * 512:(half + 1) * 512], start=(t == 0), stop=(t == HK - 1))
            mm.then_inc(down_done, 1)

        def scatter(pe, i):
            pe.wait_ge(y_ready, i + 1)
            for k in range(4):
                pe.wait_ge(acc_done, i * 4 + (k + 1))
                pe.matmul((S0, S1)[k % 2][:, :], selwT[:, k // 2], y[:, k % 2 * 512:(k % 2 + 1) * 512],
                          start=True, stop=True).then_inc(scat_done, 1)

        @block.tensor
        def _(pe):
            for t in range(TT):
                pe.wait_ge(hx_ready, t + 1)
                if t:
                    pe.wait_ge(hxT_ready, t)
                for k in range(KT):
                    mm = pe.transpose((X0, X1)[k // 4][:, k % 4 * P:(k % 4 + 1) * P], hx[:, t, k::KT], s.c("ident"))
                mm.then_inc(hxT_done, 1)
                pe.wait_ge(hxT_ready, t + 1)
                pe.wait_ge(router_in, 32)
                for k in range(KT):
                    mm = pe.matmul(S0[:, t * 64:t * 64 + GROUPS + EXPERTS], xT[:, k], router[:, k],
                                   start=(k == 0), stop=(k == KT - 1))
                mm.then_inc(logits_done, 1)
            pe.wait_ge(member_ready, 1)
            pe.matmul(S1[:, 0:EXPERTS], s.c("before"), member[:, 0], start=True, stop=True)
            for t in range(TT):
                mm = pe.matmul(S1[:, EXPERTS:2 * EXPERTS], s.c("ones" if t == 0 else "before"), member[:, t],
                               start=(t == 0), stop=(t == TT - 1))
            for t in range(TT):
                mm = pe.matmul(S1[:, 2 * EXPERTS:3 * EXPERTS], s.c("ones"), member[:, t],
                               start=(t == 0), stop=(t == TT - 1))
            mm.then_inc(rank_done, 1)

            gather(pe, 0, 0)
            turn_gathered(pe, 0)

            def pair(i, par, uses, first=False, last=False):
                gate_product(pe, i, par, uses)
                if not last:
                    gather(pe, i + 1, 1 - par)
                up_product(pe, i)
                if not last:
                    turn_gathered(pe, i + 1)
                if not first:
                    scatter(pe, i - 1)
                turn_hidden(pe, i, par)
                down_product(pe, i)

            pair(0, 0, 1, first=True)
            with pe.Fori(0, PAIRS // 2 - 1) as n:
                pair(n * 2 + 1, 1, n + 1)
                pair(n * 2 + 2, 0, n + 2)
            pair(PAIRS - 1, 1, PAIRS // 2, last=True)
            scatter(pe, PAIRS - 1)

            pe.wait_ge(extra_ready, 1)
            n_extra = pe.value_load(extra_i[0:1, EXTRA:EXTRA + 1], min_val=0, max_val=EXTRA)
            with pe.Fori(0, EXTRA // 2) as m:
                with pe.If(n_extra > m * 2):
                    i = m + PAIRS
                    gather(pe, i, 0)
                    turn_gathered(pe, i)
                    gate_product(pe, i, 0, m + (PAIRS // 2 + 1))
                    up_product(pe, i)
                    turn_hidden(pe, i, 0)
                    down_product(pe, i)
                    scatter(pe, i)

        def silu_gate(act, i):
            act.wait_ge(gate_done, i + 1)
            act.activation(sg, G[:, :], ACT.Silu).then_inc(silu_ready, 1)

        def copy_gathered(act, i):
            act.wait_ge(gath_done, i + 1)
            act.activation(xg[:, 0:512], X0[:, :], ACT.Copy)
            act.activation(xg[:, 512:D], X1[:, :], ACT.Copy).then_inc(xg_ready, 1)

        def copy_hidden(act, i):
            act.wait_ge(hT_done, i + 1)
            act.activation(flat(selwT), U[:, 0:TT * P], ACT.Copy)
            act.activation(flat(hT), G[:, :], ACT.Copy).then_inc(hT_ready, 1)

        def copy_rows(act, i):
            act.wait_ge(down_done, i + 1)
            act.activation(y[:, 0:512], Y0[:, :], ACT.Copy)
            act.activation(y[:, 512:D], Y1[:, :], ACT.Copy).then_inc(y_ready, 1)

        @block.scalar
        def _(act):
            for t in range(TT):
                act.activation(acc[:, 1, :], s.x_res[:, t], ACT.Square, accum_out=small[:, t, 0:1])
                act.drain()
            act.sem_inc(squares_done, 1)
            act.wait_ge(root_done, 1)
            act.activation(small[:, :, 2:3], small[:, :, 1:2], ACT.Sqrt).then_inc(root_done, 1)
            act.wait_ge(shifted, 1)
            for t in range(TT):
                act.activation(glog[:, t, 4:8], glog[:, t, 0:4], ACT.Exp, bias=small[:, t, 3:4],
                               accum_out=small[:, t, 4:5])
            act.activation(small[:, :, 6:7], small[:, :, 5:6], ACT.Exp)
            act.drain()
            act.sem_inc(exps_done, 1)

            copy_gathered(act, 0)

            def pair(i, last=False):
                silu_gate(act, i)
                if not last:
                    copy_gathered(act, i + 1)
                copy_hidden(act, i)
                copy_rows(act, i)

            with act.Fori(0, PAIRS - 1) as i:
                pair(i)
            pair(PAIRS - 1, last=True)
            act.wait_ge(extra_ready, 1)
            n_extra = act.value_load(extra_i[0:1, EXTRA:EXTRA + 1], min_val=0, max_val=EXTRA)
            with act.Fori(0, EXTRA // 2) as m:
                with act.If(n_extra > m * 2):
                    i = m + PAIRS
                    copy_gathered(act, i)
                    silu_gate(act, i)
                    copy_hidden(act, i)
                    copy_rows(act, i)

        def select_slots(dve, i, par):
            two = slice(2 * i, 2 * i + 2) if isinstance(i, int) else bass.ds(i * 2, 2)
            at = slot_of[:, :, two].unsqueeze(3).to_broadcast([P, TT, 2, CAP])
            wt = weight_of[:, :, two].unsqueeze(3).to_broadcast([P, TT, 2, CAP])
            io = iota[:, 0:CAP].unsqueeze(1).unsqueeze(1).to_broadcast([P, TT, 2, CAP])
            dve.tensor_tensor(sel[par], io, at, ALU.is_equal)
            dve.drain()
            dve.tensor_tensor(selw[par], sel[par], wt, ALU.mult).then_inc(sel_ready, 1)

        def hidden_rows(dve, i):
            dve.wait_ge(silu_ready, i + 1)
            dve.wait_ge(up_done, i + 1)
            dve.tensor_tensor(h, U[:, :], sg, ALU.mult).then_inc(h_ready, 1)

        def copy_turned(dve, i):
            dve.wait_ge(xgT_done, i + 1)
            dve.tensor_copy(xT[:, 0:4].rearrange("p a b -> p (a b)"), X0[:, :])
            dve.tensor_copy(xT[:, 4:8].rearrange("p a b -> p (a b)"), X1[:, :]).then_inc(xT_ready, 1)

        def add_up(dve, i):
            for k in range(4):
                dve.wait_ge(scat_done, i * 4 + (k + 1))
                part = acc[:, k // 2, k % 2 * 512:(k % 2 + 1) * 512]
                dve.tensor_tensor(part, (S0, S1)[k % 2][:, :], part, ALU.add).then_inc(acc_done, 1)

        @block.vector
        def _(dve):
            dve.wait_ge(rows_in, 48)
            dve.tensor_scalar(scale_b, scale_b, 1.0, None, ALU.add)
            dve.drain()
            dve.tensor_tensor(scale_b, scale_b, acc[:, 0, :], ALU.mult)
            dve.wait_ge(squares_done, 1)
            dve.tensor_scalar(small[:, :, 1:2], small[:, :, 0:1], 1.0 / D, NORM_EPS, ALU.mult, ALU.add).then_inc(root_done, 1)
            dve.wait_ge(root_done, 2)
            dve.reciprocal(small[:, :, 2:3], small[:, :, 2:3])
            dve.drain()
            for t in range(TT):
                dve.scalar_tensor_tensor(hx[:, t], s.x_res[:, t], small[:, t, 2:3], scale_b, ALU.mult, ALU.mult)
                dve.drain()
                dve.tensor_tensor(hx[:, t], hx[:, t], shift_b, ALU.add).then_inc(hx_ready, 1)
            for t in range(TT):
                dve.wait_ge(hxT_done, t + 1)
                if t:
                    dve.wait_ge(logits_done, t)
                dve.tensor_copy(xT[:, 0:4].rearrange("p a b -> p (a b)"), X0[:, :])
                dve.tensor_copy(xT[:, 4:8].rearrange("p a b -> p (a b)"), X1[:, :]).then_inc(hxT_ready, 1)
            dve.memset(acc, 0.0)
            dve.wait_ge(logits_done, TT)
            NL = GROUPS + EXPERTS
            for t in range(TT):
                dve.tensor_tensor(logit[:, t], S0[:, t * 64:t * 64 + NL], router_b, ALU.add)
            dve.memset(glog, -3.0e38)
            dve.drain()
            dve.tensor_copy(glog[:, :, 0:4], logit[:, :, 0:4])
            dve.drain()
            for t in range(TT):
                dve.max(top[:, t], glog[:, t])
            dve.drain()
            for t in range(TT):
                dve.max_index(topi[:, t], top[:, t], glog[:, t])
            dve.drain()
            dve.tensor_scalar(small[:, :, 3:4], top[:, :, 0:1], -1.0, None, ALU.mult)
            dve.tensor_copy(small[:, :, 8:9], topi[:, :, 0:1])
            dve.drain()
            of_group = iota[:, 0:GROUPS].unsqueeze(1).to_broadcast([P, TT, GROUPS])
            dve.tensor_tensor(tmp[:, :, 0:GROUPS], of_group, small[:, :, 8:9].to_broadcast([P, TT, GROUPS]), ALU.is_equal)
            dve.drain()
            for t in range(TT):
                dve.tensor_tensor(tmp2[:, t].rearrange("p (e g) -> p g e", g=GROUPS),
                                  logit[:, t, GROUPS:].rearrange("p (g e) -> p g e", g=GROUPS),
                                  tmp[:, t, 0:GROUPS].unsqueeze(2).to_broadcast([P, GROUPS, PER_GROUP]), ALU.mult)
            dve.drain()
            for t in range(TT):
                dve.tensor_reduce(member[:, t, 0:PER_GROUP], tmp2[:, t].rearrange("p (e g) -> p e g", g=GROUPS), AX.X, ALU.add)
            dve.drain()
            for t in range(TT):
                dve.max(top[:, t], member[:, t, 0:PER_GROUP])
            dve.drain()
            for t in range(TT):
                dve.max_index(topi[:, t], top[:, t], member[:, t, 0:PER_GROUP])
            dve.tensor_tensor(small[:, :, 5:6], top[:, :, 1:2], top[:, :, 0:1], ALU.subtract)
            dve.drain()
            dve.sem_inc(shifted, 1)
            dve.tensor_copy(small[:, :, 9:11], topi[:, :, 0:2])
            dve.drain()
            dve.tensor_scalar(small[:, :, 8:9], small[:, :, 8:9], float(PER_GROUP), None, ALU.mult)
            dve.drain()
            dve.tensor_tensor(small[:, :, 9:11], small[:, :, 9:11], small[:, :, 8:9].to_broadcast([P, TT, 2]), ALU.add)
            dve.drain()
            dve.wait_ge(exps_done, 1)
            dve.tensor_scalar(small[:, :, 11:12], small[:, :, 6:7], 1.0, None, ALU.add)
            dve.drain()
            dve.tensor_tensor(small[:, :, 11:12], small[:, :, 11:12], small[:, :, 4:5], ALU.mult)
            dve.drain()
            dve.reciprocal(small[:, :, 12:13], small[:, :, 11:12])
            dve.drain()
            dve.tensor_tensor(small[:, :, 13:14], small[:, :, 12:13], small[:, :, 6:7], ALU.mult)
            dve.drain()
            of_expert = iota[:, 0:EXPERTS].unsqueeze(1).to_broadcast([P, TT, EXPERTS])
            dve.tensor_tensor(tmp, of_expert, small[:, :, 9:10].to_broadcast([P, TT, EXPERTS]), ALU.is_equal)
            dve.tensor_tensor(tmp2, of_expert, small[:, :, 10:11].to_broadcast([P, TT, EXPERTS]), ALU.is_equal)
            dve.drain()
            dve.tensor_tensor(member, tmp, tmp2, ALU.add).then_inc(member_ready, 1)
            dve.tensor_tensor(tmp, tmp, small[:, :, 12:13].to_broadcast([P, TT, EXPERTS]), ALU.mult)
            dve.tensor_tensor(tmp2, tmp2, small[:, :, 13:14].to_broadcast([P, TT, EXPERTS]), ALU.mult)
            dve.drain()
            dve.tensor_tensor(weight_of[:, :, 0:EXPERTS], tmp, tmp2, ALU.add)
            dve.wait_ge(rank_done, 1)
            dve.drain()
            dve.scalar_tensor_tensor(slot_of[:, :, 0:EXPERTS], S1[:, 0:2 * EXPERTS].rearrange("p (t e) -> p t e", t=TT),
                                     1.0, member, ALU.add, ALU.mult)
            dve.tensor_copy(cnt, S1[:, 2 * EXPERTS:3 * EXPERTS])
            dve.drain()
            dve.tensor_scalar(slot_of[:, :, 0:EXPERTS], slot_of[:, :, 0:EXPERTS], -1.0, None, ALU.add)
            dve.drain()
            select_slots(dve, 0, 0)
            dve.sem_inc(acc_done, 2)
            flags = flat(flag)

            def find_extras():
                for b in range(3):
                    dve.tensor_scalar(flag[:, b], cnt, float(CAP * (b + 1)), None, ALU.is_gt)
                    dve.tensor_scalar(base[:, :, b], slot_of[:, :, 0:EXPERTS], float(1 - CAP * (b + 1)), None, ALU.add)
                    dve.tensor_copy(wbase[:, :, b], weight_of[:, :, 0:EXPERTS])
                    dve.tensor_copy(num[:, b], iota[:, 0:EXPERTS])
                dve.drain()
                dve.tensor_tensor_scan(order, s.c("ones", 3 * EXPERTS), flags, 0.0, ALU.mult, ALU.add)
                dve.drain()

            def take_extras(ks):
                for k in ks:
                    dve.scalar_tensor_tensor(pick, order, float(k + 1), flags, ALU.is_equal, ALU.mult)
                    dve.drain()
                    for src, out in [(flat(num), extra_f[:, k:k + 1])] + [
                            (v[:, t].rearrange("p a b -> p (a b)"), o[:, t, EXPERTS + k:EXPERTS + k + 1])
                            for v, o in ((base, slot_of), (wbase, weight_of)) for t in range(TT)]:
                        dve.tensor_tensor(prod, pick, src, ALU.mult)
                        dve.drain()
                        dve.tensor_reduce(out, prod, AX.X, ALU.add)
                        dve.drain()

            def count_extras():
                dve.tensor_scalar(slot_of[:, :, EXPERTS:NE], slot_of[:, :, EXPERTS:NE], -1.0, None, ALU.add)
                dve.tensor_copy(extra_f[:, EXTRA:EXTRA + 1], order[:, 3 * EXPERTS - 1:3 * EXPERTS])
                dve.drain()
                dve.tensor_copy(extra_i, extra_f).then_inc(extra_ready, 1)

            find_extras()
            take_extras(range(0, 2))

            copy_turned(dve, 0)

            def pair(i, par, first=False, last=False):
                if not first:
                    dve.wait_ge(hT_done, i)
                if not last:
                    select_slots(dve, i + 1, 1 - par)
                if first:
                    take_extras(range(2, 6))
                hidden_rows(dve, i)
                if not last:
                    copy_turned(dve, i + 1)
                if not first:
                    add_up(dve, i - 1)

            pair(0, 0, first=True)
            take_extras(range(6, EXTRA))
            count_extras()
            with dve.Fori(0, PAIRS // 2 - 1) as n:
                pair(n * 2 + 1, 1)
                pair(n * 2 + 2, 0)
            pair(PAIRS - 1, 1, last=True)
            add_up(dve, PAIRS - 1)
            n_extra = dve.value_load(extra_i[0:1, EXTRA:EXTRA + 1], min_val=0, max_val=EXTRA)
            with dve.Fori(0, EXTRA // 2) as m:
                with dve.If(n_extra > m * 2):
                    i = m + PAIRS
                    dve.wait_ge(hT_done, i)
                    select_slots(dve, i, 0)
                    copy_turned(dve, i)
                    hidden_rows(dve, i)
                    add_up(dve, i)
            dve.drain()
            dve.sem_inc(all_added, 1)
            dve.wait_ge(gate_in, 16)
            dve.tensor_tensor(acc[:, 0], acc[:, 0], gate_b, ALU.mult)
            dve.drain()
            dve.tensor_tensor(s.x_res[:, 0], s.x_res[:, 0], acc[:, 0], ALU.add)

        @block.gpsimd
        def _(pool):
            pool.wait_ge(gate_in, 16)
            pool.wait_ge(all_added, 1)
            pool.tensor_tensor(acc[:, 1], acc[:, 1], gate_b, ALU.mult)
            pool.drain()
            pool.tensor_tensor(s.x_res[:, 1], s.x_res[:, 1], acc[:, 1], ALU.add)
            pool.drain()


EMB, BANDS, FH = 33, 16, 64
FREQ = L
TWO_PI = 2.0 * math.pi
TWO_PI_HI = 6.28125
TWO_PI_LO = TWO_PI - TWO_PI_HI
ROUND = 1.5 * 2.0 ** 23


def hyena_constants():
    t32 = np.linspace(0.0, 1.0, L, dtype=np.float32)
    w = (np.float32(2.0 * math.pi) * np.arange(L, dtype=np.float32) / np.float32(L))[:, None]
    f = np.linspace(1e-4, BANDS - 1, BANDS, dtype=np.float32)[None]
    z = np.zeros((P, L), np.float32)
    z[:EMB] = np.concatenate([t32[:, None], np.cos(f * w), -np.sin(f * w)], -1).T
    ang = np.arange(L)[:, None] * (np.arange(FREQ)[None] + 0.5) * (math.pi / FREQ)
    tiles = lambda m: m.reshape(2, P, -1).transpose(1, 0, 2).reshape(P, -1)
    cos, sin = np.cos(ang), np.sin(ang)
    minus_t = -t32.reshape(TT, P).T
    keep = (np.arange(L) > 0).astype(np.float32).reshape(TT, P).T
    mats = [tiles(cos), tiles(sin), tiles(cos.T), tiles(sin.T)]
    deltas = np.abs(np.linspace(math.log(1e-2) / 1.5, math.log(1e-2) / 0.3, D, dtype=np.float32))
    return np.concatenate([z, minus_t, keep] + mats, 1).astype(np.float32), deltas


HY_CONST, HY_DELTAS = hyena_constants()


def hyena_layer(s, ins, mods):
    nc = s.nc
    s.at = 0
    BLK = 3 * CH
    SLOTS = 2
    AHEAD = 4 * SLOTS
    win_ring = [s.take(KT, 512) for _ in range(SLOTS)]
    hc = s.take(HY_CONST.shape[1])
    zT = hc[:, 0:L]
    minus_t, keep = hc[:, L:L + TT], hc[:, L + TT:L + 2 * TT]
    o = L + 2 * TT
    fwd = [hc[:, o + n * 512:o + (n + 1) * 512].rearrange("p (i f) -> p i f", i=2) for n in range(2)]
    inv = [hc[:, o + (2 + n) * 512:o + (3 + n) * 512].rearrange("p (i f) -> p i f", i=2) for n in range(2)]
    khat = s.take(2, 2, 2, D)
    big = s.take(2, 2, 2, D)
    hsum, hdif = big[:, 0], big[:, 1]
    vhat, prod = big[:, 0], big[:, 1]
    f_w3 = s.take(2 * 2 * D)
    window = s.take(TT, D)
    hT = s.take(KT, L)
    vt = s.take(TT, D)
    tmp = s.take(2, D)
    u = s.take(BLK, L)
    up = [s.take(L + 2) for _ in range(2)]
    w1, wi = s.take(FH), s.take(2, FH)
    fv = s.take(4)
    hd = s.take(L)
    arg, turns = s.take(L), s.take(L)
    chv = s.take(P)
    skip = s.take(16)
    norm = s.take(16)
    sc, sh, ng = s.take(KT), s.take(KT), s.take(KT)
    stat = s.take(2)
    pos = s.take(L)
    rows, rows2 = up[0][:, 0:P], up[1][:, 0:P]
    gate, b_out = tmp[:, 0], tmp[:, 1]
    w_out = s.arena[:, 0:CH * D].rearrange("p (m n) -> p m n", m=CH)
    half_a, half_b = (f_w3[:, k * D:(k + 1) * D].rearrange("p (f n) -> p f n", f=2) for k in range(2))
    S = lambda n: s.sem("hy_" + n)
    hc_in, w_in, f3_in, win_in = S("hc_in"), S("w_in"), S("f3_in"), S("window_in")
    ring_in = [S(f"ring_in{k}") for k in range(SLOTS)]
    arg_done, hd_ready, f_done, win_ready = S("arg"), S("hd"), S("f"), S("win")
    taps_done, taps_ready, spec_done, spec_ready, abs_ready, abs_done = (S(n) for n in
        ("taps_done", "taps_ready", "spec_done", "spec_ready", "abs_ready", "abs_done"))
    mag_ready = S("mag_ready")

    vec_in, rows_in, chv_done = S("vec_in"), S("rows_in"), S("chv_done")
    sq_done, var_done, root_done, xn_ready, xnT_done, hT_ready, scale_ready = (S(n) for n in
        ("sq", "var", "root", "xn", "xnT", "hT", "scale"))
    in_done, up_ready, u_ready = S("in_done"), S("up_ready"), S("u_ready")
    wout_in, row_in = [S(f"wout_in{h}") for h in range(2)], S("row_in")
    TAPS = (3, 4, 5, 6)

    with nc.Block(name="hyena_inputs", no_gpsimd_drain=True) as block:

        @block.sync
        def _(sp):
            for n, v in enumerate((ins["hy_f_freq"][0], ins["hy_f_b1"][0], ins["hy_f_bi"][0, 0], ins["hy_f_bi"][0, 1])):
                sp.dma_start(fv[0:FH, n:n + 1], v.unsqueeze(1)).then_inc(w_in, 16)
            sp.dma_start(sc, mods[1, 0, D:2 * D].rearrange("(p t) -> p t", t=KT)).then_inc(vec_in, 16)
            sp.dma_start(sh, mods[1, 0, 0:D].rearrange("(p t) -> p t", t=KT)).then_inc(vec_in, 16)
            sp.dma_start(ng, ins["norm_g"][1, 0].rearrange("(p t) -> p t", t=KT)).then_inc(vec_in, 16)
            sp.dma_start(w1[0:EMB, :], ins["hy_f_w1"][0]).then_inc(w_in, 16)
            sp.dma_start(hc, ins["hy_const"]).then_inc(hc_in, 16)
            src = ins["hy_w_in"][0].rearrange("(p t) n -> p t n", t=KT)
            sp.dma_start(win_ring[0], src[:, :, 0:512]).then_inc(ring_in[0], 16)
            sp.dma_start(wi[0:FH], ins["hy_f_wi"][0].rearrange("n i o -> i n o")).then_inc(w_in, 16)
            vecs = [ins["hy_b_in"][0], ins["hy_conv_b"][0]] + [ins["hy_conv_w"][0, k] for k in range(3)]
            for n, v in enumerate(vecs):
                sp.dma_start(rows[n * BLK:(n + 1) * BLK, :], v.rearrange("(m p) -> m p", p=P)).then_inc(rows_in, 16)
            sp.dma_start(rows2[0:16, :], ins["hy_skip"][0].rearrange("o (m p) -> (o m) p", p=P)).then_inc(rows_in, 16)
            for i in range(TT):
                sp.dma_start(window[:, i], ins["hy_deltas"].partition_broadcast(P)).then_inc(win_in, 16)
            sp.dma_start(f_w3[0:FH, :], ins["hy_f_w3"][0]).then_inc(f3_in, 16)
            sp.dma_start(win_ring[1], src[:, :, 512:1024]).then_inc(ring_in[1], 16)
            for b in range(SLOTS, BLK // 4):
                sp.wait_ge(in_done, 4 * (b - SLOTS) + 4)
                sp.dma_start(win_ring[b % SLOTS], src[:, :, b * 512:(b + 1) * 512]).then_inc(ring_in[b % SLOTS], 16)

        @block.tensor
        def _(pe):
            def layer1():
                pe.wait_ge(hc_in, 16)
                pe.wait_ge(w_in, 96)
                pe.matmul(s.psum[2][0:FH, 0:L], w1[0:EMB, :], zT[0:EMB, :], start=True, stop=True).then_inc(f_done, 1)

            def inner_layer(n):
                pe.wait_ge(hd_ready, n + 1)
                pe.matmul(s.psum[2][0:FH, 0:L], wi[0:FH, n], hd[0:FH, :], start=True, stop=True).then_inc(f_done, 1)

            def taps(n):
                od, i, half = n // 4, n // 2 % 2, n % 2
                if n == 0:
                    pe.wait_ge(hd_ready, 3)
                    pe.wait_ge(f3_in, 16)
                if n >= 2:
                    pe.wait_ge(taps_ready, n - 1)
                for sign in range(2):
                    c = (od * 2 + sign) * D + half * 512
                    mm = pe.matmul(s.psum[TAPS[n % 2 * 2 + sign]][:, :], hd[0:FH, i * P:(i + 1) * P], f_w3[0:FH, c:c + 512],
                                   start=True, stop=True)
                mm.then_inc(taps_done, 1)

            def spectrum(n):
                od, part, ft, half = n // 8, n // 4 % 2, n // 2 % 2, n % 2
                if n == 0:
                    pe.wait_ge(taps_ready, 8)
                if n >= 4:
                    pe.wait_ge(spec_ready, n - 3)
                src = (hsum, hdif)[part]
                for i in range(TT):
                    mm = pe.matmul(s.psum[TAPS[n % 4]][:, :], fwd[part][:, i, ft * P:(ft + 1) * P],
                                   src[:, od, i, half * 512:(half + 1) * 512], start=(i == 0), stop=(i == TT - 1))
                mm.then_inc(spec_done, 1)

            def magnitudes():
                pe.wait_ge(abs_ready, 1)
                for od in range(2):
                    for m in range(CH):
                        for i in range(TT):
                            mm = pe.matmul(s.psum[7][:, od * CH + m:od * CH + m + 1], hsum[:, od, i, m * P:(m + 1) * P],
                                           s.c("ones")[:, 0:1], start=(i == 0), stop=(i == TT - 1))
                mm.then_inc(abs_done, 1)

            def in_block(l, k, q):
                if q == 0:
                    pe.wait_ge(ring_in[k], l * 16 + 16)
                n = l * AHEAD + (4 * k + q)
                pe.wait_ge(up_ready, n + 1)
                for t in range(KT):
                    mm = pe.matmul(s.psum[q % 2][:, 0:L], win_ring[k][:, t, q * P:(q + 1) * P], hT[:, t],
                                   start=(t == 0), stop=(t == KT - 1))
                mm.then_inc(in_done, 1)

            pe.wait_ge(xn_ready, TT)
            for t in range(KT):
                for i in range(TT):
                    mm = pe.transpose(s.psum[t][:, i * P:(i + 1) * P], vt[:, i, t::KT], s.c("ident"))
                mm.then_inc(xnT_done, 1)
            pe.wait_ge(hT_ready, KT)
            layer1()
            pe.wait_ge(rows_in, 96)
            pe.transpose(s.psum[7][:, 0:5 * BLK], rows[0:5 * BLK, :], s.c("ident")[0:5 * BLK, 0:5 * BLK])
            pe.transpose(s.psum[7][:, 128:144], rows2[0:16, :], s.c("ident")[0:16, 0:16]).then_inc(chv_done, 1)
            for n in range(AHEAD):
                in_block(0, n // 4, n % 4)
                if n < 2:
                    inner_layer(n)
                else:
                    taps(n - 2)
            taps(AHEAD - 2)
            taps(AHEAD - 1)
            for n in range(16):
                spectrum(n)
            with pe.Fori(0, BLK // AHEAD - 1) as l:
                for k in range(SLOTS):
                    for q in range(4):
                        in_block(l + 1, k, q)
            magnitudes()

        @block.scalar
        def _(act):
            def sine(n):
                act.wait_ge(arg_done, n + 1)
                act.activation(hd[0:FH, :], arg[0:FH, :], ACT.Sin).then_inc(hd_ready, 1)

            def biased(n, q):
                act.wait_ge(in_done, n + 1)
                act.wait_ge(u_ready, n + 1)
                bias = chv[:, n:n + 1] if isinstance(n, int) else chv[:, bass.ds(n, 1)]
                act.activation(up[q][:, 1:L + 1], s.psum[q][:, 0:L], ACT.Identity, bias=bias).then_inc(up_ready, 1)

            for i in range(TT):
                act.activation(tmp[:, 0], s.x_res[:, i], ACT.Square, accum_out=stat[:, i:i + 1])
                act.drain()
            act.sem_inc(sq_done, 1)
            act.wait_ge(var_done, 1)
            act.activation(stat, stat, ACT.Sqrt).then_inc(root_done, 1)
            act.wait_ge(scale_ready, 1)
            for t in range(KT):
                act.wait_ge(xnT_done, t + 1)
                act.activation(hT[:, t], s.psum[t][:, 0:L], ACT.Identity, bias=sh[:, t:t + 1], scale=sc[:, t:t + 1]).then_inc(hT_ready, 1)
            act.sem_inc(up_ready, 2)
            sine(0)
            biased(0, 0)
            sine(1)
            biased(1, 1)
            sine(2)
            act.wait_ge(win_in, 32)
            for i in range(TT):
                act.activation(window[:, i], window[:, i], ACT.Exp, scale=minus_t[:, i:i + 1]).then_inc(win_ready, 1)
            for n in range(2, AHEAD):
                biased(n, n % 2)
            for n in range(16):
                act.wait_ge(spec_done, n + 1)
                od, part, ft, half = n // 8, n // 4 % 2, n // 2 % 2, n % 2
                act.activation(khat[:, od, part, ft, half * 512:(half + 1) * 512], s.psum[TAPS[n % 4]][:, :], ACT.Copy).then_inc(spec_ready, 1)
                if n == 11:
                    act.activation(hsum, hsum, ACT.Abs)
            act.activation(hdif, hdif, ACT.Abs).then_inc(mag_ready, 1)
            with act.Fori(0, (BLK - AHEAD) // 2) as g:
                for q in range(2):
                    biased(g * 2 + (AHEAD + q), q)

        @block.vector
        def _(dve):
            def argument(n):
                dve.wait_ge(f_done, n + 1)
                x, k = arg[0:FH, :], turns[0:FH, :]
                dve.tensor_scalar(x, s.psum[2][0:FH, 0:L], fv[0:FH, n + 1:n + 2], fv[0:FH, 0:1], ALU.add, ALU.mult)
                dve.drain()
                dve.tensor_scalar(k, x, 1.0 / TWO_PI, ROUND, ALU.mult, ALU.add)
                dve.drain()
                dve.tensor_scalar(k, k, -ROUND, None, ALU.add)
                dve.drain()
                dve.scalar_tensor_tensor(x, k, -TWO_PI_HI, x, ALU.mult, ALU.add)
                dve.drain()
                dve.scalar_tensor_tensor(x, k, -TWO_PI_LO, x, ALU.mult, ALU.add)
                dve.drain()
                dve.tensor_scalar(x, x, math.pi, -math.pi, ALU.min, ALU.max).then_inc(arg_done, 1)

            def convolve(n, q):
                dve.wait_ge(up_ready, n + 3)
                if isinstance(n, int):
                    at = lambda k: chv[:, n + k * BLK:n + k * BLK + 1]
                    dst = u[:, n]
                else:
                    at = lambda k: chv[:, bass.ds(n + k * BLK, 1)]
                    dst = u[:, bass.ds(n, 1)].rearrange("p o c -> p (o c)")
                dve.tensor_scalar(pos, up[q][:, 0:L], at(2), at(1), ALU.mult, ALU.add)
                dve.drain()
                dve.scalar_tensor_tensor(pos, up[q][:, 1:L + 1], at(3), pos, ALU.mult, ALU.add)
                dve.drain()
                dve.scalar_tensor_tensor(dst, up[q][:, 2:L + 2], at(4), pos, ALU.mult, ALU.add)
                dve.drain()
                dve.sem_inc(u_ready, 1)

            def windowed(n):
                od, i, half = n // 4, n // 2 % 2, n % 2
                c = slice(half * 512, (half + 1) * 512)
                if n == 0:
                    dve.wait_ge(win_ready, TT)
                dve.wait_ge(taps_done, n + 1)
                a, b = (s.psum[TAPS[n % 2 * 2 + sign]] for sign in range(2))
                h0, h1 = tmp[:, 1, 0:512], tmp[:, 1, 512:1024]
                dve.tensor_tensor(h0, a[:, :], window[:, i, c], ALU.mult)
                dve.scalar_tensor_tensor(h1, b[:, :], keep[:, i:i + 1], window[:, i, c], ALU.mult, ALU.mult)
                dve.drain()
                dve.tensor_tensor(hsum[:, od, i, c], h0, h1, ALU.add)
                dve.tensor_tensor(hdif[:, od, i, c], h0, h1, ALU.subtract)
                dve.drain()
                dve.sem_inc(taps_ready, 1)

            dve.wait_ge(sq_done, 1)
            dve.tensor_scalar(stat, stat, 1.0 / D, NORM_EPS, ALU.mult, ALU.add).then_inc(var_done, 1)
            dve.wait_ge(root_done, 1)
            dve.reciprocal(stat, stat)
            dve.drain()
            for i in range(TT):
                dve.tensor_scalar(vt[:, i], s.x_res[:, i], stat[:, i:i + 1], None, ALU.mult).then_inc(xn_ready, 1)
            dve.wait_ge(vec_in, 48)
            dve.tensor_scalar(sc, sc, 1.0, None, ALU.add)
            dve.drain()
            dve.tensor_tensor(sc, sc, ng, ALU.mult).then_inc(scale_ready, 1)
            dve.wait_ge(chv_done, 1)
            dve.tensor_copy(chv[:, 0:5 * BLK], s.psum[7][:, 0:5 * BLK])
            dve.tensor_copy(skip, s.psum[7][:, 128:144])
            for k in range(2):
                dve.memset(up[k][:, 0:1], 0.0)
                dve.memset(up[k][:, L + 1:L + 2], 0.0)
            dve.drain()
            dve.sem_inc(u_ready, 2)
            argument(0)
            for n in range(AHEAD):
                convolve(n, n % 2)
                if n < 2:
                    argument(n + 1)
                else:
                    windowed(n - 2)
            windowed(AHEAD - 2)
            windowed(AHEAD - 1)
            dve.wait_ge(mag_ready, 1)
            for od in range(2):
                dve.tensor_tensor(hsum[:, od], hsum[:, od], hdif[:, od], ALU.max)
            dve.drain()
            dve.sem_inc(abs_ready, 1)
            with dve.Fori(0, (BLK - AHEAD) // 2) as g:
                for q in range(2):
                    convolve(g * 2 + (AHEAD + q), q)
            dve.wait_ge(abs_done, 1)
            dve.reciprocal(norm, s.psum[7][:, 0:16])
            dve.drain()
            dve.tensor_scalar(norm, norm, 1.0 / FREQ, None, ALU.mult)

    vT_done, vt_ready, dft_done, vhat_ready, real_ready, imag_ready, y_done, y_ready = (S(n) for n in
        ("vT_done", "vt_ready", "dft_done", "vhat_ready", "real_ready", "imag_ready", "y_done", "y_ready"))
    o_done = S("o_done")
    with nc.Block(name="hyena_convolutions", no_gpsimd_drain=True) as block:

        @block.sync
        def _(sp):
            src = ins["hy_w_out"][0].rearrange("(m p) n -> p m n", p=P)
            for h in range(2):
                sp.dma_start(w_out[:, 4 * h:4 * h + 4], src[:, 4 * h:4 * h + 4]).then_inc(wout_in[h], 16)
            sp.dma_start(gate, mods[1, 0, 2 * D:3 * D].partition_broadcast(P)).then_inc(row_in, 16)
            sp.dma_start(b_out, ins["hy_b_out"][0].partition_broadcast(P)).then_inc(row_in, 16)

        @block.tensor
        def _(pe):
            for od in range(2):
                for half in range(2):
                    if od:
                        pe.wait_ge(y_ready, 4 * half + 4)
                    for i in range(TT):
                        for m in range(4 * half, 4 * half + 4):
                            mm = pe.transpose(s.psum[half * 2 + i][:, m % 4 * P:(m % 4 + 1) * P], u[:, m, i * P:(i + 1) * P], s.c("ident"))
                        mm.then_inc(vT_done, 1)
                    pe.wait_ge(vt_ready, od * 4 + 2 * half + 2)
                    for n in range(4):
                        part, ft = n // 2, n % 2
                        if od or half:
                            pe.wait_ge(vhat_ready, (od * 2 + half) * 4 + n - 3)
                        for i in range(TT):
                            mm = pe.matmul(s.psum[4 + n][:, :], fwd[part][:, i, ft * P:(ft + 1) * P],
                                           vt[:, i, half * 512:(half + 1) * 512], start=(i == 0), stop=(i == TT - 1))
                        mm.then_inc(dft_done, 1)
                for m in range(CH):
                    if m % 4 == 0:
                        pe.wait_ge(real_ready, od * 2 + m // 4 + 1)
                        pe.wait_ge(imag_ready, od * 2 + m // 4 + 1)
                    k = 0
                    for part in range(2):
                        for ft in range(2):
                            mm = pe.matmul(s.psum[m // 2][:, m % 2 * L:(m % 2 + 1) * L], prod[:, part, ft, m * P:(m + 1) * P], inv[part][:, ft],
                                           start=(k == 0), stop=(k == 3))
                            k += 1
                    if m % 2:
                        mm.then_inc(y_done, 1)
            pe.wait_ge(vhat_ready, 16)
            for m in range(CH):
                pe.wait_ge(y_ready, 9 + m)
                if m % 4 == 0:
                    pe.wait_ge(wout_in[m // 4], 16)
                for i in range(TT):
                    for h in range(2):
                        mm = pe.matmul(s.psum[4 + i * 2 + h][:, :], u[:, m, i * P:(i + 1) * P], w_out[:, m, h * 512:(h + 1) * 512],
                                       start=(m == 0), stop=(m == CH - 1))
                        if m == CH - 1:
                            mm.then_inc(o_done, 1)

        @block.scalar
        def _(act):
            for od in range(2):
                for half in range(2):
                    c = slice(half * 512, (half + 1) * 512)
                    for i in range(TT):
                        act.wait_ge(vT_done, od * 4 + half * 2 + i + 1)
                        act.activation(vt[:, i, c], s.psum[half * 2 + i][:, :], ACT.Copy).then_inc(vt_ready, 1)
                    for n in range(4):
                        part, ft = n // 2, n % 2
                        act.wait_ge(dft_done, (od * 2 + half) * 4 + n + 1)
                        act.activation(vhat[:, part, ft, c], s.psum[4 + n][:, :], ACT.Copy).then_inc(vhat_ready, 1)

        @block.gpsimd
        def _(pool):
            for od in range(2):
                for half in range(2):
                    c = slice(half * 512, (half + 1) * 512)
                    pool.wait_ge(vhat_ready, (od * 2 + half) * 4 + 4)
                    pool.tensor_tensor(prod[:, 1, :, c], vhat[:, 0, :, c], khat[:, od, 1, :, c], ALU.mult)
                    pool.tensor_tensor(half_b, vhat[:, 1, :, c], khat[:, od, 0, :, c], ALU.mult)
                    pool.drain()
                    pool.tensor_tensor(prod[:, 1, :, c], prod[:, 1, :, c], half_b, ALU.add).then_inc(imag_ready, 1)
                    pool.drain()

        @block.vector
        def _(dve):
            for od in range(2):
                for half in range(2):
                    c = slice(half * 512, (half + 1) * 512)
                    dve.wait_ge(vhat_ready, (od * 2 + half) * 4 + 4)
                    dve.tensor_tensor(prod[:, 0, :, c], vhat[:, 0, :, c], khat[:, od, 0, :, c], ALU.mult)
                    dve.tensor_tensor(half_a, vhat[:, 1, :, c], khat[:, od, 1, :, c], ALU.mult)
                    dve.drain()
                    dve.tensor_tensor(prod[:, 0, :, c], prod[:, 0, :, c], half_a, ALU.subtract).then_inc(real_ready, 1)
                    dve.drain()
                for m in range(CH):
                    dve.wait_ge(y_done, od * 4 + m // 2 + 1)
                    dve.tensor_scalar(u[:, m], u[:, m], skip[:, od * CH + m:od * CH + m + 1], None, ALU.mult)
                    dve.drain()
                    dve.scalar_tensor_tensor(u[:, m], s.psum[m // 2][:, m % 2 * L:(m % 2 + 1) * L], norm[:, od * CH + m:od * CH + m + 1], u[:, m], ALU.mult, ALU.add)
                    dve.drain()
                    dve.tensor_tensor(u[:, m], u[:, m], u[:, (1 + od) * CH + m], ALU.mult).then_inc(y_ready, 1)
            dve.wait_ge(row_in, 32)
            out = khat.rearrange("p a b c d -> p (a b c d)")
            for i in range(TT):
                for h in range(2):
                    k = i * 2 + h
                    c = slice(h * 512, (h + 1) * 512)
                    part = out[:, k * 512:(k + 1) * 512]
                    dve.wait_ge(o_done, k + 1)
                    dve.tensor_tensor(part, s.psum[4 + k][:, :], b_out[:, c], ALU.add)
                    dve.drain()
                    dve.tensor_tensor(part, part, gate[:, c], ALU.mult)
                    dve.drain()
                    dve.tensor_tensor(s.x_res[:, i, c], s.x_res[:, i, c], part, ALU.add)


def final_norm(s, ins, out):
    nc = s.nc
    s.at = 0
    g = s.take(D)
    junk = s.take(D)
    y = s.take(TT, D)
    stat = s.take(2)
    g_in, sq_done, var_done, root_done, y_ready, y_out = (s.sem("fin_" + n) for n in ("g", "sq", "var", "root", "y", "out"))
    with nc.Block(name="final_norm", no_gpsimd_drain=True) as block:

        @block.sync
        def _(sp):
            sp.dma_start(g, ins["final_g"].partition_broadcast(P)).then_inc(g_in, 16)
            dst = out[0].rearrange("(i p) d -> i p d", p=P)
            for i in range(TT):
                sp.wait_ge(y_ready, i + 1)
                sp.dma_start(dst[i], y[:, i]).then_inc(y_out, 16)
            sp.wait_ge(y_out, 16 * TT)

        @block.scalar
        def _(act):
            for i in range(TT):
                act.activation(junk, s.x_res[:, i], ACT.Square, accum_out=stat[:, i:i + 1])
                act.drain()
            act.sem_inc(sq_done, 1)
            act.wait_ge(var_done, 1)
            act.activation(stat, stat, ACT.Sqrt).then_inc(root_done, 1)

        @block.vector
        def _(dve):
            dve.wait_ge(sq_done, 1)
            dve.tensor_scalar(stat, stat, 1.0 / D, NORM_EPS, ALU.mult, ALU.add).then_inc(var_done, 1)
            dve.wait_ge(root_done, 1)
            dve.reciprocal(stat, stat)
            dve.wait_ge(g_in, 16)
            dve.drain()
            for i in range(TT):
                dve.scalar_tensor_tensor(y[:, i], s.x_res[:, i], stat[:, i:i + 1], g, ALU.mult, ALU.mult).then_inc(y_ready, 1)


def load_constants(s, ins):
    nc = s.nc
    const_in = s.sem("const_in")
    with nc.Block(name="constants", no_gpsimd_drain=True) as block:

        @block.sync
        def _(sp):
            sp.dma_start(s.const[:, :], ins["const"]).then_inc(const_in, 16)
            sp.wait_ge(const_in, 16)


USED = ["x", "c", "ctx", "c_ctx", "ada_w", "ada_b", "norm_g", "final_g",
        "rw_mix", "rw_wrkv", "rw_wo", "rw_w0", "rw_w1", "rw_w2", "rw_a0", "rw_a1", "rw_a2", "rw_g1", "rw_g2",
        "rw_kk", "rw_ka", "rw_rk", "rw_lnw", "rw_lnb",
        "hy_w_in", "hy_b_in", "hy_conv_w", "hy_conv_b", "hy_f_w1", "hy_f_b1", "hy_f_freq", "hy_f_wi", "hy_f_bi",
        "hy_f_w3", "hy_skip", "hy_w_out", "hy_b_out",
        "moe_router", "moe_router_b", "moe_w_gate", "moe_w_up", "moe_w_down"]
ARENA = 48000


def build(nc, ins, out):
    mods = nc.dram_tensor("mods", (2, 2, 6 * D), F32, kind="Internal").ap()
    with ExitStack() as ctx:
        s = Shared(nc, ctx, ARENA)
        load_constants(s, ins)
        r = RwkvTensors(s)
        rwkv_inputs(s, r, ins, mods)
        rwkv_heads(s, r, ins, mods)
        rwkv_output(s, r, ins, mods)
        s.clear_semaphores()
        expert_layer(s, 0, ins, mods)
        hyena_layer(s, ins, mods)
        expert_layer(s, 1, ins, mods)
        final_norm(s, ins, out)


def kernel(**inputs):
    import concourse.bacc as bacc
    from concourse.bass_utils import run_bass_kernel_spmd

    nc = bacc.Bacc("TRN2", target_bir_lowering=False, num_devices=1)
    arrays = {f"in_{n}": np.ascontiguousarray(inputs[n]) for n in USED}
    arrays["in_const"], arrays["in_hy_const"], arrays["in_hy_deltas"] = CONST_ARRAY, HY_CONST, HY_DELTAS
    ins = {n[3:]: nc.dram_tensor(n, a.shape, F32, kind="ExternalInput").ap() for n, a in arrays.items()}
    out = nc.dram_tensor("out", (1, L, D), F32, kind="ExternalOutput").ap()
    build(nc, ins, out)
    result = run_bass_kernel_spmd(nc, [arrays], core_ids=[0])
    return result.results[0]["out"]
```
